# Optimizing a Trainium2 kernel written in Bass

```python
import jax, jax.numpy as jnp
from jax import lax
import numpy as np

D_MODEL = 1024
BATCH = 1
SEQ = 2048
DEPTH = 1
DEC_BATCH = 8
DEC_SEQ = 8
PAST_LEN = 16384
PAGE_SIZE = 128

D_MIX = D_MODEL
HEAD_DIM = 64
W_CONV = D_MIX // 4
W_GMLP = D_MIX // 2
W_POOL = D_MIX - W_CONV - W_GMLP
N_GMLP_HEADS = W_GMLP // HEAD_DIM
POOL_WINDOWS = (2, 4, 8, 16)
N_POOL_GROUPS = len(POOL_WINDOWS)
POOL_GROUP_DIM = W_POOL // N_POOL_GROUPS
CONV_WIDTH = 3
CONV_BUF = CONV_WIDTH - 1
POOL_BUF = max(POOL_WINDOWS) - 1
CHUNK = 128
D_FF = 4 * D_MODEL
D_IN_PROJ = 3 * W_CONV + 2 * W_GMLP + W_POOL
DEEPNORM_ALPHA = (2.0 * DEPTH) ** 0.25
DEEPNORM_BETA = (8.0 * DEPTH) ** -0.25
LN_EPS = 1e-5

kernel_name = "hymba_conv_gmlp_pool_deepnorm_adaln_step"

def layer_norm(x, g, b):
    xf = x.astype(jnp.float32)
    mu = jnp.mean(xf, axis=-1, keepdims=True)
    var = jnp.mean(jnp.square(xf - mu), axis=-1, keepdims=True)
    y = (xf - mu) * lax.rsqrt(var + LN_EPS)
    return (y * g.astype(jnp.float32) + b.astype(jnp.float32)).astype(x.dtype)

def short_conv(z, prefix, conv_w):
    t = z.shape[1]
    ext = jnp.concatenate([prefix, z], axis=1)
    y = ext[:, 0:t] * conv_w[0] + ext[:, 1:t + 1] * conv_w[1] + ext[:, 2:t + 2] * conv_w[2]
    return y, ext[:, -CONV_BUF:]

def chunk_sgu(u, v, sgu_g, sgu_b, w_s, b_s):
    bsz, t, _ = v.shape
    v_n = layer_norm(v, sgu_g, sgu_b)
    lc = min(t, CHUNK)
    nc = t // lc
    mask = jnp.tril(jnp.ones((lc, lc), dtype=bool))
    ws = jnp.where(mask[None], w_s[:, :lc, :lc], jnp.zeros((), w_s.dtype))
    vc = v_n.reshape(bsz, nc, lc, N_GMLP_HEADS, HEAD_DIM)
    s = jnp.einsum("hij,bnjhd->bnihd", ws, vc) + b_s[:, :lc].T[None, None, :, :, None]
    return u * s.reshape(bsz, t, W_GMLP), v_n

def multiscale_pool(z, prefix, n_valid, pool_w, pool_scale):
    bsz, t, _ = z.shape
    ext = jnp.concatenate([prefix, z], axis=1)
    cs = jnp.cumsum(ext.astype(jnp.float32), axis=1)
    cs = jnp.concatenate([jnp.zeros((bsz, 1, W_POOL), jnp.float32), cs], axis=1)
    p = POOL_BUF
    pos = jnp.arange(t)
    pooled = []
    for g, w in enumerate(POOL_WINDOWS):
        lo, hi = g * POOL_GROUP_DIM, (g + 1) * POOL_GROUP_DIM
        s = cs[:, p + 1:p + t + 1, lo:hi] - cs[:, p + 1 - w:p + t + 1 - w, lo:hi]
        count = jnp.minimum(w, pos + 1 + n_valid).astype(jnp.float32)
        pooled.append(s / count[None, :, None])
    pooled = jnp.concatenate(pooled, axis=-1)
    d = (pooled - z.astype(jnp.float32)).astype(z.dtype)
    y = jnp.einsum("btgc,gcd->btgd", d.reshape(bsz, t, N_POOL_GROUPS, POOL_GROUP_DIM), pool_w)
    return y.reshape(bsz, t, W_POOL) * pool_scale, ext[:, -POOL_BUF:]

def mixer_block(h, conv_prefix, pool_prefix, n_valid, w_in, conv_w, sgu_g, sgu_b, w_s, b_s,
                pool_w, pool_scale, w_out):
    proj = jnp.einsum("btd,de->bte", h, w_in)
    cuts = [W_CONV, 2 * W_CONV, 3 * W_CONV, 3 * W_CONV + W_GMLP, 3 * W_CONV + 2 * W_GMLP]
    a_b, a_c, a_x, g_u, g_v, p_x = jnp.split(proj, cuts, axis=-1)
    conv_out, new_conv = short_conv(a_c * a_x, conv_prefix, conv_w)
    y_a = a_b * conv_out
    y_b, v_rows = chunk_sgu(g_u, g_v, sgu_g, sgu_b, w_s, b_s)
    y_c, new_pool = multiscale_pool(p_x, pool_prefix, n_valid, pool_w, pool_scale)
    mix = jnp.concatenate([y_a, y_b, y_c], axis=-1)
    return jnp.einsum("bte,ed->btd", mix, w_out), new_conv, new_pool, v_rows

def decoder_layer(x, c, conv_prefix, pool_prefix, n_valid, w_ada, b_ada, w_in, conv_w, sgu_g,
                  sgu_b, w_s, b_s, pool_w, pool_scale, w_out, ln1_g, ln1_b, w_up, w_down,
                  ln2_g, ln2_b):
    mod = jnp.einsum("bd,de->be", jax.nn.silu(c), w_ada) + b_ada
    sh1, sc1, g1, sh2, sc2, g2 = jnp.split(mod[:, None, :], 6, axis=-1)
    h = x * (1.0 + sc1) + sh1
    mix, new_conv, new_pool, v_rows = mixer_block(h, conv_prefix, pool_prefix, n_valid, w_in,
                                                  conv_w, sgu_g, sgu_b, w_s, b_s, pool_w,
                                                  pool_scale, w_out)
    x = layer_norm(DEEPNORM_ALPHA * x + g1 * mix, ln1_g, ln1_b)
    h2 = x * (1.0 + sc2) + sh2
    f = jnp.einsum("btf,fd->btd", jnp.square(jax.nn.relu(jnp.einsum("btd,df->btf", h2, w_up))), w_down)
    x = layer_norm(DEEPNORM_ALPHA * x + g2 * f, ln2_g, ln2_b)
    return x, new_conv, new_pool, v_rows

def setup_inputs(seed: int = 0) -> dict:
    key = jax.random.key(seed)
    ks = jax.random.split(key, 24)

    def nrm(k, shape, scale=1.0):
        return jax.random.normal(k, shape, jnp.float32) * scale

    return {
        "x_prompt": nrm(ks[0], (BATCH, SEQ, D_MODEL)),
        "x_sample": nrm(ks[1], (DEC_BATCH, DEC_SEQ, D_MODEL)),
        "c_prompt": nrm(ks[2], (BATCH, D_MODEL)),
        "c_sample": nrm(ks[3], (DEC_BATCH, D_MODEL)),
        "state_conv": nrm(ks[4], (DEPTH, DEC_BATCH, CONV_BUF, W_CONV)),
        "state_pool": nrm(ks[5], (DEPTH, DEC_BATCH, POOL_BUF, W_POOL)),
        "w_ada": nrm(ks[6], (DEPTH, D_MODEL, 6 * D_MODEL), 0.5 * D_MODEL ** -0.5),
        "b_ada": nrm(ks[7], (DEPTH, 6 * D_MODEL), 0.01),
        "w_in": nrm(ks[8], (DEPTH, D_MODEL, D_IN_PROJ), D_MODEL ** -0.5),
        "conv_w": nrm(ks[9], (DEPTH, CONV_WIDTH, W_CONV), CONV_WIDTH ** -0.5),
        "sgu_g": 1.0 + nrm(ks[10], (DEPTH, W_GMLP), 0.1),
        "sgu_b": nrm(ks[11], (DEPTH, W_GMLP), 0.01),
        "w_s": nrm(ks[12], (DEPTH, N_GMLP_HEADS, CHUNK, CHUNK), CHUNK ** -0.5),
        "b_s": 1.0 + nrm(ks[13], (DEPTH, N_GMLP_HEADS, CHUNK), 0.1),
        "pool_w": nrm(ks[14], (DEPTH, N_POOL_GROUPS, POOL_GROUP_DIM, POOL_GROUP_DIM), POOL_GROUP_DIM ** -0.5),
        "pool_scale": 1.0 + nrm(ks[15], (DEPTH, W_POOL), 0.1),
        "w_out": nrm(ks[16], (DEPTH, D_MIX, D_MODEL), DEEPNORM_BETA * D_MIX ** -0.5),
        "ln1_g": 1.0 + nrm(ks[17], (DEPTH, D_MODEL), 0.1),
        "ln1_b": nrm(ks[18], (DEPTH, D_MODEL), 0.01),
        "w_up": nrm(ks[19], (DEPTH, D_MODEL, D_FF), D_MODEL ** -0.5),
        "w_down": nrm(ks[20], (DEPTH, D_FF, D_MODEL), DEEPNORM_BETA * D_FF ** -0.5),
        "ln2_g": 1.0 + nrm(ks[21], (DEPTH, D_MODEL), 0.1),
        "ln2_b": nrm(ks[22], (DEPTH, D_MODEL), 0.01),
    }

def reference(x_prompt, x_sample, c_prompt, c_sample, state_conv, state_pool, w_ada, b_ada, w_in,
              conv_w, sgu_g, sgu_b, w_s, b_s, pool_w, pool_scale, w_out, ln1_g, ln1_b, w_up,
              w_down, ln2_g, ln2_b):
    bp = x_prompt.shape[0]
    xp, xs = x_prompt, x_sample
    conv_p, pool_p, conv_s, pool_s, v_s = [], [], [], [], []
    for l in range(DEPTH):
        params = (w_ada[l], b_ada[l], w_in[l], conv_w[l], sgu_g[l], sgu_b[l], w_s[l], b_s[l],
                  pool_w[l], pool_scale[l], w_out[l], ln1_g[l], ln1_b[l], w_up[l], w_down[l],
                  ln2_g[l], ln2_b[l])
        zc = jnp.zeros((bp, CONV_BUF, W_CONV), xp.dtype)
        zp = jnp.zeros((bp, POOL_BUF, W_POOL), xp.dtype)
        xp, nc_p, np_p, _ = decoder_layer(xp, c_prompt, zc, zp, 0, *params)
        xs, nc_s, np_s, v_rows = decoder_layer(xs, c_sample, state_conv[l], state_pool[l], POOL_BUF, *params)
        conv_p.append(nc_p)
        pool_p.append(np_p)
        conv_s.append(nc_s)
        pool_s.append(np_s)
        v_s.append(v_rows)
    new_state_conv_prompt = jnp.stack(conv_p)
    new_state_pool_prompt = jnp.stack(pool_p)
    new_state_conv_sample = jnp.stack(conv_s)
    new_state_pool_sample = jnp.stack(pool_s)
    new_state_gmlp_v_sample = jnp.stack(v_s)
    return (xp, xs, new_state_conv_prompt, new_state_pool_prompt, new_state_conv_sample,
            new_state_pool_sample, new_state_gmlp_v_sample)


_drawn_inputs = setup_inputs


def setup_inputs(seed=0):
    import zlib

    import numpy as np

    out = dict(_drawn_inputs(seed))
    spreads = {}
    factors = {'b_ada': 3.207,
     'sgu_b': 5.525,
     'b_s': 4.395,
     'pool_scale': 8.0,
     'ln1_b': 5.796,
     'ln2_b': 5.699}
    for name, (base, spread) in spreads.items():
        noise = np.random.default_rng([zlib.crc32(name.encode()), seed]).standard_normal(out[name].shape)
        drawn = base * np.exp(spread * noise) if base else spread * noise
        out[name] = __import__('jax').numpy.asarray(drawn.astype(out[name].dtype))
    for name, factor in factors.items():
        out[name] = (out[name] * factor).astype(out[name].dtype)
    return out
```

```python
from contextlib import ExitStack

import concourse.bass as bass
from concourse import mybir

F32 = mybir.dt.float32
F32R = mybir.dt.float32r
I32 = mybir.dt.int32
ACT = mybir.ActivationFunctionType
ALU = mybir.AluOpType

P = 128
D = 1024
KD = D // P
SEQ = 2048
GT = 512
SUPERS = SEQ // GT
NB, DT = 8, 8
ST = NB * DT
W_CONV, W_GMLP, W_POOL = 256, 512, 256
FF = 4 * D
HEADS = 8
HALF = D // 2
COL_B, COL_C, COL_X = 0, W_CONV, 2 * W_CONV
COL_U = 3 * W_CONV
COL_V = COL_U + W_GMLP
COL_P = COL_V + W_GMLP
CONV_BUF, POOL_BUF = 2, 15
WINDOWS = (2, 4, 8, 16)
ALPHA = 2.0 ** 0.25
EPS = 1e-5
RSQRT_MAGIC = float(0x5F3759DF)
SH1, SC1, G1, SH2, SC2, G2 = range(6)

SLOTS = 4
RAW = 2
N_SLABS = 88
SLAB_FM, SLAB_O, SLAB_UP0 = 4, 16, 24
N_FM = 12
MLP_GROUPS = 16
FM_COLS = [COL_C, COL_X, COL_B, COL_C + P, COL_X + P, COL_B + P, COL_P, COL_P + P] + \
          [COL_U + P * i for i in range(4)]
O_PAIRS = [(0, 1), (2, 3), (6, 7), (4, 5)]
V_BANK = [4, 5, 6, 7, 3]
TR_BANK = [6, 0]


N_PRE = 5 + 2 + 2 + 2 + 1 + 2
DVE_STEPS = 175


def bcast(ap, n):
    return ap.partition_broadcast(n)


def o_bank(h, t):
    return (4 + 5 * h + t) % 8


def decoder_layer_kernel(nc, x_prompt, x_sample, c_prompt, c_sample, state_conv, state_pool,
                         w_ada, b_ada, w_in, conv_w, sgu_g, sgu_b, w_s, b_s, pool_w, pool_scale,
                         w_out, ln1_g, ln1_b, w_up, w_down, ln2_g, ln2_b,
                         y_prompt, y_sample, o_conv_p, o_pool_p, o_conv_s, o_pool_s, o_v_s,
                         mod_rows):
    ctx = ExitStack()
    with ctx:
        ctx.enter_context(nc.allow_non_contiguous_dma(reason="small tables turned by the DMA, once"))

        def sb(name, shape, dt=F32):
            return ctx.enter_context(nc.sbuf_tensor(name, shape, dt))

        def sem(name):
            return ctx.enter_context(nc.semaphore(name))

        W = sb("w_hilo", [P, SLOTS, 2, D], F32R)
        raw = sb("w_raw", [P, RAW, D])
        hT = sb("hT", [P, 2, KD, GT + ST], F32R)
        MH = sb("mixT_hidden", [P, 2, KD, GT + ST], F32R)
        xt = sb("xt", [P, 5, D])
        acc = sb("acc", [P, 5, D])
        rs = sb("rs", [P, 2, 2, GT + ST], F32R)
        wsT = sb("wsT", [P, 2, HEADS, P], F32R)
        wsS = sb("wsS", [P, 2, HEADS, ST], F32R)
        bsR = sb("bsR", [P, 4, P])
        pwT = sb("pwT", [P, 2, 2, P], F32R)
        ident = sb("ident", [P, P])
        modT = sb("modT", [P, 6 * KD, 1 + NB])
        scale2 = sb("scale2", [P, KD, 1 + NB])
        bias2 = sb("bias2", [P, KD, 1 + NB])
        rows = sb("rows", [P, 3, D])
        gs = sb("gs", [P, D])
        sgu_gb = sb("sgu_gb", [P, 2, W_GMLP])
        htmp = sb("htmp", [P, 2, GT + ST])
        convw = sb("convw", [P, 2, 3])
        pscale = sb("pscale", [P, 2])
        invw = sb("invw", [P, 2])
        invtab = sb("invtab", [P, 2, 16])
        zcarry = sb("zcarry", [P, 2, CONV_BUF])
        pcarry = sb("pcarry", [P, 2, POOL_BUF])
        zstate = sb("zstate", [P, 2, NB * CONV_BUF])
        pstate = sb("pstate", [P, 2, NB * POOL_BUF])
        lnT = sb("lnT", [P, 2, KD])
        st = sb("st", [P, 2, 6])
        mv = sb("mv", [P, 5, 2])
        rstd = sb("rstd", [P, 5])
        rtmp = sb("rtmp", [P, 5])
        ps = ctx.enter_context(nc.psum_tensor("ps", [P, 8, 512], F32))

        flat = acc[:, :, :].rearrange("p t d -> p (t d)")
        off = [0]

        def scratch(n):
            off[0] += n
            assert off[0] <= 5 * D
            return flat[:, off[0] - n:off[0]]

        sg = scratch(4 * (GT + ST)).rearrange("p (c n) -> p c n", c=4)
        zp_ = scratch(CONV_BUF + GT)
        zs_ = scratch(NB * (CONV_BUF + DT)).rearrange("p (b n) -> p b n", b=NB)
        pp_ = scratch(POOL_BUF + GT)
        psm = scratch(NB * (POOL_BUF + DT)).rearrange("p (b n) -> p b n", b=NB)
        bufA = scratch(GT + ST)
        bufB = scratch(GT + ST)
        zlast = scratch(2 * (CONV_BUF + NB * CONV_BUF)).rearrange("p (c n) -> p c n", c=2)
        plast = scratch(2 * (POOL_BUF + NB * POOL_BUF)).rearrange("p (c n) -> p c n", c=2)

        siluT = acc[:, 4, 0:KD * (1 + NB)]
        STATES = [(o_conv_p[0, 0], CONV_BUF, 0), (o_conv_s[0].rearrange("b r c -> (b r) c"), NB * CONV_BUF, 1),
                  (o_pool_p[0, 0], POOL_BUF, 2), (o_pool_s[0].rearrange("b r c -> (b r) c"), NB * POOL_BUF, 3)]

        s_pre = sem("s_pre")
        s_ada_in = [sem("s_ada_in0"), sem("s_ada_in1")]
        s_ada_mm = sem("s_ada_mm")
        s_ada_row = sem("s_ada_row")
        s_ada_tr = sem("s_ada_tr")
        s_ada_T = sem("s_ada_T")
        s_ada_out = [sem("s_ada_out0"), sem("s_ada_out1")]
        s_corner = sem("s_corner")
        s_fence_pe, s_fence_dve = sem("s_fence_pe"), sem("s_fence_dve")
        s_cT = sem("s_cT")
        s_silu = sem("s_silu")
        s_prepe = sem("s_prepe")
        s_prep = sem("s_prep")
        s_pool0 = sem("s_pool0")
        s_pret = sem("s_pret")
        s_ready = sem("s_ready")
        s_chain = sem("s_chain")
        s_chain_act = sem("s_chain_act")
        raw_loaded = [sem(f"raw_loaded{i}") for i in range(RAW)]
        hi_done = sem("hi_done")
        lo_done = sem("lo_done")
        slab_used = sem("slab_used")
        x_loaded = [sem(f"x_loaded{t}") for t in range(5)]
        rows_loaded = sem("rows_loaded")
        gs_loaded = sem("gs_loaded")
        tr_done = sem("tr_done")
        tmp_ready = sem("tmp_ready")
        hT_ready = sem("hT_ready")
        v_norm = sem("v_norm")
        sgu_done = sem("sgu_done")
        sgu_evac = sem("sgu_evac")
        fm_evac = sem("fm_evac")
        d_ready = sem("d_ready")
        pm_done = sem("pm_done")
        mix_ready = sem("mix_ready")
        o_done = sem("o_done")
        o_evac = sem("o_evac")
        xn_ready = sem("xn_ready")
        x1_ready = sem("x1_ready")
        relu_done = sem("relu_done")
        hid_ready = sem("hid_ready")
        d_done = sem("d_done")
        d_evac = sem("d_evac")
        y_ready = sem("y_ready")
        y_stored = sem("y_stored")
        v_stored = sem("v_stored")
        s_hid_hi = sem("s_hid_hi")
        st_tr = sem("st_tr")
        st_rows = sem("st_rows")
        st_stored = sem("st_stored")

        w_in_v = w_in[0].rearrange("(k p) e -> p k e", p=P)
        w_out_v = w_out[0].rearrange("(k p) e -> p k e", p=P)
        w_up_v = w_up[0].rearrange("(k p) e -> p k e", p=P)
        w_down_v = w_down[0].rearrange("(f p) e -> p f e", p=P)
        w_ada_v = w_ada[0].rearrange("(k p) e -> p k e", p=P)

        def rows_of(t):
            return P if t < 4 else ST

        def tokens(t):
            return slice(P * t, P * t + rows_of(t))

        def chunks(nt):
            return [(0, GT)] if nt == 4 else [(0, (GT + ST) // 2), ((GT + ST) // 2, GT + ST)]

        def fm_view(pair, nt):
            n = GT if nt == 4 else (GT + ST) // 2
            return ps[:, 2 * pair:2 * pair + len(chunks(nt)), 0:n]

        def as_fm(ap, nt):
            return ap[:, 0:GT + (ST if nt == 5 else 0)].rearrange("p (c n) -> p c n", c=len(chunks(nt)))

        def pieces(pair, nt):
            if nt == 4:
                return [(ps[:, 2 * pair, 0:GT], 0)]
            n = (GT + ST) // 2
            return [(ps[:, 2 * pair, 0:n], 0), (ps[:, 2 * pair + 1, 0:GT - n], n),
                    (ps[:, 2 * pair + 1, GT - n:n], None)]

        def vorder(nt):
            return [0, 1, 2, 3] if nt == 4 else [4, 0, 1, 2, 3]

        def mixer_stages(nt):
            o = vorder(nt)
            out = [("F", 0)] + ([("F", 1)] if nt == 4 else [])
            f, i = len(out), 0
            while i < len(o):
                out.append(("S", o[i:i + 2], i))
                i += 2
                if i < len(o):
                    out += [("F", f), ("F", f + 1)]
                    f += 2
            out += [("F", n) for n in range(f, 9)]
            return out + [("M", 0), ("F", 9), ("M", 1), ("F", 10), ("F", 11)]

        def down_bank(nt, parity, j):
            return 4 + (2 * nt * parity + j) % 4

        block = ctx.enter_context(nc.Block())

        @block.sync
        def _(sp):
            sp.dma_start(rows[0:1, 2, :], c_prompt).then_inc(s_pre, 16)
            sp.dma_start(rows[1:1 + NB, 2, :], c_sample).then_inc(s_pre, 16)
            sp.dma_start(gs[:, :].rearrange("p (h j) -> p h j", h=HEADS),
                         w_s[0].rearrange("h i j -> i h j")).then_inc(s_pre, 16)
            sp.dma_start(htmp[0:NB * CONV_BUF, 0, 0:W_CONV],
                         state_conv[0].rearrange("b r c -> (b r) c")).then_inc(s_pre, 16)
            sp.dma_start(htmp[0:NB * POOL_BUF, 1, 0:W_POOL],
                         state_pool[0].rearrange("b r c -> (b r) c")).then_inc(s_pre, 16)

            def ada_chunk(cc, j):
                sp.dma_start((xt if j == 0 else acc)[:, 0:4, :].rearrange("p t (a n) -> p (t a) n", a=2),
                             w_ada_v[:, :, bass.ds(cc * 512, 512)]).then_inc(s_ada_in[j], 16)
                sp.dma_start(rows[0:1 + NB, 0, 512 * j:512 * j + 512],
                             bcast(b_ada[0, bass.ds(cc * 512, 512)], 1 + NB)).then_inc(s_ada_in[j], 16)

            def ada_rows_out(cc, j):
                sp.wait_ge(s_ada_row, cc + 1)
                sp.dma_start(mod_rows[:, bass.ds(cc * 512, 512)],
                             rows[0:1 + NB, 1, 512 * j:512 * j + 512]).then_inc(s_ada_out[j], 16)

            for j in range(2):
                ada_chunk(j, j)
            for half in range(2):
                sp.dma_start(bsR[64 * half:64 * half + 64, :, :],
                             bcast(b_s[0].rearrange("(q two) i -> two q i", two=2)[half], 64)
                             ).then_inc(s_pre, 16)
            sp.dma_start(sgu_gb[:, 0, :], bcast(sgu_g[0], P)).then_inc(s_pre, 16)
            sp.dma_start(sgu_gb[:, 1, :], bcast(sgu_b[0], P)).then_inc(s_pre, 16)
            for c in range(2):
                sp.dma_start(convw[:, c, :],
                             conv_w[0, :, P * c:P * c + P].rearrange("w p -> p w")).then_inc(s_pre, 16)
            sp.dma_start(pscale[:, :], pool_scale[0].rearrange("(c p) -> p c", p=P)).then_inc(s_pre, 16)
            sp.dma_start(lnT[:, 0, :], ln1_g[0].rearrange("(k p) -> p k", p=P)).then_inc(s_pre, 16)
            sp.dma_start(lnT[:, 1, :], ln1_b[0].rearrange("(k p) -> p k", p=P)).then_inc(s_pre, 16)
            sp.wait_ge(s_prep, 1)
            for g in range(4):
                q, c = 64 * (g % 2), g // 2
                sp.dma_start(raw[q:q + 64, 0, P * c + q:P * c + q + 64], pool_w[0, g]).then_inc(s_corner, 16)
            sp.wait_ge(s_pret, 1)
            for b in range(NB):
                sp.dma_start(raw[DT * b:DT * b + DT, 0, 2 * P:2 * P + HEADS * ST].rearrange(
                                 "p (h i) -> p h i", h=HEADS)[:, :, DT * b:DT * b + DT],
                             raw[0:DT, 1, :].rearrange("p (h i) -> p h i", h=HEADS)[:, :, 0:DT]
                             ).then_inc(s_corner, 16)
            with sp.Fori(1, 6) as i:
                for j in range(2):
                    sp.wait_ge(s_ada_row, 2 * i + j - 1)
                    ada_chunk(2 * i + j, j)
                    ada_rows_out(2 * i + j - 2, j)
            for j in range(2):
                ada_rows_out(10 + j, j)
            for j in range(2):
                sp.wait_ge(s_ada_out[j], 16 * 6)
            sp.wait_ge(s_ready, 1)

            def load_rows1():
                sp.dma_start(rows[:, 0, :], bcast(mod_rows[0, G1 * D:G1 * D + D], P)).then_inc(rows_loaded, 16)
                sp.dma_start(rows[:, 1, :], bcast(ln1_g[0], P)).then_inc(rows_loaded, 16)
                sp.dma_start(rows[:, 2, :], bcast(ln1_b[0], P)).then_inc(rows_loaded, 16)

            def super_dma(s, nt):
                for t in range(nt):
                    if t < 4:
                        src = x_prompt[0, bass.ds(s * GT + P * t, P), :]
                    else:
                        src = x_sample.rearrange("b t d -> (b t) d")
                    sp.dma_start(xt[0:rows_of(t), t, :], src).then_inc(x_loaded[t], 16)

                def slab(n, src, sizes, i=None, free=True):
                    slot = (n if i is None else i) % RAW
                    if free:
                        sp.wait_ge(lo_done, s * N_SLABS + n - RAW + 1)
                    dst = raw[:, slot, :]
                    if sizes:
                        dst = dst.rearrange("p (k n) -> p k n", k=sizes)
                    sp.dma_start(dst, src).then_inc(raw_loaded[slot], 16)

                for n in range(4):
                    slab(n, w_in_v[:, 2 * n:2 * n + 2, COL_V:COL_V + W_GMLP], 2, free=n >= RAW)
                for n, col in enumerate(FM_COLS):
                    slab(SLAB_FM + n, w_in_v[:, :, col:col + P], KD)
                if nt == 5:
                    sp.wait_ge(v_norm, 4 * s + 1)
                    sp.dma_start(o_v_s[0].rearrange("b t c -> (b t) c"), gs[0:ST, 0:W_GMLP]).then_inc(v_stored, 16)
                    sp.wait_ge(v_stored, 16)
                    load_gs(G1)
                for h in range(2):
                    for q, (k, _) in enumerate(O_PAIRS):
                        slab(SLAB_O + 4 * h + q, w_out_v[:, k:k + 2, HALF * h:HALF * h + HALF], 2)

                def up(g, f, i, n):
                    slab(n, w_up_v[:, :, bass.ds(f * P, P)], KD, i)

                def down(f, i, n):
                    slab(n, w_down_v[:, bass.ds(f, 1), :].rearrange("p a n -> p (a n)"), 0, i)

                for i in range(2):
                    up(0, i, i, SLAB_UP0 + i)
                for i in range(2):
                    up(1, 2 + i, i, SLAB_UP0 + 2 + i)
                for i in range(2):
                    down(i, i, SLAB_UP0 + 4 + i)
                sp.wait_ge(x1_ready, s + 1)
                sp.dma_start(rows[:, 0, :], bcast(mod_rows[0, G2 * D:G2 * D + D], P)).then_inc(rows_loaded, 16)
                sp.dma_start(rows[:, 1, :], bcast(ln2_g[0], P)).then_inc(rows_loaded, 16)
                sp.dma_start(rows[:, 2, :], bcast(ln2_b[0], P)).then_inc(rows_loaded, 16)
                if nt == 5:
                    sp.wait_ge(st_rows, 8)
                    for dst, n, q in STATES:
                        sp.dma_start(dst, gs[0:n, 2 * P * q:2 * P * q + 2 * P]).then_inc(st_stored, 16)
                    sp.wait_ge(st_stored, 16 * len(STATES))
                    load_gs(G2)
                with sp.Fori(1, 15) as g:
                    for i in range(2):
                        up(g + 1, 2 * g + 2 + i, i, SLAB_UP0 + 2 + 4 * g + i)
                    for i in range(2):
                        down(2 * g + i, i, SLAB_UP0 + 4 + 4 * g + i)
                for i in range(2):
                    down(30 + i, i, 86 + i)
                for t in range(nt):
                    sp.wait_ge(y_ready, 4 * s + t + 1)
                    if t < 4:
                        dst = y_prompt[0, bass.ds(s * GT + P * t, P), :]
                    else:
                        dst = y_sample.rearrange("b t d -> (b t) d")
                    sp.dma_start(dst, acc[0:rows_of(t), t, :]).then_inc(y_stored, 16)
                sp.wait_ge(y_stored, 64 * s + 16 * nt)
                if nt == 4:
                    load_rows1()

            def load_gs(which):
                for b in range(NB):
                    sp.dma_start(gs[DT * b:DT * b + DT, :],
                                 bcast(mod_rows[1 + b, which * D:which * D + D], DT)).then_inc(gs_loaded, 16)

            load_rows1()
            with sp.Fori(0, SUPERS - 1) as s:
                super_dma(s, 4)
            super_dma(SUPERS - 1, 5)

        @block.gpsimd
        def _(pool):
            count = [0]

            def step(ins):
                count[0] += 1
                ins.then_inc(s_pool0, 1)
                pool.wait_ge(s_pool0, count[0])

            step(pool.memset(raw[:, :, :], 0.0))
            step(pool.memset(ident[:, :], 0.0))
            step(pool.affine_select(out=ident[:, :], in_=ident[:, :], compare_op=ALU.not_equal, fill=1.0,
                                    base=0, pattern=[[-1, P]], channel_multiplier=1))
            pool.memset(mv[:, :, :], 1.0).then_inc(s_prep, 1)
            step(pool.memset(zcarry[:, :, :], 0.0))
            step(pool.memset(pcarry[:, :, :], 0.0))
            for g, w in enumerate(WINDOWS):
                q, c = 64 * (g % 2), g // 2
                step(pool.memset(invw[q:q + 64, c:c + 1], 1.0 / w))
                step(pool.memset(invtab[q:q + 64, c, :], 1.0 / w))
                for t in range(w - 1):
                    step(pool.memset(invtab[q:q + 64, c, t:t + 1], 1.0 / (t + 1)))
            pool.wait_ge(s_corner, 16 * (4 + NB))
            v = raw[0:ST, 0, 2 * P:2 * P + HEADS * ST].rearrange("p (h i) -> p h i", h=HEADS)
            step(pool.affine_select(out=v, in_=v, compare_op=ALU.is_ge, fill=0.0,
                                    base=0, pattern=[[0, HEADS], [1, ST]], channel_multiplier=-1))
            step(pool.tensor_copy(wsS[0:ST, 0, :, :], v))
            step(pool.tensor_tensor(wsS[0:ST, 1, :, :], v, wsS[0:ST, 0, :, :], ALU.subtract))
            v = raw[:, 0, 0:2 * P].rearrange("p (c n) -> p c n", c=2)
            step(pool.tensor_copy(pwT[:, 0, :, :], v))
            step(pool.tensor_tensor(pwT[:, 1, :, :], v, pwT[:, 0, :, :], ALU.subtract))
            v = raw[:, 1, :].rearrange("p (h i) -> p h i", h=HEADS)
            step(pool.affine_select(out=v, in_=v, compare_op=ALU.is_ge, fill=0.0,
                                    base=0, pattern=[[0, HEADS], [1, P]], channel_multiplier=-1))
            step(pool.tensor_copy(wsT[:, 0, :, :], v))
            pool.tensor_tensor(wsT[:, 1, :, :], v, wsT[:, 0, :, :], ALU.subtract).then_inc(s_prep, 1)

            with pool.Fori(0, SUPERS * N_SLABS // SLOTS) as i:
                for j in range(SLOTS):
                    pool.wait_ge(hi_done, SLOTS * i + j + 1)
                    pool.tensor_tensor(W[:, j, 1, :], raw[:, j % RAW, :], W[:, j, 0, :],
                                       ALU.subtract).then_inc(lo_done, 1)

        @block.scalar
        def _(act):
            act.wait_ge(s_cT, 1)
            act.activation(siluT, ps[:, 7, 0:KD * (1 + NB)], ACT.Silu).then_inc(s_silu, 1)
            act.wait_ge(s_ready, 1)

            def hi_part(s, n, slot=None, turn=None, free=True):
                slot = n % SLOTS if slot is None else slot
                turn = n // RAW if turn is None else turn
                act.wait_ge(raw_loaded[slot % RAW], (s * (N_SLABS // RAW) + turn + 1) * 16)
                if free:
                    act.wait_ge(slab_used, s * N_SLABS + n - SLOTS + 1)
                act.activation(W[:, slot, 0, :], raw[:, slot % RAW, :], ACT.Copy).then_inc(hi_done, 1)

            def affine(s, nt, phase):
                for t in range(4):
                    act.wait_ge(tr_done, 8 * s + phase * nt + t + 1)
                    for k in range(KD):
                        b = TR_BANK[t % 2] + k // 4
                        sc = modT[:, SC1 * KD + k, 0:1] if phase == 0 else scale2[:, k, 0:1]
                        bi = modT[:, SH1 * KD + k, 0:1] if phase == 0 else bias2[:, k, 0:1]
                        ins = act.activation(acc[:, t, P * k:P * k + P], ps[:, b, P * (k % 4):P * (k % 4) + P],
                                             ACT.Identity, bias=bi, scale=sc)
                    ins.then_inc(tmp_ready, 1)

            def relu2(s, f, i, n, nt, base, first=False):
                act.wait_ge(slab_used, s * N_SLABS + n + 1)
                if not first:
                    act.wait_ge(hid_ready, s * 32 + f - 1)
                h = as_fm(htmp[:, i, :], nt)
                act.activation(h, fm_view(i, nt), ACT.Relu).then_inc(s_chain_act, 1)
                act.wait_ge(s_chain_act, s * 32 + f + 1)
                act.activation(h, h, ACT.Square).then_inc(relu_done, 1)

            def super_act(s, nt):
                for n in range(SLOTS):
                    hi_part(s, n, free=False)
                affine(s, nt, 0)
                for n in range(SLAB_UP0 - SLOTS):
                    hi_part(s, n + SLOTS)
                for n in range(SLAB_UP0 - SLOTS, SLAB_UP0):
                    hi_part(s, n + SLOTS)
                affine(s, nt, 1)
                for i in range(2):
                    relu2(s, i, i, SLAB_UP0 + i, nt, 0, first=True)
                    hi_part(s, SLAB_UP0 + SLOTS + i)
                for i in range(2):
                    relu2(s, 2 + i, i, SLAB_UP0 + 2 + i, nt, 0)
                    hi_part(s, SLAB_UP0 + 2 + SLOTS + i)
                for i in range(2):
                    hi_part(s, SLAB_UP0 + 4 + SLOTS + i)

                def ups(g):
                    for i in range(2):
                        n = SLAB_UP0 + 2 + 4 * g + i
                        relu2(s, 2 * g + 2 + i, i, n, nt, 0)
                        hi_part(s, n + SLOTS, slot=2 + i, turn=(SLAB_UP0 + 2 + SLOTS) // RAW + 2 * g)

                with act.Fori(1, 14) as g:
                    ups(g)
                    for i in range(2):
                        hi_part(s, SLAB_UP0 + 4 + 4 * g + i + SLOTS, slot=i,
                                turn=(SLAB_UP0 + 4 + SLOTS) // RAW + 2 * g)
                ups(14)

            with act.Fori(0, SUPERS - 1) as s:
                super_act(s, 4)
            super_act(SUPERS - 1, 5)

        @block.tensor
        def _(pe):
            def mm3(out, w_hi, w_lo, x_hi, x_lo, start, stop):
                pe.matmul(out, w_hi, x_hi, start=start, stop=False)
                pe.matmul(out, w_hi, x_lo, start=False, stop=False)
                return pe.matmul(out, w_lo, x_hi, start=False, stop=stop)

            pe.wait_ge(s_pre, 16 * N_PRE)
            pe.wait_ge(s_prep, 1)
            for k in range(KD):
                ins = pe.transpose(ps[:, 7, (1 + NB) * k:(1 + NB) * (k + 1)],
                                   rows[0:1 + NB, 2, P * k:P * k + P], ident[0:1 + NB, 0:1 + NB])
            ins.then_inc(s_cT, 1)
            for c in range(2):
                pe.transpose(ps[:, 6, 16 * c:16 * c + 16], htmp[0:16, 0, P * c:P * c + P], ident[0:16, 0:16])
            for c in range(2):
                pe.transpose(ps[:, 6, 128 + 120 * c:128 + 120 * c + 120],
                             htmp[0:120, 1, P * c:P * c + P], ident[0:120, 0:120])
            for h in range(HEADS):
                ins = pe.transpose(ps[:, 4 + h // 4, P * (h % 4):P * (h % 4) + P],
                                   gs[:, P * h:P * h + P], ident[:, :])
            ins.then_inc(s_prepe, 1)

            def ada_product(cc, i, j):
                pe.wait_ge(s_ada_in[j], 32 * (i + 1))
                if not (isinstance(i, int) and i == 0):
                    pe.wait_ge(s_ada_row, cc - 1)
                buf = (xt if j == 0 else acc)[:, 0:4, :].rearrange("p t (a n) -> p (t a) n", a=2)
                for k in range(KD):
                    ins = pe.matmul(ps[0:1 + NB, j, :], siluT[:, (1 + NB) * k:(1 + NB) * (k + 1)],
                                    buf[:, k, :], start=(k == 0), stop=(k == KD - 1))
                ins.then_inc(s_ada_mm, 1)

            def ada_turn(cc, i, j):
                pe.wait_ge(s_ada_row, cc + 1)
                if not (isinstance(i, int) and i == 0):
                    pe.wait_ge(s_ada_T, cc - 1)
                pe.sem_inc(s_fence_pe, 1)
                for q in range(4):
                    ins = pe.transpose(ps[:, 2 + j, (1 + NB) * q:(1 + NB) * (q + 1)],
                                       rows[0:1 + NB, 1, 512 * j + P * q:512 * j + P * q + P],
                                       ident[0:1 + NB, 0:1 + NB])
                ins.then_inc(s_ada_tr, 1)

            pe.wait_ge(s_silu, 1)
            ada_product(0, 0, 0)
            ada_product(1, 0, 1)
            for j in range(2):
                ada_turn(j, 0, j)
            with pe.Fori(1, 6) as i:
                for j in range(2):
                    ada_product(2 * i + j, i, j)
                for j in range(2):
                    ada_turn(2 * i + j, i, j)
            pe.wait_ge(s_ready, 1)

            def transposes(s, nt, phase, t):
                r = rows_of(t)
                if t >= 2:
                    pe.wait_ge(tmp_ready, 8 * s + 4 * phase + t - 1)
                for k in range(KD):
                    ins = pe.transpose(ps[:, TR_BANK[t % 2] + k // 4, P * (k % 4):P * (k % 4) + r],
                                       xt[0:r, t, P * k:P * k + P], ident[0:r, 0:r])
                ins.then_inc(tr_done, 1)

            def fm_product(s, n, slot, pair, nt):
                pe.wait_ge(lo_done, s * N_SLABS + n + 1)
                w = W[:, slot, :, :].rearrange("p l (k n) -> p l k n", k=KD)
                for c, (a, b) in enumerate(chunks(nt)):
                    for k in range(KD):
                        ins = mm3(ps[:, 2 * pair + c, 0:b - a], w[:, 0, k, :], w[:, 1, k, :],
                                  hT[:, 0, k, a:b], hT[:, 1, k, a:b], k == 0, k == KD - 1)
                ins.then_inc(slab_used, 1)

            def sgu_half(s, nt, t, pos, half):
                r = rows_of(t)
                w = wsT if t < 4 else wsS
                n = 2 * r
                for q in range(2):
                    pair = 2 * half + q
                    v = rs[0:r, pos % 2, :, P * pair:P * pair + P]
                    ins = mm3(ps[:, V_BANK[t], n * q:n * q + n], v[:, 0, :], v[:, 1, :],
                              w[0:r, 0, 2 * pair:2 * pair + 2, :], w[0:r, 1, 2 * pair:2 * pair + 2, :],
                              True, True)
                ins.then_inc(sgu_done, 1)

            def super_pe(s, nt):
                for t in range(nt):
                    pe.wait_ge(x_loaded[t], 16 * (s + 1) if t < 4 else 16)
                    transposes(s, nt, 0, t)
                pe.wait_ge(hT_ready, 8 * s + nt)
                for n in range(4):
                    pe.wait_ge(lo_done, s * N_SLABS + n + 1)
                    for t in range(nt):
                        r = rows_of(t)
                        for kk in range(2):
                            k = 2 * n + kk
                            ins = mm3(ps[0:r, V_BANK[t], :], hT[:, 0, k, tokens(t)], hT[:, 1, k, tokens(t)],
                                      W[:, n, 0, 512 * kk:512 * kk + 512], W[:, n, 1, 512 * kk:512 * kk + 512],
                                      k == 0, k == KD - 1)
                    ins.then_inc(slab_used, 1)
                halves = 0
                for stage in mixer_stages(nt):
                    if stage[0] == "F":
                        f = stage[1]
                        if f >= 2:
                            pe.wait_ge(fm_evac, s * N_FM + f - 1)
                        if f == 1 and nt == 5:
                            pe.wait_ge(sgu_evac, 8 * s + 3)
                        fm_product(s, SLAB_FM + f, f % SLOTS, f % 2, nt)
                    elif stage[0] == "S":
                        tiles, pos = stage[1], stage[2]
                        for half in range(2):
                            for i, t in enumerate(tiles):
                                if half == 0:
                                    pe.wait_ge(v_norm, 4 * s + pos + i + 1)
                                else:
                                    pe.wait_ge(sgu_evac, 8 * s + halves + i + 1)
                                sgu_half(s, nt, t, pos + i, half)
                        halves += 2 * len(tiles)
                    else:
                        c = stage[1]
                        pe.wait_ge(d_ready, 2 * s + c + 1)
                        for q, (a, b) in enumerate(chunks(nt)):
                            ins = mm3(ps[:, 4 + 2 * c + q, 0:b - a], pwT[:, 0, c, :], pwT[:, 1, c, :],
                                      rs[:, c, 0, a:b], rs[:, c, 1, a:b], True, True)
                        ins.then_inc(pm_done, 1)
                for h in range(2):
                    for q, pair in enumerate(O_PAIRS):
                        n = SLAB_O + 4 * h + q
                        pe.wait_ge(lo_done, s * N_SLABS + n + 1)
                        if h == 0:
                            pe.wait_ge(mix_ready, 8 * s + (8 if q == 3 else 6))
                        elif q == 0:
                            pe.wait_ge(o_evac, 8 * s + 2)
                        for t in range(nt):
                            if h == 0 and q == 0 and t == 4:
                                pe.wait_ge(mix_ready, 8 * s + 7)
                            r = rows_of(t)
                            for kk, k in enumerate(pair):
                                ins = mm3(ps[0:r, o_bank(h, t), :],
                                          MH[:, 0, k, tokens(t)], MH[:, 1, k, tokens(t)],
                                          W[:, q, 0, 512 * kk:512 * kk + 512],
                                          W[:, q, 1, 512 * kk:512 * kk + 512],
                                          q == 0 and kk == 0, q == 3 and kk == 1)
                            if q == 3 and t < nt - 1:
                                ins.then_inc(o_done, 1)
                        ins.then_inc(slab_used, 1)
                for t in range(nt):
                    pe.wait_ge(xn_ready, 4 * s + t + 1)
                    transposes(s, nt, 1, t)

                def up(g, slab0, slot0):
                    for i in range(2):
                        if not (isinstance(g, int) and g == 0):
                            pe.wait_ge(relu_done, s * 32 + 2 * g + i - 1)
                        fm_product(s, slab0 + i, slot0 + i, i, nt)

                def down(g, parity, slab0, slot0):
                    pe.wait_ge(lo_done, s * N_SLABS + slab0 + 2)
                    pe.wait_ge(hid_ready, s * 32 + 2 * g + 2)
                    for t in range(nt):
                        r = rows_of(t)
                        for h in range(2):
                            j = 2 * t + h
                            if j >= 4 or not (isinstance(g, int) and g == 0):
                                pe.wait_ge(d_evac, s * 128 + g * (2 * nt) + j - 3)
                            last = j == 2 * nt - 1
                            for kk in range(2):
                                ins = mm3(ps[0:r, down_bank(nt, parity, j), :],
                                          MH[:, 0, 2 * parity + kk, tokens(t)],
                                          MH[:, 1, 2 * parity + kk, tokens(t)],
                                          W[:, slot0 + kk, 0, HALF * h:HALF * h + HALF],
                                          W[:, slot0 + kk, 1, HALF * h:HALF * h + HALF],
                                          kk == 0, kk == 1)
                                if last:
                                    ins.then_inc(slab_used, 1)
                            if not last:
                                ins.then_inc(d_done, 1)

                if nt == 5:
                    for c in range(2):
                        for q, a in enumerate((zlast[:, c, 0:CONV_BUF], zlast[:, c, CONV_BUF:],
                                               plast[:, c, 0:POOL_BUF], plast[:, c, POOL_BUF:])):
                            ins = pe.transpose(ps[0:a.shape[1], 4 + c, P * q:P * q + P], a, ident[:, :])
                    ins.then_inc(st_tr, 1)
                pe.wait_ge(hT_ready, 8 * s + 2 * nt)
                up(0, SLAB_UP0, 0)
                up(1, SLAB_UP0 + 2, 2)
                if nt == 5:
                    pe.wait_ge(st_rows, 8)
                down(0, 0, SLAB_UP0 + 4, 0)
                with pe.Fori(0, 7) as j:
                    for par in (1, 0):
                        g = 2 * j + (1 if par else 2)
                        up(g + 1, SLAB_UP0 + 2 + 4 * g, 2)
                        down(g, par, SLAB_UP0 + 4 + 4 * g, 0)
                down(15, 1, 86, 2)

            with pe.Fori(0, SUPERS - 1) as s:
                super_pe(s, 4)
            super_pe(SUPERS - 1, 5)

        @block.vector
        def _(dve):
            base, local = [0], [0]

            def step(ins):
                ins.then_inc(s_chain, 1)
                local[0] += 1

            def sync():
                dve.wait_ge(s_chain, base[0] + local[0])

            def do(ins):
                step(ins)
                sync()

            def signal(ins, sem_, value):
                ins.then_inc(sem_, 1)
                dve.wait_ge(sem_, value)

            dve.wait_ge(s_prepe, 1)
            do(dve.tensor_copy(zstate[:, :, :], ps[:, 6, 0:32].rearrange("p (c n) -> p c n", c=2)))
            do(dve.tensor_copy(pstate[:, :, :], ps[:, 6, 128:368].rearrange("p (c n) -> p c n", c=2)))
            dve.wait_ge(s_prep, 1)
            dve.tensor_copy(raw[:, 1, :].rearrange("p (b n) -> p b n", b=2), ps[:, 4:6, :]).then_inc(s_pret, 1)

            def ada_bias(cc, i, j):
                dve.wait_ge(s_ada_mm, cc + 1)
                if not (isinstance(i, int) and i == 0):
                    dve.wait_ge(s_ada_out[j], 16 * i)
                dve.tensor_tensor(rows[0:1 + NB, 1, 512 * j:512 * j + 512], ps[0:1 + NB, j, :],
                                  rows[0:1 + NB, 0, 512 * j:512 * j + 512], ALU.add).then_inc(s_ada_row, 1)

            def ada_T(cc, j):
                dve.wait_ge(s_ada_tr, cc + 1)
                dve.tensor_copy(modT[:, bass.ds(cc * 4, 4), :],
                                ps[:, 2 + j, 0:4 * (1 + NB)].rearrange("p (q n) -> p q n", q=4)
                                ).then_inc(s_ada_T, 1)

            for j in range(2):
                ada_bias(j, 0, j)
            for j in range(2):
                ada_T(j, j)
            with dve.Fori(1, 6) as i:
                for j in range(2):
                    ada_bias(2 * i + j, i, j)
                for j in range(2):
                    ada_T(2 * i + j, j)
            dve.wait_ge(s_ada_T, 12)
            for q in (SC1, SC2):
                m = modT[:, q * KD:q * KD + KD, :]
                do(dve.tensor_scalar(m, m, 1.0, None, ALU.add))
            sh2, sc2 = (modT[:, q * KD:q * KD + KD, :] for q in (SH2, SC2))
            lng, lnb = (lnT[:, i, :].unsqueeze(2).to_broadcast([P, KD, 1 + NB]) for i in range(2))
            do(dve.tensor_tensor(scale2[:, :, :], sc2, lng, ALU.mult))
            do(dve.tensor_tensor(bias2[:, :, :], sc2, lnb, ALU.mult))
            dve.wait_ge(s_prep, 2)
            dve.tensor_tensor(bias2[:, :, :], bias2[:, :, :], sh2, ALU.add).then_inc(s_ready, 1)
            prelude_steps = local[0]

            def rsqrt(n):
                var, y, u = mv[:, 0:n, 1], rstd[:, 0:n], rtmp[:, 0:n]
                do(dve.tensor_scalar(var, var, EPS, None, ALU.add))
                do(dve.tensor_scalar(y.bitcast(I32), var.bitcast(I32), 1, None, ALU.logical_shift_right))
                do(dve.tensor_scalar(y.bitcast(I32), y.bitcast(I32), -1.0, RSQRT_MAGIC, ALU.mult, ALU.add))
                for _ in range(3):
                    do(dve.tensor_tensor(u, y, y, ALU.mult))
                    do(dve.scalar_tensor_tensor(u, u, -0.5, var, ALU.mult, ALU.mult))
                    do(dve.scalar_tensor_tensor(y, u, 1.5, y, ALU.add, ALU.mult))

            def stats(t, parts):
                r = rows_of(t)
                for i, a in enumerate(parts):
                    step(dve.bn_stats(st[0:r, i, :], a))
                sync()
                dve.sem_inc(s_fence_dve, 1)
                do(dve.bn_aggr(mv[0:r, t, :], st[0:r, 0:len(parts), :].rearrange("p a b -> p (a b)")))

            def normalise(out, x, t):
                r = rows_of(t)
                return dve.tensor_scalar(out, x, mv[0:r, t, 0:1], rstd[0:r, t:t + 1],
                                         ALU.subtract, ALU.mult)

            def split(hi, lo, x):
                do(dve.tensor_copy(hi, x))
                return dve.tensor_tensor(lo, x, hi, ALU.subtract)

            def hT_tile(s, nt, phase, t):
                r = rows_of(t)
                x = acc[:, t, 0:KD * r].rearrange("p (k n) -> p k n", k=KD)
                if t < 4:
                    dve.wait_ge(tmp_ready, 8 * s + 4 * phase + t + 1)
                else:
                    dve.wait_ge(tr_done, 8 * s + phase * nt + t + 1)
                    mul = modT[:, SC1 * KD:SC1 * KD + KD, 1:] if phase == 0 else scale2[:, :, 1:]
                    add = modT[:, SH1 * KD:SH1 * KD + KD, 1:] if phase == 0 else bias2[:, :, 1:]
                    for half in range(2):
                        ks = slice(4 * half, 4 * half + 4)
                        o = x[:, ks, :].rearrange("p k (b t) -> p k b t", b=NB)
                        src = ps[:, TR_BANK[t % 2] + half, :].rearrange("p (k n) -> p k n", k=4)[:, :, 0:ST]
                        src = src.rearrange("p k (b t) -> p k b t", b=NB)
                        do(dve.tensor_tensor(o, src, mul[:, ks, :].unsqueeze(3).to_broadcast([P, 4, NB, DT]),
                                             ALU.mult))
                        do(dve.tensor_tensor(o, o, add[:, ks, :].unsqueeze(3).to_broadcast([P, 4, NB, DT]),
                                             ALU.add))
                signal(split(hT[:, 0, :, tokens(t)], hT[:, 1, :, tokens(t)], x),
                       hT_ready, 8 * s + phase * nt + t + 1)

            def v_tile(s, nt, t, pos):
                r = rows_of(t)
                x = htmp[0:r, 1, 0:W_GMLP] if t < 4 else gs[0:r, 0:W_GMLP]
                do(normalise(x, ps[0:r, V_BANK[t], :], t))
                do(dve.tensor_tensor(x, x, sgu_gb[0:r, 0, :], ALU.mult))
                do(dve.tensor_tensor(x, x, sgu_gb[0:r, 1, :], ALU.add))
                signal(split(rs[0:r, pos % 2, 0, 0:W_GMLP], rs[0:r, pos % 2, 1, 0:W_GMLP], x),
                       v_norm, 4 * s + pos + 1)

            def sgu_half(s, t, half, count):
                dve.wait_ge(sgu_done, 8 * s + count)
                r = rows_of(t)
                pr = slice(2 * half, 2 * half + 2)
                for odd in range(2):
                    q = slice(64 * odd, 64 * odd + 64)
                    src = ps[q, V_BANK[t], 0:4 * r].rearrange("p (a h i) -> p a h i", a=2, h=2)[:, :, odd, :]
                    dst = sg[q, pr, tokens(t)]
                    bias = bsR[q, pr, 0:r]
                    if t == 4:
                        src = src.rearrange("p a (b i) -> p a b i", b=NB)
                        dst = dst.rearrange("p a (b i) -> p a b i", b=NB)
                        bias = bsR[q, pr, 0:DT].unsqueeze(2).to_broadcast([64, 2, NB, DT])
                    if odd:
                        dve.tensor_tensor(dst, src, bias, ALU.add).then_inc(sgu_evac, 1)
                    else:
                        step(dve.tensor_tensor(dst, src, bias, ALU.add))

            def copy_pieces(s, f, nt, prompt, sample, other=None):
                ps_ = pieces(f % 2, nt)
                for n, (src, a) in enumerate(ps_):
                    w = src.shape[1]
                    if a is not None:
                        dst = prompt[:, a:a + w]
                        o = None if other is None else other[:, a:a + w]
                    else:
                        src = src.rearrange("p (b i) -> p b i", b=NB)
                        dst = sample
                        o = None if other is None else other[:, GT:GT + ST].rearrange("p (b i) -> p b i", b=NB)
                    ins = dve.tensor_copy(dst, src) if o is None else dve.tensor_tensor(dst, src, o, ALU.mult)
                    if n == len(ps_) - 1:
                        ins.then_inc(fm_evac, 1)
                    else:
                        step(ins)

            mix_order = [0, 1, 2, 6, 3, 7, 4, 5]

            def mix_out(s, nt, k, x):
                n = GT + (ST if nt == 5 else 0)
                signal(split(MH[:, 0, k, 0:n], MH[:, 1, k, 0:n], x),
                       mix_ready, 8 * s + mix_order.index(k) + 1)

            def wait_fm(s, f):
                dve.wait_ge(slab_used, s * N_SLABS + SLAB_FM + f + 1)

            def conv_fm(s, nt, f):
                c, what = f // 3, f % 3
                wait_fm(s, f)
                if what == 0:
                    dve.tensor_copy(as_fm(htmp[:, 0, :], nt), fm_view(f % 2, nt)).then_inc(fm_evac, 1)
                    dve.wait_ge(fm_evac, s * N_FM + f + 1)
                elif what == 1:
                    do(dve.tensor_copy(zp_[:, 0:CONV_BUF], zcarry[:, c, :]))
                    if nt == 5:
                        do(dve.tensor_copy(zs_[:, :, 0:CONV_BUF],
                                           zstate[:, c, :].rearrange("p (b n) -> p b n", b=NB)))
                    copy_pieces(s, f, nt, zp_[:, CONV_BUF:], zs_[:, :, CONV_BUF:], htmp[:, 0, :])
                    sync()
                    dve.wait_ge(fm_evac, s * N_FM + f + 1)
                    seqs = [(bufA[:, 0:GT], lambda a: zp_[:, a:a + GT])]
                    if nt == 5:
                        seqs.append((bufA[:, GT:GT + ST].rearrange("p (b i) -> p b i", b=NB),
                                     lambda a: zs_[:, :, a:a + DT]))
                    for o, z in seqs:
                        do(dve.tensor_scalar(o, z(0), convw[:, c, 0:1], None, ALU.mult))
                        for a in (1, 2):
                            do(dve.scalar_tensor_tensor(o, z(a), convw[:, c, a:a + 1], o, ALU.mult, ALU.add))
                    step(dve.tensor_copy(zcarry[:, c, :], zp_[:, GT:GT + CONV_BUF]))
                    if nt == 5:
                        step(dve.tensor_copy(zlast[:, c, 0:CONV_BUF], zp_[:, GT:GT + CONV_BUF]))
                        step(dve.tensor_copy(
                            zlast[:, c, CONV_BUF:].rearrange("p (b n) -> p b n", b=NB), zs_[:, :, DT:]))
                    sync()
                else:
                    dve.tensor_tensor(as_fm(bufB, nt), fm_view(f % 2, nt), as_fm(bufA, nt),
                                      ALU.mult).then_inc(fm_evac, 1)
                    dve.wait_ge(fm_evac, s * N_FM + f + 1)
                    mix_out(s, nt, c, bufB[:, 0:GT + (ST if nt == 5 else 0)])

            def pool_fm(s, nt, f):
                c = f - 6
                wait_fm(s, f)
                do(dve.tensor_copy(pp_[:, 0:POOL_BUF], pcarry[:, c, :]))
                if nt == 5:
                    do(dve.tensor_copy(psm[:, :, 0:POOL_BUF],
                                       pstate[:, c, :].rearrange("p (b n) -> p b n", b=NB)))
                copy_pieces(s, f, nt, pp_[:, POOL_BUF:], psm[:, :, POOL_BUF:])
                sync()
                dve.wait_ge(fm_evac, s * N_FM + f + 1)
                seqs = [(pp_, lambda b, lo, hi: b[:, lo:hi], GT, htmp[:, 0, 0:GT], lambda b: b)]
                if nt == 5:
                    seqs.append((psm, lambda b, lo, hi: b[:, :, lo:hi], DT,
                                 htmp[:, 0, GT:GT + ST].rearrange("p (b i) -> p b i", b=NB),
                                 lambda b: b[:, 0:NB * (POOL_BUF + DT)].rearrange("p (b n) -> p b n", b=NB)))
                for z, cut, n, d, shape in seqs:
                    L = POOL_BUF + n
                    A, B = shape(bufA), shape(bufB)
                    do(dve.tensor_tensor(cut(A, 1, L), cut(z, 1, L), cut(z, 0, L - 1), ALU.add))
                    do(dve.tensor_tensor(cut(B, 3, L), cut(A, 3, L), cut(A, 1, L - 2), ALU.add))
                    if c == 1:
                        do(dve.tensor_tensor(cut(A, 7, L), cut(B, 7, L), cut(B, 3, L - 4), ALU.add))
                        do(dve.tensor_tensor(cut(B, 15, L), cut(A, 15, L), cut(A, 7, L - 8), ALU.add))
                    for q, S in ((slice(0, 64), A), (slice(64, P), B)):
                        step(dve.scalar_tensor_tensor(d[q], cut(S, POOL_BUF, L)[q], invw[q, c:c + 1],
                                                      cut(z, POOL_BUF, L)[q], ALU.mult, ALU.subtract))
                    sync()
                    if n == GT:
                        for q, S in ((slice(0, 64), A), (slice(64, P), B)):
                            step(dve.tensor_tensor(d[q, 0:16], S[q, POOL_BUF:POOL_BUF + 16],
                                                   invtab[q, c, :], ALU.mult))
                        sync()
                        do(dve.tensor_tensor(d[:, 0:16], d[:, 0:16], z[:, POOL_BUF:POOL_BUF + 16],
                                             ALU.subtract))
                do(dve.tensor_scalar(invtab[:, c, :], invtab[:, c, :], 0.0, invw[:, c:c + 1],
                                     ALU.mult, ALU.add))
                step(dve.tensor_copy(pcarry[:, c, :], pp_[:, GT:GT + POOL_BUF]))
                if nt == 5:
                    step(dve.tensor_copy(plast[:, c, 0:POOL_BUF], pp_[:, GT:GT + POOL_BUF]))
                    step(dve.tensor_copy(
                        plast[:, c, POOL_BUF:].rearrange("p (b n) -> p b n", b=NB), psm[:, :, DT:]))
                sync()
                n = GT + (ST if nt == 5 else 0)
                signal(split(rs[:, c, 0, 0:n], rs[:, c, 1, 0:n], htmp[:, 0, 0:n]), d_ready, 2 * s + c + 1)

            def pool_out(s, nt, c):
                dve.wait_ge(pm_done, 2 * s + c + 1)
                pv = fm_view(2 + c, nt)
                k = 6 + c
                do(dve.tensor_scalar(as_fm(bufA, nt), pv, pscale[:, c:c + 1], None, ALU.mult))
                mix_out(s, nt, k, bufA[:, 0:GT + (ST if nt == 5 else 0)])

            def u_fm(s, nt, f):
                c = f - 8
                wait_fm(s, f)
                dve.tensor_tensor(as_fm(bufB, nt), fm_view(f % 2, nt), as_fm(sg[:, c, :], nt),
                                  ALU.mult).then_inc(fm_evac, 1)
                dve.wait_ge(fm_evac, s * N_FM + f + 1)
                mix_out(s, nt, 2 + c, bufB[:, 0:GT + (ST if nt == 5 else 0)])

            def gate_rows(t):
                return rows[:, 0, :] if t < 4 else gs[0:ST, :]

            def residual(t, cols, src, sem_, tmp):
                r = rows_of(t)
                ins = dve.tensor_tensor(tmp, src, gate_rows(t)[0:r, cols], ALU.mult)
                if sem_ is None:
                    do(ins)
                else:
                    ins.then_inc(sem_[0], 1)
                    dve.wait_ge(sem_[0], sem_[1])
                x = xt[0:r, t, cols]
                return dve.scalar_tensor_tensor(x, x, ALPHA, tmp, ALU.mult, ALU.add)

            def super_dve(s, nt, per_super):
                base[0] = prelude_steps + s * per_super
                local[0] = 0
                for t in range(nt):
                    hT_tile(s, nt, 0, t)
                dve.wait_ge(slab_used, s * N_SLABS + 4)
                for t in range(nt):
                    stats(t, [ps[0:rows_of(t), V_BANK[t], :]])
                rsqrt(nt)
                halves = [0]
                todo = list(enumerate(vorder(nt)))

                def two_v():
                    for _ in range(2):
                        if todo:
                            pos, t = todo.pop(0)
                            v_tile(s, nt, t, pos)

                two_v()
                for stage in mixer_stages(nt):
                    if stage[0] == "F":
                        f = stage[1]
                        (conv_fm if f < 6 else pool_fm if f < 8 else u_fm)(s, nt, f)
                    elif stage[0] == "S":
                        for half in range(2):
                            for t in stage[1]:
                                halves[0] += 1
                                sgu_half(s, t, half, halves[0])
                        sync()
                        dve.wait_ge(sgu_evac, 8 * s + halves[0])
                        two_v()
                    else:
                        pool_out(s, nt, stage[1])
                dve.wait_ge(rows_loaded, 96 * s + 48)
                for h in range(2):
                    for t in range(nt):
                        if h == 0 and t == 4:
                            dve.wait_ge(gs_loaded, 16 * NB)
                        if t < nt - 1:
                            dve.wait_ge(o_done, 6 * s + (nt - 1) * h + t + 1)
                        else:
                            dve.wait_ge(slab_used, s * N_SLABS + SLAB_O + 4 * h + 4)
                        cols = slice(HALF * h, HALF * h + HALF)
                        r = rows_of(t)
                        do(residual(t, cols, ps[0:r, o_bank(h, t), :], (o_evac, 8 * s + nt * h + t + 1),
                                    htmp[0:r, t % 2, 0:HALF]))
                for t in range(nt):
                    r = rows_of(t)
                    stats(t, [xt[0:r, t, 0:512], xt[0:r, t, 512:1024]])
                rsqrt(nt)
                for t in range(nt):
                    r = rows_of(t)
                    signal(normalise(xt[0:r, t, :], xt[0:r, t, :], t), xn_ready, 4 * s + t + 1)
                for t in range(nt):
                    hT_tile(s, nt, 1, t)
                if nt == 5:
                    dve.wait_ge(st_tr, 1)
                    for q, (_, n, _) in enumerate(STATES):
                        for c in range(2):
                            dve.tensor_copy(gs[0:n, 2 * P * q + P * c:2 * P * q + P * c + P],
                                            ps[0:n, 4 + c, P * q:P * q + P]).then_inc(st_rows, 1)

                def hidden(f, i, parity):
                    dve.wait_ge(relu_done, s * 32 + f + 1)
                    n = GT + (ST if nt == 5 else 0)
                    k = 2 * parity + i
                    split_loop(MH[:, 0, k, 0:n], MH[:, 1, k, 0:n], htmp[:, i, 0:n], s, f)

                def split_loop(hi, lo, x, s, f):
                    dve.tensor_copy(hi, x).then_inc(s_hid_hi, 1)
                    dve.wait_ge(s_hid_hi, s * 32 + f + 1)
                    signal(dve.tensor_tensor(lo, x, hi, ALU.subtract), hid_ready, s * 32 + f + 1)

                def down(g, parity, first, last_slab):
                    for t in range(nt):
                        r = rows_of(t)
                        for h in range(2):
                            j = 2 * t + h
                            if j == 2 * nt - 1:
                                dve.wait_ge(slab_used, s * N_SLABS + last_slab + 1)
                            else:
                                dve.wait_ge(d_done, s * 112 + g * (2 * nt - 1) + j + 1)
                            a = acc[0:r, t, HALF * h:HALF * h + HALF]
                            src = ps[0:r, down_bank(nt, parity, j), :]
                            if first:
                                dve.tensor_copy(a, src).then_inc(d_evac, 1)
                            else:
                                dve.wait_ge(d_evac, s * 128 + (g - 1) * (2 * nt) + j + 1)
                                dve.tensor_tensor(a, a, src, ALU.add).then_inc(d_evac, 1)

                for i in range(2):
                    hidden(i, i, 0)
                for t in range(nt):
                    r = rows_of(t)
                    x = xt[0:r, t, :]
                    do(dve.tensor_tensor(x, x, rows[0:r, 1, :], ALU.mult))
                    ins = dve.tensor_tensor(x, x, rows[0:r, 2, :], ALU.add)
                    if t == nt - 1:
                        signal(ins, x1_ready, s + 1)
                    else:
                        step(ins)
                for i in range(2):
                    hidden(2 + i, i, 1)
                down(0, 0, True, SLAB_UP0 + 5)
                with dve.Fori(0, 7) as jj:
                    for par in (0, 1):
                        g = 2 * jj + 1 + par
                        for i in range(2):
                            hidden(2 * g + 2 + i, i, par)
                        down(g, 1 - par, False, SLAB_UP0 + 5 + 4 * g)
                down(15, 1, False, 87)
                dve.wait_ge(rows_loaded, 96 * s + 96)
                if nt == 5:
                    dve.wait_ge(gs_loaded, 2 * 16 * NB)
                dve.wait_ge(d_evac, s * 128 + 16 * 2 * nt)
                for t in range(nt):
                    r = rows_of(t)
                    a = acc[0:r, t, :]
                    do(dve.tensor_tensor(a, a, gate_rows(t)[0:r, :], ALU.mult))
                    do(dve.scalar_tensor_tensor(a, xt[0:r, t, :], ALPHA, a, ALU.mult, ALU.add))
                    stats(t, [acc[0:r, t, 0:512], acc[0:r, t, 512:1024]])
                rsqrt(nt)
                for t in range(nt):
                    r = rows_of(t)
                    a = acc[0:r, t, :]
                    do(normalise(a, a, t))
                    do(dve.tensor_tensor(a, a, rows[0:r, 1, :], ALU.mult))
                    signal(dve.tensor_tensor(a, a, rows[0:r, 2, :], ALU.add), y_ready, 4 * s + t + 1)
                return local[0]

            with dve.Fori(0, SUPERS - 1) as s:
                used = super_dve(s, 4, DVE_STEPS)
                assert used == DVE_STEPS, used
            super_dve(SUPERS - 1, 5, DVE_STEPS)


_INS = ["x_prompt", "x_sample", "c_prompt", "c_sample", "state_conv", "state_pool", "w_ada", "b_ada",
        "w_in", "conv_w", "sgu_g", "sgu_b", "w_s", "b_s", "pool_w", "pool_scale", "w_out", "ln1_g",
        "ln1_b", "w_up", "w_down", "ln2_g", "ln2_b"]
_OUTS = [(1, SEQ, D), (NB, DT, D), (1, 1, CONV_BUF, W_CONV), (1, 1, POOL_BUF, W_POOL),
         (1, NB, CONV_BUF, W_CONV), (1, NB, POOL_BUF, W_POOL), (1, NB, DT, W_GMLP)]


def kernel(**inputs):
    import numpy as np
    import concourse.bacc as bacc
    from concourse.bass_utils import run_bass_kernel_spmd

    nc = bacc.Bacc("TRN2", target_bir_lowering=False, num_devices=1)
    arrays, args = {}, []
    for name in _INS:
        a = np.ascontiguousarray(inputs[name])
        arrays[f"in_{name}"] = a
        args.append(nc.dram_tensor(f"in_{name}", a.shape, mybir.dt.from_np(a.dtype), kind="ExternalInput").ap())
    for i, shape in enumerate(_OUTS):
        args.append(nc.dram_tensor(f"out_{i}", shape, F32, kind="ExternalOutput").ap())
    args.append(nc.dram_tensor("mod_rows", (1 + NB, 6 * D), F32).ap())
    decoder_layer_kernel(nc, *args)
    r = run_bass_kernel_spmd(nc, [arrays], core_ids=[0])
    return tuple(r.results[0][f"out_{i}"] for i in range(len(_OUTS)))
```

```python
from contextlib import ExitStack

import concourse.bass as bass
from concourse import mybir

F32 = mybir.dt.float32
F32R = mybir.dt.float32r
I32 = mybir.dt.int32
ACT = mybir.ActivationFunctionType
ALU = mybir.AluOpType

P = 128
D = 1024
KD = D // P
SEQ = 2048
GT = 512
SUPERS = SEQ // GT
NB, DT = 8, 8
ST = NB * DT
W_CONV, W_GMLP, W_POOL = 256, 512, 256
FF = 4 * D
HEADS = 8
HALF = D // 2
COL_B, COL_C, COL_X = 0, W_CONV, 2 * W_CONV
COL_U = 3 * W_CONV
COL_V = COL_U + W_GMLP
COL_P = COL_V + W_GMLP
CONV_BUF, POOL_BUF = 2, 15
WINDOWS = (2, 4, 8, 16)
ALPHA = 2.0 ** 0.25
EPS = 1e-5
RSQRT_MAGIC = float(0x5F3759DF)
SH1, SC1, G1, SH2, SC2, G2 = range(6)

SLOTS = 4
RAW = 2
N_SLABS = 88
SLAB_FM, SLAB_O, SLAB_UP0 = 4, 16, 24
N_FM = 12
MLP_GROUPS = 16
FM_COLS = [COL_C, COL_X, COL_B, COL_C + P, COL_X + P, COL_B + P, COL_P, COL_P + P] + \
          [COL_U + P * i for i in range(4)]
O_PAIRS = [(0, 1), (2, 3), (6, 7), (4, 5)]
XN_ACT = (0, 1, 3)
V_BANK = [4, 5, 6, 7, 3]
N_ADA = 24
ADA_COLS = 6 * D // N_ADA
ADA_FIRST = 2 * D // ADA_COLS


N_PRE = 3 + 2 + 2 + 2 + 1 + 2 + 1
DVE_STEPS = 195


def bcast(ap, n):
    return ap.partition_broadcast(n)


def o_bank(h, t):
    return (4 + 5 * h + t) % 8


def decoder_layer_kernel(nc, x_prompt, x_sample, c_prompt, c_sample, state_conv, state_pool,
                         w_ada, b_ada, w_in, conv_w, sgu_g, sgu_b, w_s, b_s, pool_w, pool_scale,
                         w_out, ln1_g, ln1_b, w_up, w_down, ln2_g, ln2_b,
                         y_prompt, y_sample, o_conv_p, o_pool_p, o_conv_s, o_pool_s, o_v_s,
                         mod_rows):
    ctx = ExitStack()
    with ctx:
        ctx.enter_context(nc.allow_non_contiguous_dma(reason="small tables turned by the DMA, once"))

        def sb(name, shape, dt=F32):
            return ctx.enter_context(nc.sbuf_tensor(name, shape, dt))

        def sem(name):
            return ctx.enter_context(nc.semaphore(name))

        W = sb("w_hilo", [P, SLOTS, 2, D], F32R)
        raw = sb("w_raw", [P, RAW, D])
        hT = sb("hT", [P, 2, KD, GT + ST], F32R)
        MH = sb("mixT_hidden", [P, 2, KD, GT + ST], F32R)
        xt = sb("xt", [P, 5, D])
        acc = sb("acc", [P, 5, D])
        rs = sb("rs", [P, 2, 2, GT + ST], F32R)
        wsT = sb("wsT", [P, 2, HEADS, P], F32R)
        wsS = sb("wsS", [P, 2, HEADS, ST], F32R)
        bsR = sb("bsR", [P, 4, P])
        pwT = sb("pwT", [P, 2, 2, P], F32R)
        ident = sb("ident", [P, P])
        modT = sb("modT", [P, 6 * KD, 1 + NB])
        scale2 = sb("scale2", [P, KD, 1 + NB])
        bias2 = sb("bias2", [P, KD, 1 + NB])
        rows = sb("rows", [P, 3, D])
        gs = sb("gs", [P, D])
        sgu_gb = sb("sgu_gb", [P, 2, W_GMLP])
        htmp = sb("htmp", [P, 2, GT + ST])
        convw = sb("convw", [P, 2, 3])
        pscale = sb("pscale", [P, 2])
        invw = sb("invw", [P, 2])
        invtab = sb("invtab", [P, 2, 16])
        zcarry = sb("zcarry", [P, 2, CONV_BUF])
        pcarry = sb("pcarry", [P, 2, POOL_BUF])
        zstate = sb("zstate", [P, 2, NB * CONV_BUF])
        pstate = sb("pstate", [P, 2, NB * POOL_BUF])
        lnT = sb("lnT", [P, 2, KD])
        st = sb("st", [P, 5, 2, 6])
        siluT = sb("siluT", [P, KD * (1 + NB)])
        ln_now = (sb("mv", [P, 5, 2]), sb("rstd", [P, 5]), sb("rtmp", [P, 5]))
        ln_end = (sb("mv_end", [P, 5, 2]), sb("rstd_end", [P, 5]), sb("rtmp_end", [P, 5]))
        ps = ctx.enter_context(nc.psum_tensor("ps", [P, 8, 512], F32))

        flat = acc[:, :, :].rearrange("p t d -> p (t d)")
        off = [0]

        def scratch(n):
            off[0] += n
            assert off[0] <= 5 * D
            return flat[:, off[0] - n:off[0]]

        sg = scratch(4 * (GT + ST)).rearrange("p (c n) -> p c n", c=4)
        zp_ = scratch(CONV_BUF + GT)
        zs_ = scratch(NB * (CONV_BUF + DT)).rearrange("p (b n) -> p b n", b=NB)
        pp_ = scratch(POOL_BUF + GT)
        psm = scratch(NB * (POOL_BUF + DT)).rearrange("p (b n) -> p b n", b=NB)
        bufA = scratch(GT + ST)
        bufB = scratch(GT + ST)
        zlast = scratch(2 * (CONV_BUF + NB * CONV_BUF)).rearrange("p (c n) -> p c n", c=2)
        plast = scratch(2 * (POOL_BUF + NB * POOL_BUF)).rearrange("p (c n) -> p c n", c=2)

        STATES = [(o_conv_p[0, 0], CONV_BUF, 0), (o_conv_s[0].rearrange("b r c -> (b r) c"), NB * CONV_BUF, 1),
                  (o_pool_p[0, 0], POOL_BUF, 2), (o_pool_s[0].rearrange("b r c -> (b r) c"), NB * POOL_BUF, 3)]

        s_c = sem("s_c")
        s_pre = sem("s_pre")
        x0_loaded = sem("x0_loaded")
        ada_in = [sem(f"ada_in{i}") for i in range(4)]
        ada_mm = sem("ada_mm")
        ada_row = sem("ada_row")
        ada_tr = sem("ada_tr")
        ada_T = sem("ada_T")
        ada_out = [sem(f"ada_out{i}") for i in range(4)]
        s_mod1 = sem("s_mod1")
        s_mod2 = sem("s_mod2")
        s_corner = sem("s_corner")
        s_fence = sem("s_fence")
        s_cT = sem("s_cT")
        s_ident = sem("s_ident")
        xs_split = sem("xs_split")
        s_silu = sem("s_silu")
        s_prepe = sem("s_prepe")
        s_prep = sem("s_prep")
        s_pool0 = sem("s_pool0")
        s_pret = sem("s_pret")
        s_chain = sem("s_chain")
        s_chain_act = sem("s_chain_act")
        raw_loaded = [sem(f"raw_loaded{i}") for i in range(RAW)]
        hi_done = sem("hi_done")
        lo_done = sem("lo_done")
        slab_used = sem("slab_used")
        x_loaded = [sem(f"x_loaded{t}") for t in range(5)]
        rows_loaded = sem("rows_loaded")
        gs_loaded = sem("gs_loaded")
        gs_x = sem("gs_x")
        xt_tr = sem("xt_tr")
        x_tmp = sem("x_tmp")
        x_split = sem("x_split")
        xs_tr = sem("xs_tr")
        o_tr = sem("o_tr")
        o_tmp = sem("o_tmp")
        o_split = sem("o_split")
        v_done = sem("v_done")
        v_norm = sem("v_norm")
        sgu_done = sem("sgu_done")
        sgu_evac = sem("sgu_evac")
        fm_evac = sem("fm_evac")
        d_ready = sem("d_ready")
        pm_done = sem("pm_done")
        mix_ready = sem("mix_ready")
        o_done = sem("o_done")
        o_evac = sem("o_evac")
        o_stats = sem("o_stats")
        xn_act = sem("xn_act")
        xn_dve = sem("xn_dve")
        x1_ready = sem("x1_ready")
        relu_done = sem("relu_done")
        hid_ready = sem("hid_ready")
        d_done = sem("d_done")
        d_evac = sem("d_evac")
        y_ready = sem("y_ready")
        acc_gated = sem("acc_gated")
        e_stats = sem("e_stats")
        e_norm = sem("e_norm")
        y_scaled = sem("y_scaled")
        y_stored = sem("y_stored")
        v_stored = sem("v_stored")
        s_hid_hi = sem("s_hid_hi")
        st_tr = sem("st_tr")
        st_rows = sem("st_rows")
        st_stored = sem("st_stored")

        w_in_v = w_in[0].rearrange("(k p) e -> p k e", p=P)
        w_out_v = w_out[0].rearrange("(k p) e -> p k e", p=P)
        w_up_v = w_up[0].rearrange("(k p) e -> p k e", p=P)
        w_down_v = w_down[0].rearrange("(f p) e -> p f e", p=P)
        w_ada_v = w_ada[0].rearrange("(k p) e -> p k e", p=P)

        def rows_of(t):
            return P if t < 4 else ST

        def tokens(t):
            return slice(P * t, P * t + rows_of(t))

        def chunks(nt):
            return [(0, GT)] if nt == 4 else [(0, (GT + ST) // 2), ((GT + ST) // 2, GT + ST)]

        def fm_bank(f, nt, first=False):
            if nt == 5 or first:
                return 2 * (f % 2)
            return f % 4

        def fm_turns(nt, first):
            return 2 if nt == 5 or first else 4

        def fm_view(bank, nt):
            n = GT if nt == 4 else (GT + ST) // 2
            return ps[:, bank:bank + len(chunks(nt)), 0:n]

        def as_fm(ap, nt):
            return ap[:, 0:GT + (ST if nt == 5 else 0)].rearrange("p (c n) -> p c n", c=len(chunks(nt)))

        def pieces(bank, nt):
            if nt == 4:
                return [(ps[:, bank, 0:GT], 0)]
            n = (GT + ST) // 2
            return [(ps[:, bank, 0:n], 0), (ps[:, bank + 1, 0:GT - n], n),
                    (ps[:, bank + 1, GT - n:n], None)]

        def v_order(nt):
            return [0, 1, 2, 3] if nt == 4 else [4, 0, 1, 2, 3]

        def mixer_stages(nt, first, vector):
            F = [("F", n) for n in range(N_FM)]
            tail = F[8:10] + [("M", 0), F[10], ("M", 1), F[11]]
            if nt == 5:
                a = [F[0], ("S", [4, 0], 0), ("V",), F[1], F[2], ("S", [1, 2], 2), ("V",), F[3], F[4],
                     ("S", [3], 4), ("N", 0), F[5], ("N", 1), F[6], ("N", 2), F[7], ("N", 3)]
            elif first:
                a = [F[0], F[1], ("S", [0, 1], 0), ("V",), F[2], F[3], ("S", [2, 3], 2)] + F[4:8]
            elif vector:
                a = [F[0], F[1], ("S", [0, 1], 0), ("V",), F[2], F[3], ("S", [2, 3], 2),
                     F[4], ("N", 0), F[5], ("N", 1), F[6], ("N", 2), F[7], ("N", 3)]
            else:
                a = F[0:4] + [("S", [0, 1], 0), F[4], F[5], ("S", [2, 3], 2), F[6], F[7]]
            a = a + tail
            if first:
                out, u = [], ADA_FIRST
                for x in a:
                    out.append(x)
                    if x[0] == "F":
                        for _ in range(2 if x[1] < 4 else 1):
                            out.append(("A", u))
                            u += 1
                a = out + [("E", u - 1)]
            return [x for x in a if vector or x[0] not in "VN"]

        def ada_pieces_after(f):
            return [ADA_FIRST + 2 * f, ADA_FIRST + 2 * f + 1] if f < 4 else [ADA_FIRST + 4 + f]

        def ada_buffer(u):
            b = (u % 4) if u < ADA_FIRST else (u % 2)
            t = (xt if b < 2 else acc)[:, 2 * (b % 2):2 * (b % 2) + 2, :]
            return t.rearrange("p t (a n) -> p (t a) n", a=4)

        def ada_bias(u):
            return gs[0:1 + NB, ADA_COLS * (u % 4):ADA_COLS * (u % 4) + ADA_COLS]

        x0_tile = [acc[:, 4, :], rows[:, 1, :], rows[:, 0, :], rows[:, 2, :]]

        def down_bank(nt, parity, j):
            return 4 + (2 * nt * parity + j) % 4

        def sgu_bank(nt, t, half):
            return 4 if nt == 5 and half and t in (1, 3) else V_BANK[t]

        block = ctx.enter_context(nc.Block())

        @block.sync
        def _(sp):
            def ada_weights(u):
                if u >= 4:
                    sp.wait_ge(ada_mm, u - 3 if u < ADA_FIRST + 2 else u - 1)
                sp.dma_start(ada_buffer(u), w_ada_v[:, :, ADA_COLS * u:ADA_COLS * u + ADA_COLS]
                             ).then_inc(ada_in[u % 4], 16)

            def ada_bias_in(u):
                if u >= 4:
                    sp.wait_ge(ada_tr, u - 3)
                    sp.wait_ge(ada_out[u % 4], 16 * (u // 4))
                sp.dma_start(ada_bias(u), bcast(b_ada[0, ADA_COLS * u:ADA_COLS * u + ADA_COLS], 1 + NB)
                             ).then_inc(ada_in[u % 4], 16)

            def ada_rows_out(u):
                sp.wait_ge(ada_row, u + 1)
                sp.dma_start(mod_rows[:, ADA_COLS * u:ADA_COLS * u + ADA_COLS], ada_bias(u)
                             ).then_inc(ada_out[u % 4], 16)

            def ada_piece(u):
                ada_weights(u)
                ada_rows_out(u - 3)
                ada_bias_in(u)

            def x0_load(t):
                sp.dma_start(x0_tile[t], x_prompt[0, P * t:P * t + P, :]).then_inc(x0_loaded, 16)

            sp.dma_start(rows[0:1, 2, :], c_prompt).then_inc(s_c, 16)
            sp.dma_start(rows[1:1 + NB, 2, :], c_sample).then_inc(s_c, 16)
            for u in range(4):
                ada_weights(u)
                ada_bias_in(u)
            sp.dma_start(rows[:, 0, :].rearrange("p (h j) -> p h j", h=HEADS),
                         w_s[0].rearrange("h i j -> i h j")).then_inc(s_pre, 16)
            sp.dma_start(htmp[0:NB * CONV_BUF, 0, 0:W_CONV],
                         state_conv[0].rearrange("b r c -> (b r) c")).then_inc(s_pre, 16)
            sp.dma_start(htmp[0:NB * POOL_BUF, 1, 0:W_POOL],
                         state_pool[0].rearrange("b r c -> (b r) c")).then_inc(s_pre, 16)
            for half in range(2):
                sp.dma_start(bsR[64 * half:64 * half + 64, :, :],
                             bcast(b_s[0].rearrange("(q two) i -> two q i", two=2)[half], 64)
                             ).then_inc(s_pre, 16)
            sp.dma_start(sgu_gb[:, 0, :], bcast(sgu_g[0], P)).then_inc(s_pre, 16)
            sp.dma_start(sgu_gb[:, 1, :], bcast(sgu_b[0], P)).then_inc(s_pre, 16)
            for c in range(2):
                sp.dma_start(convw[:, c, :],
                             conv_w[0, :, P * c:P * c + P].rearrange("w p -> p w")).then_inc(s_pre, 16)
            sp.dma_start(pscale[:, :], pool_scale[0].rearrange("(c p) -> p c", p=P)).then_inc(s_pre, 16)
            sp.dma_start(lnT[:, 0, :], ln1_g[0].rearrange("(k p) -> p k", p=P)).then_inc(s_pre, 16)
            sp.dma_start(lnT[:, 1, :], ln1_b[0].rearrange("(k p) -> p k", p=P)).then_inc(s_pre, 16)
            sp.dma_start(xt[0:ST, 4, :], x_sample.rearrange("b t d -> (b t) d")).then_inc(s_pre, 16)
            ada_rows_out(0)
            ada_piece(4)
            for t in range(2):
                x0_load(t)
            sp.wait_ge(s_prep, 1)
            for g in range(4):
                q, c = 64 * (g % 2), g // 2
                sp.dma_start(raw[q:q + 64, 0, P * c + q:P * c + q + 64], pool_w[0, g]).then_inc(s_corner, 16)
            ada_piece(5)
            sp.wait_ge(s_pret, 1)
            for b in range(NB):
                sp.dma_start(raw[DT * b:DT * b + DT, 0, 2 * P:2 * P + HEADS * ST].rearrange(
                                 "p (h i) -> p h i", h=HEADS)[:, :, DT * b:DT * b + DT],
                             raw[0:DT, 1, :].rearrange("p (h i) -> p h i", h=HEADS)[:, :, 0:DT]
                             ).then_inc(s_corner, 16)
            ada_piece(6)
            for t in (2, 3):
                x0_load(t)
            ada_piece(7)

            def slab(s, n, src, sizes, i=None, free=True):
                slot = (n if i is None else i) % RAW
                if free:
                    sp.wait_ge(lo_done, s * N_SLABS + n - RAW + 1)
                dst = raw[:, slot, :]
                if sizes:
                    dst = dst.rearrange("p (k n) -> p k n", k=sizes)
                sp.dma_start(dst, src).then_inc(raw_loaded[slot], 16)

            def early_slab(s, n, free=True):
                if n < SLAB_FM:
                    slab(s, n, w_in_v[:, 2 * n:2 * n + 2, COL_V:COL_V + W_GMLP], 2, free=free)
                elif n < SLAB_O:
                    col = FM_COLS[n - SLAB_FM]
                    slab(s, n, w_in_v[:, :, col:col + P], KD)
                else:
                    h, k = (n - SLAB_O) // 4, O_PAIRS[(n - SLAB_O) % 4][0]
                    slab(s, n, w_out_v[:, k:k + 2, HALF * h:HALF * h + HALF], 2)

            def load_residual(s):
                for t in range(4):
                    sp.dma_start(xt[:, t, :], x_prompt[0, bass.ds(s * GT + P * t, P), :]
                                 ).then_inc(x_loaded[t], 16)
                sp.dma_start(rows[:, 0, :], bcast(mod_rows[0, G1 * D:G1 * D + D], P)).then_inc(rows_loaded, 16)
                sp.dma_start(rows[:, 1, :], bcast(ln1_g[0], P)).then_inc(rows_loaded, 16)
                sp.dma_start(rows[:, 2, :], bcast(ln1_b[0], P)).then_inc(rows_loaded, 16)

            def load_gs(which):
                for b in range(NB):
                    sp.dma_start(gs[DT * b:DT * b + DT, :],
                                 bcast(mod_rows[1 + b, which * D:which * D + D], DT)).then_inc(gs_loaded, 16)

            def store(s, t):
                sp.wait_ge(y_ready, 4 * s + t + 1)
                if t < 4:
                    dst = y_prompt[0, bass.ds(s * GT + P * t, P), :]
                else:
                    dst = y_sample.rearrange("b t d -> (b t) d")
                sp.dma_start(dst, xt[0:rows_of(t), t, :]).then_inc(y_stored, 16)

            def mixer_slab(s, n):
                early_slab(s, n)
                if 14 <= n < 18:
                    store(s - 1, n - 14)
                if n == 18:
                    sp.wait_ge(y_stored, 64 * s)
                    load_residual(s)

            def mlp_dma(s, nt, last):
                def up(g, f, i, n):
                    slab(s, n, w_up_v[:, :, bass.ds(f * P, P)], KD, i)

                def down(f, i, n):
                    slab(s, n, w_down_v[:, bass.ds(f, 1), :].rearrange("p a n -> p (a n)"), 0, i)

                def next_x(t):
                    if t:
                        sp.wait_ge(xt_tr, 4 * s + 4 + t)
                    sp.dma_start(gs[:, :], x_prompt[0, bass.ds(s * GT + GT + P * t, P), :]).then_inc(gs_x, 16)

                for i in range(2):
                    up(0, i, i, SLAB_UP0 + i)
                for i in range(2):
                    up(1, 2 + i, i, SLAB_UP0 + 2 + i)
                for i in range(2):
                    down(i, i, SLAB_UP0 + 4 + i)
                with sp.Fori(1, 4) as g:
                    for i in range(2):
                        up(g + 1, 2 * g + 2 + i, i, SLAB_UP0 + 2 + 4 * g + i)
                    for i in range(2):
                        down(2 * g + i, i, SLAB_UP0 + 4 + 4 * g + i)
                sp.wait_ge(x1_ready, s + 1)
                sp.dma_start(rows[:, 0, :], bcast(mod_rows[0, G2 * D:G2 * D + D], P)).then_inc(rows_loaded, 16)
                sp.dma_start(rows[:, 1, :], bcast(ln2_g[0], P)).then_inc(rows_loaded, 16)
                sp.dma_start(rows[:, 2, :], bcast(ln2_b[0], P)).then_inc(rows_loaded, 16)
                if last:
                    sp.wait_ge(st_rows, 8)
                    for dst, n, q in STATES:
                        sp.dma_start(dst, gs[0:n, 2 * P * q:2 * P * q + 2 * P]).then_inc(st_stored, 16)
                    sp.wait_ge(st_stored, 16 * len(STATES))
                    load_gs(G2)
                else:
                    next_x(0)
                with sp.Fori(4, 15) as g:
                    for i in range(2):
                        up(g + 1, 2 * g + 2 + i, i, SLAB_UP0 + 2 + 4 * g + i)
                    for i in range(2):
                        down(2 * g + i, i, SLAB_UP0 + 4 + 4 * g + i)
                for i in range(2):
                    down(30 + i, i, 86 + i)
                if not last:
                    for n in range(12):
                        if n in (0, 2, 4):
                            next_x(1 + n // 2)
                        early_slab(s + 1, n)

            sp.wait_ge(s_prep, 2)
            for n in range(9):
                early_slab(0, n, free=n >= RAW)
            for f in range(N_FM):
                early_slab(0, 9 + f)
                for u in ada_pieces_after(f):
                    ada_piece(u)
            for u in range(N_ADA - 3, N_ADA):
                ada_rows_out(u)
            for i in range(4):
                sp.wait_ge(ada_out[i], 16 * (N_ADA // 4))
            sp.wait_ge(x_split, 8)
            load_residual(0)
            for n in range(21, 24):
                early_slab(0, n)
            mlp_dma(0, 4, False)
            with sp.Fori(1, SUPERS - 1) as s:
                for n in range(12, 24):
                    mixer_slab(s, n)
                mlp_dma(s, 4, False)
            s = SUPERS - 1
            for n in range(12, 16):
                mixer_slab(s, n)
            sp.wait_ge(v_norm, 4 * s + 1)
            sp.dma_start(o_v_s[0].rearrange("b t c -> (b t) c"), gs[0:ST, 0:W_GMLP]).then_inc(v_stored, 16)
            sp.wait_ge(v_stored, 16)
            load_gs(G1)
            for n in range(16, 24):
                mixer_slab(s, n)
            mlp_dma(s, 5, True)
            for t in range(5):
                store(s, t)
            sp.wait_ge(y_stored, 64 * SUPERS + 16)

        @block.gpsimd
        def _(pool):
            count = [0]

            def step(ins):
                count[0] += 1
                ins.then_inc(s_pool0, 1)
                pool.wait_ge(s_pool0, count[0])

            step(pool.memset(ident[:, :], 0.0))
            pool.affine_select(out=ident[:, :], in_=ident[:, :], compare_op=ALU.not_equal, fill=1.0,
                               base=0, pattern=[[-1, P]], channel_multiplier=1).then_inc(s_ident, 1)
            for m in (ln_now, ln_end):
                step(pool.memset(m[0][:, :, :], 1.0))
            pool.memset(raw[:, :, :], 0.0).then_inc(s_prep, 1)
            step(pool.memset(zcarry[:, :, :], 0.0))
            step(pool.memset(pcarry[:, :, :], 0.0))
            for g, w in enumerate(WINDOWS):
                q, c = 64 * (g % 2), g // 2
                step(pool.memset(invw[q:q + 64, c:c + 1], 1.0 / w))
                step(pool.memset(invtab[q:q + 64, c, :], 1.0 / w))
                for t in range(w - 1):
                    step(pool.memset(invtab[q:q + 64, c, t:t + 1], 1.0 / (t + 1)))
            pool.wait_ge(s_corner, 16 * (4 + NB))
            v = raw[0:ST, 0, 2 * P:2 * P + HEADS * ST].rearrange("p (h i) -> p h i", h=HEADS)
            step(pool.affine_select(out=v, in_=v, compare_op=ALU.is_ge, fill=0.0,
                                    base=0, pattern=[[0, HEADS], [1, ST]], channel_multiplier=-1))
            step(pool.tensor_copy(wsS[0:ST, 0, :, :], v))
            step(pool.tensor_tensor(wsS[0:ST, 1, :, :], v, wsS[0:ST, 0, :, :], ALU.subtract))
            v = raw[:, 0, 0:2 * P].rearrange("p (c n) -> p c n", c=2)
            step(pool.tensor_copy(pwT[:, 0, :, :], v))
            step(pool.tensor_tensor(pwT[:, 1, :, :], v, pwT[:, 0, :, :], ALU.subtract))
            v = raw[:, 1, :].rearrange("p (h i) -> p h i", h=HEADS)
            step(pool.affine_select(out=v, in_=v, compare_op=ALU.is_ge, fill=0.0,
                                    base=0, pattern=[[0, HEADS], [1, P]], channel_multiplier=-1))
            step(pool.tensor_copy(wsT[:, 0, :, :], v))
            pool.tensor_tensor(wsT[:, 1, :, :], v, wsT[:, 0, :, :], ALU.subtract).then_inc(s_prep, 1)

            with pool.Fori(0, SUPERS * N_SLABS // SLOTS) as i:
                for j in range(SLOTS):
                    pool.wait_ge(hi_done, SLOTS * i + j + 1)
                    pool.tensor_tensor(W[:, j, 1, :], raw[:, j % RAW, :], W[:, j, 0, :],
                                       ALU.subtract).then_inc(lo_done, 1)

            def gate_acc(t):
                pool.wait_ge(d_evac, 128 * (SUPERS - 1) + 15 * 10 + 2 * t + 2)
                a = acc[0:rows_of(t), t, :]
                pool.tensor_tensor(a, a, rows[:, 0, :] if t < 4 else gs[0:ST, :],
                                   ALU.mult).then_inc(acc_gated, 1)

            def gain(t):
                pool.wait_ge(e_norm, t + 1)
                x = xt[0:rows_of(t), t, :]
                pool.tensor_tensor(x, x, rows[0:rows_of(t), 1, :], ALU.mult).then_inc(y_scaled, 1)

            pool.wait_ge(rows_loaded, 96 * SUPERS)
            pool.wait_ge(gs_loaded, 2 * 16 * NB)
            for t in range(3):
                gate_acc(t)
            gain(0)
            gate_acc(3)
            gain(1)
            gate_acc(4)
            for t in range(2, 5):
                gain(t)

        @block.scalar
        def _(act):
            act.wait_ge(s_cT, 1)
            act.activation(siluT[:, :], ps[:, 0, 0:KD * (1 + NB)], ACT.Silu).then_inc(s_silu, 1)

            def hi_part(s, n, slot=None, turn=None, free=True):
                slot = n % SLOTS if slot is None else slot
                turn = n // RAW if turn is None else turn
                act.wait_ge(raw_loaded[slot % RAW], (s * (N_SLABS // RAW) + turn + 1) * 16)
                if free:
                    act.wait_ge(slab_used, s * N_SLABS + n - SLOTS + 1)
                act.activation(W[:, slot, 0, :], raw[:, slot % RAW, :], ACT.Copy).then_inc(hi_done, 1)

            def x_affine(s, t, prologue=False):
                act.wait_ge(xt_tr, 4 * s + t + 1)
                for half in range(2):
                    if t:
                        act.wait_ge(x_split, 8 * s + 2 * t + half - 1)
                    elif not prologue:
                        act.wait_ge(hid_ready, 32 * s - 1 + half)
                    for q in range(4):
                        k = 4 * half + q
                        ins = act.activation(htmp[:, half, P * q:P * q + P],
                                             ps[:, 2 * (t % 2) + half, P * q:P * q + P], ACT.Identity,
                                             bias=modT[:, SH1 * KD + k, 0:1], scale=modT[:, SC1 * KD + k, 0:1])
                    ins.then_inc(x_tmp, 1)

            def relu2(s, f, i, n, nt, first=False):
                act.wait_ge(slab_used, s * N_SLABS + n + 1)
                if not first:
                    act.wait_ge(hid_ready, s * 32 + f - 1)
                h = as_fm(htmp[:, i, :], nt)
                act.activation(h, fm_view(2 * i, nt), ACT.Relu).then_inc(s_chain_act, 1)
                act.wait_ge(s_chain_act, s * 32 + f + 1)
                act.activation(h, h, ACT.Square).then_inc(relu_done, 1)

            def super_act(s, nt, first, last):
                def o_normal(t):
                    act.wait_ge(o_stats, 2 * s + (1 if t < 2 else 2))
                    act.activation(xt[:, t, :], xt[:, t, :], ACT.Identity, bias=ln_now[2][:, t:t + 1],
                                   scale=ln_now[1][:, t:t + 1]).then_inc(xn_act, 1)

                for n in range(SLAB_UP0 - 2):
                    hi_part(s, n + SLOTS)
                o_normal(0)
                o_normal(1)
                for n in range(SLAB_UP0 - 2, SLAB_UP0):
                    hi_part(s, n + SLOTS)
                o_normal(3)
                if first:
                    act.wait_ge(s_mod2, 1)
                for k in range(KD):
                    act.wait_ge(o_tr, 8 * s + k + 1)
                    if k >= 2:
                        act.wait_ge(o_split, 8 * s + k - 1)
                    act.activation(htmp[:, k % 2, 0:GT], ps[:, 4 + 2 * (k % 2), :], ACT.Identity,
                                   bias=bias2[:, k, 0:1], scale=scale2[:, k, 0:1]).then_inc(o_tmp, 1)
                for i in range(2):
                    relu2(s, i, i, SLAB_UP0 + i, nt, first=True)
                    hi_part(s, SLAB_UP0 + SLOTS + i)
                for i in range(2):
                    relu2(s, 2 + i, i, SLAB_UP0 + 2 + i, nt)
                    hi_part(s, SLAB_UP0 + 2 + SLOTS + i)
                for i in range(2):
                    hi_part(s, SLAB_UP0 + 4 + SLOTS + i)

                def ups(g):
                    for i in range(2):
                        n = SLAB_UP0 + 2 + 4 * g + i
                        relu2(s, 2 * g + 2 + i, i, n, nt)
                        hi_part(s, n + SLOTS, slot=2 + i, turn=(SLAB_UP0 + 2 + SLOTS) // RAW + 2 * g)

                with act.Fori(1, 14) as g:
                    ups(g)
                    for i in range(2):
                        hi_part(s, SLAB_UP0 + 4 + 4 * g + i + SLOTS, slot=i,
                                turn=(SLAB_UP0 + 4 + SLOTS) // RAW + 2 * g)
                ups(14)
                if not last:
                    for half in range(2):
                        for t in (2 * half, 2 * half + 1):
                            x_affine(s + 1, t)
                        for i in range(2):
                            hi_part(s, N_SLABS + 2 * half + i)

            for n in range(2):
                hi_part(0, n, free=False)
            act.wait_ge(s_mod1, 1)
            act.wait_ge(xs_split, 1)
            for t in range(4):
                x_affine(0, t, prologue=True)
                if t < 2:
                    hi_part(0, 2 + t, free=False)
            super_act(0, 4, True, False)
            with act.Fori(1, SUPERS - 1) as s:
                super_act(s, 4, False, False)
            super_act(SUPERS - 1, 5, False, True)
            for t in range(5):
                act.wait_ge(e_stats, t // 2 + 1)
                r = rows_of(t)
                act.activation(xt[0:r, t, :], xt[0:r, t, :], ACT.Identity, bias=ln_end[2][0:r, t:t + 1],
                               scale=ln_end[1][0:r, t:t + 1]).then_inc(e_norm, 1)

        @block.tensor
        def _(pe):
            def mm3(out, w_hi, w_lo, x_hi, x_lo, start, stop):
                pe.matmul(out, w_hi, x_hi, start=start, stop=False)
                pe.matmul(out, w_hi, x_lo, start=False, stop=False)
                return pe.matmul(out, w_lo, x_hi, start=False, stop=stop)

            def ada_product(u):
                pe.wait_ge(ada_in[u % 4], 32 * (u // 4 + 1))
                if u >= 2:
                    pe.wait_ge(ada_T, u - 1)
                buf = ada_buffer(u)
                for k in range(KD):
                    ins = pe.matmul(ps[0:1 + NB, 1 + 2 * (u % 2), 0:ADA_COLS],
                                    siluT[:, (1 + NB) * k:(1 + NB) * (k + 1)], buf[:, k, :],
                                    start=(k == 0), stop=(k == KD - 1))
                ins.then_inc(ada_mm, 1)

            def ada_turn(u):
                pe.wait_ge(ada_row, u + 1)
                for q in range(2):
                    ins = pe.transpose(ps[:, 1 + 2 * (u % 2), (1 + NB) * q:(1 + NB) * (q + 1)],
                                       ada_bias(u)[:, P * q:P * q + P], ident[0:1 + NB, 0:1 + NB])
                ins.then_inc(ada_tr, 1)

            def x_transposes(src, t, s):
                for k in range(KD):
                    ins = pe.transpose(ps[:, 2 * (t % 2) + k // 4, P * (k % 4):P * (k % 4) + P],
                                       src[:, P * k:P * k + P], ident[:, :])
                ins.then_inc(xt_tr, 1)

            pe.wait_ge(s_c, 32)
            pe.wait_ge(s_ident, 1)
            for k in range(KD):
                ins = pe.transpose(ps[:, 0, (1 + NB) * k:(1 + NB) * (k + 1)],
                                   rows[0:1 + NB, 2, P * k:P * k + P], ident[0:1 + NB, 0:1 + NB])
            ins.then_inc(s_cT, 1)
            pe.wait_ge(s_silu, 1)
            ada_product(0)
            for u in range(1, 4):
                ada_product(u)
                ada_turn(u - 1)
            pe.wait_ge(s_pre, 16 * N_PRE)
            for c in range(2):
                pe.transpose(ps[:, 5, 16 * c:16 * c + 16], htmp[0:16, 0, P * c:P * c + P], ident[0:16, 0:16])
            for c in range(2):
                pe.transpose(ps[:, 5, 128 + 120 * c:128 + 120 * c + 120],
                             htmp[0:120, 1, P * c:P * c + P], ident[0:120, 0:120])
            for h in range(HEADS):
                ins = pe.transpose(ps[:, 6 + h // 4, P * (h % 4):P * (h % 4) + P],
                                   rows[:, 0, P * h:P * h + P], ident[:, :])
            ins.then_inc(s_prepe, 1)
            for u in range(4, ADA_FIRST):
                ada_product(u)
                ada_turn(u - 1)
            ada_turn(ADA_FIRST - 1)
            pe.wait_ge(s_pret, 1)
            for k in range(KD):
                ins = pe.transpose(ps[:, 4 + k // 4, P * (k % 4):P * (k % 4) + ST],
                                   xt[0:ST, 4, P * k:P * k + P], ident[0:ST, 0:ST])
            ins.then_inc(xs_tr, 1)
            pe.wait_ge(x0_loaded, 64)
            pe.wait_ge(ada_T, ADA_FIRST)
            for t in range(4):
                if t >= 2:
                    pe.wait_ge(x_tmp, 2 * t - 2)
                x_transposes(x0_tile[t], t, 0)

            def fm_product(s, n, slot, bank, nt):
                pe.wait_ge(lo_done, s * N_SLABS + n + 1)
                w = W[:, slot, :, :].rearrange("p l (k n) -> p l k n", k=KD)
                for c, (a, b) in enumerate(chunks(nt)):
                    for k in range(KD):
                        ins = mm3(ps[:, bank + c, 0:b - a], w[:, 0, k, :], w[:, 1, k, :],
                                  hT[:, 0, k, a:b], hT[:, 1, k, a:b], k == 0, k == KD - 1)
                ins.then_inc(slab_used, 1)

            def sgu_half(s, nt, t, pos, half):
                r = rows_of(t)
                w = wsT if t < 4 else wsS
                n = 2 * r
                for q in range(2):
                    pair = 2 * half + q
                    v = rs[0:r, pos % 2, :, P * pair:P * pair + P]
                    ins = mm3(ps[:, sgu_bank(nt, t, half), n * q:n * q + n], v[:, 0, :], v[:, 1, :],
                              w[0:r, 0, 2 * pair:2 * pair + 2, :], w[0:r, 1, 2 * pair:2 * pair + 2, :],
                              True, True)
                ins.then_inc(sgu_done, 1)

            def super_pe(s, nt, first, last):
                for n in range(4):
                    pe.wait_ge(lo_done, s * N_SLABS + n + 1)
                    order = v_order(nt) if n else range(nt)
                    for pos, t in enumerate(order):
                        r = rows_of(t)
                        if n == 0:
                            pe.wait_ge(x_split, 8 * s + 2 * min(t, 3) + 2)
                        if n == 0 and not first:
                            pe.wait_ge(d_evac, 128 * s - 3 + min(t, 3))
                        for kk in range(2):
                            k = 2 * n + kk
                            ins = mm3(ps[0:r, V_BANK[t], :], hT[:, 0, k, tokens(t)], hT[:, 1, k, tokens(t)],
                                      W[:, n, 0, 512 * kk:512 * kk + 512], W[:, n, 1, 512 * kk:512 * kk + 512],
                                      k == 0, k == KD - 1)
                        if n == 3 and pos < nt - 1:
                            ins.then_inc(v_done, 1)
                    ins.then_inc(slab_used, 1)
                halves = 0
                for stage in mixer_stages(nt, first, False):
                    if stage[0] == "F":
                        f = stage[1]
                        turns = fm_turns(nt, first)
                        if f >= turns:
                            pe.wait_ge(fm_evac, s * N_FM + f - turns + 1)
                        if f == 1 and nt == 5:
                            pe.wait_ge(sgu_evac, 8 * s + 3)
                        fm_product(s, SLAB_FM + f, f % SLOTS, fm_bank(f, nt, first), nt)
                    elif stage[0] == "S":
                        tiles, pos = stage[1], stage[2]
                        for half in range(2):
                            for i, t in enumerate(tiles):
                                if half == 0:
                                    pe.wait_ge(v_norm, 4 * s + pos + i + 1)
                                elif sgu_bank(nt, t, 1) == V_BANK[t]:
                                    pe.wait_ge(sgu_evac, 8 * s + halves + i + 1)
                                else:
                                    pe.wait_ge(sgu_evac, 8 * s + halves)
                                sgu_half(s, nt, t, pos + i, half)
                        halves += 2 * len(tiles)
                    elif stage[0] == "A":
                        ada_product(stage[1])
                        if stage[1] > ADA_FIRST:
                            ada_turn(stage[1] - 1)
                    elif stage[0] == "E":
                        ada_turn(stage[1])
                    else:
                        c = stage[1]
                        pe.wait_ge(d_ready, 2 * s + c + 1)
                        for q, (a, b) in enumerate(chunks(nt)):
                            ins = mm3(ps[:, 4 + 2 * c + q, 0:b - a], pwT[:, 0, c, :], pwT[:, 1, c, :],
                                      rs[:, c, 0, a:b], rs[:, c, 1, a:b], True, True)
                        ins.then_inc(pm_done, 1)
                def o_product(h, q, t):
                    r = rows_of(t)
                    for kk, k in enumerate(O_PAIRS[q]):
                        ins = mm3(ps[0:r, o_bank(h, t), :],
                                  MH[:, 0, k, tokens(t)], MH[:, 1, k, tokens(t)],
                                  W[:, q, 0, 512 * kk:512 * kk + 512],
                                  W[:, q, 1, 512 * kk:512 * kk + 512],
                                  q == 0 and kk == 0, q == 3 and kk == 1)
                    return ins

                for h in range(2):
                    for q in range(4):
                        n = SLAB_O + 4 * h + q
                        pe.wait_ge(lo_done, s * N_SLABS + n + 1)
                        if h == 0:
                            pe.wait_ge(mix_ready, 8 * s + (8 if q == 3 else 7))
                        elif q == 0:
                            pe.wait_ge(o_evac, 8 * s + 2)
                            if first:
                                pe.wait_ge(ada_T, N_ADA)
                        if h == 1 and q == 2:
                            continue
                        for t in range(nt):
                            if h == 0 and q == 0 and t == 4:
                                pe.wait_ge(mix_ready, 8 * s + 7)
                            if h == 1 and q == 3:
                                ins = o_product(h, 2, t)
                                if t == nt - 1:
                                    ins.then_inc(slab_used, 1)
                            ins = o_product(h, q, t)
                            if q == 3 and t < nt - 1:
                                ins.then_inc(o_done, 1)
                        ins.then_inc(slab_used, 1)

                def o_transpose(k, t):
                    r, bank = rows_of(t), 4 + 2 * (k % 2)
                    dst = ps[:, bank, P * t:P * t + P] if t < 4 else ps[:, bank + 1, 0:ST]
                    return pe.transpose(dst, xt[0:r, t, P * k:P * k + P], ident[0:r, 0:r])

                def o_transposes(k):
                    pe.wait_ge(o_tmp, 8 * s + k - 1)
                    if nt == 5:
                        pe.wait_ge(o_split, 8 * s + k - 1)
                    for t in range(nt):
                        ins = o_transpose(k, t)
                    ins.then_inc(o_tr, 1)

                for t in range(nt):
                    if t in XN_ACT:
                        pe.wait_ge(xn_act, 3 * s + XN_ACT.index(t) + 1)
                    else:
                        pe.wait_ge(xn_dve, s + 1 + (t == 4))
                    if t == 0:
                        pe.wait_ge(o_evac, 8 * s + 2 * nt)
                    for k in range(2):
                        ins = o_transpose(k, t)
                        if t == nt - 1:
                            ins.then_inc(o_tr, 1)
                w = W[:, 0:2, :, :].rearrange("p s l (k n) -> p s l k n", k=KD)
                for k in range(KD):
                    pe.wait_ge(o_split, 8 * s + k + 1)
                    for i in range(2):
                        if k == 0:
                            pe.wait_ge(lo_done, s * N_SLABS + SLAB_UP0 + i + 1)
                        for c, (a, b) in enumerate(chunks(nt)):
                            ins = mm3(ps[:, 2 * i + c, 0:b - a], w[:, i, 0, k, :], w[:, i, 1, k, :],
                                      hT[:, 0, k, a:b], hT[:, 1, k, a:b], k == 0, k == KD - 1)
                        if k == KD - 1:
                            ins.then_inc(slab_used, 1)
                    if k + 2 < KD:
                        o_transposes(k + 2)

                def up(g, slab0, slot0):
                    for i in range(2):
                        pe.wait_ge(relu_done, s * 32 + 2 * g + i - 1)
                        fm_product(s, slab0 + i, slot0 + i, 2 * i, nt)

                def down(g, parity, slab0, slot0, after=None):
                    pe.wait_ge(lo_done, s * N_SLABS + slab0 + 2)
                    pe.wait_ge(hid_ready, s * 32 + 2 * g + 2)
                    for t in range(nt):
                        r = rows_of(t)
                        for h in range(2):
                            j = 2 * t + h
                            if j >= 4 or not (isinstance(g, int) and g == 0):
                                pe.wait_ge(d_evac, s * 128 + g * (2 * nt) + j - 3)
                            end = j == 2 * nt - 1
                            for kk in range(2):
                                ins = mm3(ps[0:r, down_bank(nt, parity, j), :],
                                          MH[:, 0, 2 * parity + kk, tokens(t)],
                                          MH[:, 1, 2 * parity + kk, tokens(t)],
                                          W[:, slot0 + kk, 0, HALF * h:HALF * h + HALF],
                                          W[:, slot0 + kk, 1, HALF * h:HALF * h + HALF],
                                          kk == 0, kk == 1)
                                if end:
                                    ins.then_inc(slab_used, 1)
                            if not end:
                                ins.then_inc(d_done, 1)
                        if after:
                            after(t)

                def next_x(t):
                    pe.wait_ge(gs_x, 64 * s + 16 * t + 16)
                    if t < 2:
                        pe.wait_ge(relu_done, 32 * s + 31 + t)
                    else:
                        pe.wait_ge(x_tmp, 8 * (s + 1) + 2 * t - 2)
                    x_transposes(gs, t, s + 1)

                up(1, SLAB_UP0 + 2, 2)
                if last:
                    pe.wait_ge(o_tmp, 8 * s + 8)
                    for c in range(2):
                        for q, a in enumerate((zlast[:, c, 0:CONV_BUF], zlast[:, c, CONV_BUF:],
                                               plast[:, c, 0:POOL_BUF], plast[:, c, POOL_BUF:])):
                            ins = pe.transpose(ps[0:a.shape[1], 6 + c, P * q:P * q + P], a, ident[:, :])
                    ins.then_inc(st_tr, 1)
                down(0, 0, SLAB_UP0 + 4, 0,
                     after=(lambda t: pe.wait_ge(st_rows, 8) if t == 0 else None) if last else None)
                with pe.Fori(0, 6) as j:
                    for par in (1, 0):
                        g = 2 * j + (1 if par else 2)
                        up(g + 1, SLAB_UP0 + 2 + 4 * g, 2)
                        down(g, par, SLAB_UP0 + 4 + 4 * g, 0)
                up(14, SLAB_UP0 + 2 + 4 * 13, 2)
                down(13, 1, SLAB_UP0 + 4 + 4 * 13, 0)
                up(15, SLAB_UP0 + 2 + 4 * 14, 2)
                down(14, 0, SLAB_UP0 + 4 + 4 * 14, 0,
                     after=None if last else lambda t: None if t % 2 else next_x(t // 2))
                down(15, 1, 86, 2,
                     after=None if last else lambda t: None if t % 2 else next_x(2 + t // 2))

            super_pe(0, 4, True, False)
            with pe.Fori(1, SUPERS - 1) as s:
                super_pe(s, 4, False, False)
            super_pe(SUPERS - 1, 5, False, True)

        @block.vector
        def _(dve):
            base, local = [0], [0]

            def step(ins):
                ins.then_inc(s_chain, 1)
                local[0] += 1

            def sync():
                dve.wait_ge(s_chain, base[0] + local[0])

            def do(ins):
                step(ins)
                sync()

            def signal(ins, sem_, value):
                ins.then_inc(sem_, 1)
                dve.wait_ge(sem_, value)

            def ada_add(u):
                dve.wait_ge(ada_mm, u + 1)
                dve.tensor_tensor(ada_bias(u), ps[0:1 + NB, 1 + 2 * (u % 2), 0:ADA_COLS], ada_bias(u),
                                  ALU.add).then_inc(ada_row, 1)

            def ada_turned(u):
                dve.wait_ge(ada_tr, u + 1)
                dve.tensor_copy(modT[:, 2 * u:2 * u + 2, :],
                                ps[:, 1 + 2 * (u % 2), 0:2 * (1 + NB)].rearrange("p (q n) -> p q n", q=2)
                                ).then_inc(ada_T, 1)

            def second_modulation():
                dve.wait_ge(ada_T, N_ADA)
                sh2, sc2 = (modT[:, q * KD:q * KD + KD, :] for q in (SH2, SC2))
                lng, lnb = (lnT[:, i, :].unsqueeze(2).to_broadcast([P, KD, 1 + NB]) for i in range(2))
                do(dve.tensor_scalar(sc2, sc2, 1.0, None, ALU.add))
                do(dve.tensor_tensor(scale2[:, :, :], sc2, lng, ALU.mult))
                do(dve.tensor_tensor(bias2[:, :, :], sc2, lnb, ALU.mult))
                signal(dve.tensor_tensor(bias2[:, :, :], bias2[:, :, :], sh2, ALU.add), s_mod2, 1)

            def rsqrt(a, b, ln):
                mv, rstd, rtmp = ln
                var, y, u = mv[:, a:b, 1], rstd[:, a:b], rtmp[:, a:b]
                do(dve.tensor_scalar(var, var, EPS, None, ALU.add))
                do(dve.tensor_scalar(y.bitcast(I32), var.bitcast(I32), 1, None, ALU.logical_shift_right))
                do(dve.tensor_scalar(y.bitcast(I32), y.bitcast(I32), -1.0, RSQRT_MAGIC, ALU.mult, ALU.add))
                for _ in range(3):
                    do(dve.tensor_tensor(u, y, y, ALU.mult))
                    do(dve.scalar_tensor_tensor(u, u, -0.5, var, ALU.mult, ALU.mult))
                    do(dve.scalar_tensor_tensor(y, u, 1.5, y, ALU.add, ALU.mult))

            def sums(t, i, x):
                step(dve.bn_stats(st[0:rows_of(t), t, i, :], x))

            def mean_var(t, n, ln):
                r = rows_of(t)
                sync()
                dve.sem_inc(s_fence, 1)
                step(dve.bn_aggr(ln[0][0:r, t, :], st[0:r, t, 0:n, :].rearrange("p a b -> p (a b)")))

            def normalise(out, x, t, ln):
                r = rows_of(t)
                return dve.tensor_scalar(out, x, ln[0][0:r, t, 0:1], ln[1][0:r, t:t + 1],
                                         ALU.subtract, ALU.mult)

            def scale_bias(a, b, ln, sem_, value):
                sync()
                rsqrt(a, b, ln)
                signal(dve.scalar_tensor_tensor(ln[2][:, a:b], ln[0][:, a:b, 0], -1.0, ln[1][:, a:b],
                                                ALU.mult, ALU.mult), sem_, value)

            def split(hi, lo, x):
                do(dve.tensor_copy(hi, x))
                return dve.tensor_tensor(lo, x, hi, ALU.subtract)

            def modulate_sample(o, src, mul, add):
                do(dve.tensor_tensor(o, src, mul, ALU.mult))
                do(dve.tensor_tensor(o, o, add, ALU.add))

            def x_sample():
                dve.wait_ge(xs_tr, 1)
                x = htmp[:, 0, 0:KD * ST].rearrange("p (k b t) -> p k b t", k=KD, b=NB)
                for half in range(2):
                    ks = slice(4 * half, 4 * half + 4)
                    src = ps[:, 4 + half, :].rearrange("p (k n) -> p k n", k=4)[:, :, 0:ST]
                    mul, add = (modT[:, q * KD + 4 * half:q * KD + 4 * half + 4, 1:].unsqueeze(3)
                                .to_broadcast([P, 4, NB, DT]) for q in (SC1, SH1))
                    modulate_sample(x[:, ks], src.rearrange("p k (b t) -> p k b t", b=NB), mul, add)
                x = htmp[:, 0, 0:KD * ST].rearrange("p (k n) -> p k n", k=KD)
                signal(split(hT[:, 0, :, GT:GT + ST], hT[:, 1, :, GT:GT + ST], x), xs_split, 1)

            def x_tile(s, t):
                for half in range(2):
                    n = 8 * s + 2 * t + half + 1
                    dve.wait_ge(x_tmp, n)
                    ks = slice(4 * half, 4 * half + 4)
                    x = htmp[:, half, 0:4 * P].rearrange("p (k n) -> p k n", k=4)
                    signal(split(hT[:, 0, ks, tokens(t)], hT[:, 1, ks, tokens(t)], x), x_split, n)

            def o_feature(s, nt, k):
                i, n = k % 2, GT + (ST if nt == 5 else 0)
                if nt == 5:
                    dve.wait_ge(o_tr, 8 * s + k + 1)
                    mul, add = (m[:, k, 1:].unsqueeze(2).to_broadcast([P, NB, DT]) for m in (scale2, bias2))
                    modulate_sample(htmp[:, i, GT:n].rearrange("p (b t) -> p b t", b=NB),
                                    ps[:, 5 + 2 * i, 0:ST].rearrange("p (b t) -> p b t", b=NB), mul, add)
                dve.wait_ge(o_tmp, 8 * s + k + 1)
                signal(split(hT[:, 0, k, 0:n], hT[:, 1, k, 0:n], htmp[:, i, 0:n]), o_split, 8 * s + k + 1)

            def v_tile(s, nt, t, pos):
                r = rows_of(t)
                x = htmp[0:r, 1, 0:W_GMLP] if t < 4 else gs[0:r, 0:W_GMLP]
                do(normalise(x, ps[0:r, V_BANK[t], :], t, ln_now))
                do(dve.tensor_tensor(x, x, sgu_gb[0:r, 0, :], ALU.mult))
                do(dve.tensor_tensor(x, x, sgu_gb[0:r, 1, :], ALU.add))
                signal(split(rs[0:r, pos % 2, 0, 0:W_GMLP], rs[0:r, pos % 2, 1, 0:W_GMLP], x),
                       v_norm, 4 * s + pos + 1)

            def sgu_half(s, nt, t, half, count):
                dve.wait_ge(sgu_done, 8 * s + count)
                r = rows_of(t)
                pr = slice(2 * half, 2 * half + 2)
                for odd in range(2):
                    q = slice(64 * odd, 64 * odd + 64)
                    src = ps[q, sgu_bank(nt, t, half), 0:4 * r].rearrange("p (a h i) -> p a h i", a=2, h=2)[:, :, odd, :]
                    dst = sg[q, pr, tokens(t)]
                    bias = bsR[q, pr, 0:r]
                    if t == 4:
                        src = src.rearrange("p a (b i) -> p a b i", b=NB)
                        dst = dst.rearrange("p a (b i) -> p a b i", b=NB)
                        bias = bsR[q, pr, 0:DT].unsqueeze(2).to_broadcast([64, 2, NB, DT])
                    if odd:
                        dve.tensor_tensor(dst, src, bias, ALU.add).then_inc(sgu_evac, 1)
                    else:
                        step(dve.tensor_tensor(dst, src, bias, ALU.add))

            def copy_pieces(s, f, nt, bank, prompt, sample, other=None):
                ps_ = pieces(bank, nt)
                for n, (src, a) in enumerate(ps_):
                    w = src.shape[1]
                    if a is not None:
                        dst = prompt[:, a:a + w]
                        o = None if other is None else other[:, a:a + w]
                    else:
                        src = src.rearrange("p (b i) -> p b i", b=NB)
                        dst = sample
                        o = None if other is None else other[:, GT:GT + ST].rearrange("p (b i) -> p b i", b=NB)
                    ins = dve.tensor_copy(dst, src) if o is None else dve.tensor_tensor(dst, src, o, ALU.mult)
                    if n == len(ps_) - 1:
                        ins.then_inc(fm_evac, 1)
                    else:
                        step(ins)

            mix_order = [0, 1, 2, 3, 6, 4, 7, 5]

            def mix_out(s, nt, k, x):
                n = GT + (ST if nt == 5 else 0)
                signal(split(MH[:, 0, k, 0:n], MH[:, 1, k, 0:n], x),
                       mix_ready, 8 * s + mix_order.index(k) + 1)

            def wait_fm(s, f):
                dve.wait_ge(slab_used, s * N_SLABS + SLAB_FM + f + 1)

            def conv_fm(s, nt, f, bank):
                c, what = f // 3, f % 3
                wait_fm(s, f)
                if what == 0:
                    dve.tensor_copy(as_fm(htmp[:, 0, :], nt), fm_view(bank, nt)).then_inc(fm_evac, 1)
                    dve.wait_ge(fm_evac, s * N_FM + f + 1)
                elif what == 1:
                    do(dve.tensor_copy(zp_[:, 0:CONV_BUF], zcarry[:, c, :]))
                    if nt == 5:
                        do(dve.tensor_copy(zs_[:, :, 0:CONV_BUF],
                                           zstate[:, c, :].rearrange("p (b n) -> p b n", b=NB)))
                    copy_pieces(s, f, nt, bank, zp_[:, CONV_BUF:], zs_[:, :, CONV_BUF:], htmp[:, 0, :])
                    sync()
                    dve.wait_ge(fm_evac, s * N_FM + f + 1)
                    seqs = [(bufA[:, 0:GT], lambda a: zp_[:, a:a + GT])]
                    if nt == 5:
                        seqs.append((bufA[:, GT:GT + ST].rearrange("p (b i) -> p b i", b=NB),
                                     lambda a: zs_[:, :, a:a + DT]))
                    for o, z in seqs:
                        do(dve.tensor_scalar(o, z(0), convw[:, c, 0:1], None, ALU.mult))
                        for a in (1, 2):
                            do(dve.scalar_tensor_tensor(o, z(a), convw[:, c, a:a + 1], o, ALU.mult, ALU.add))
                    step(dve.tensor_copy(zcarry[:, c, :], zp_[:, GT:GT + CONV_BUF]))
                    if nt == 5:
                        step(dve.tensor_copy(zlast[:, c, 0:CONV_BUF], zp_[:, GT:GT + CONV_BUF]))
                        step(dve.tensor_copy(
                            zlast[:, c, CONV_BUF:].rearrange("p (b n) -> p b n", b=NB), zs_[:, :, DT:]))
                    sync()
                else:
                    dve.tensor_tensor(as_fm(bufB, nt), fm_view(bank, nt), as_fm(bufA, nt),
                                      ALU.mult).then_inc(fm_evac, 1)
                    dve.wait_ge(fm_evac, s * N_FM + f + 1)
                    mix_out(s, nt, c, bufB[:, 0:GT + (ST if nt == 5 else 0)])

            def pool_fm(s, nt, f, bank):
                c = f - 6
                wait_fm(s, f)
                do(dve.tensor_copy(pp_[:, 0:POOL_BUF], pcarry[:, c, :]))
                if nt == 5:
                    do(dve.tensor_copy(psm[:, :, 0:POOL_BUF],
                                       pstate[:, c, :].rearrange("p (b n) -> p b n", b=NB)))
                copy_pieces(s, f, nt, bank, pp_[:, POOL_BUF:], psm[:, :, POOL_BUF:])
                sync()
                dve.wait_ge(fm_evac, s * N_FM + f + 1)
                seqs = [(pp_, lambda b, lo, hi: b[:, lo:hi], GT, htmp[:, 0, 0:GT], lambda b: b)]
                if nt == 5:
                    seqs.append((psm, lambda b, lo, hi: b[:, :, lo:hi], DT,
                                 htmp[:, 0, GT:GT + ST].rearrange("p (b i) -> p b i", b=NB),
                                 lambda b: b[:, 0:NB * (POOL_BUF + DT)].rearrange("p (b n) -> p b n", b=NB)))
                for z, cut, n, d, shape in seqs:
                    L = POOL_BUF + n
                    A, B = shape(bufA), shape(bufB)
                    do(dve.tensor_tensor(cut(A, 1, L), cut(z, 1, L), cut(z, 0, L - 1), ALU.add))
                    do(dve.tensor_tensor(cut(B, 3, L), cut(A, 3, L), cut(A, 1, L - 2), ALU.add))
                    if c == 1:
                        do(dve.tensor_tensor(cut(A, 7, L), cut(B, 7, L), cut(B, 3, L - 4), ALU.add))
                        do(dve.tensor_tensor(cut(B, 15, L), cut(A, 15, L), cut(A, 7, L - 8), ALU.add))
                    for q, S in ((slice(0, 64), A), (slice(64, P), B)):
                        step(dve.scalar_tensor_tensor(d[q], cut(S, POOL_BUF, L)[q], invw[q, c:c + 1],
                                                      cut(z, POOL_BUF, L)[q], ALU.mult, ALU.subtract))
                    sync()
                    if n == GT:
                        for q, S in ((slice(0, 64), A), (slice(64, P), B)):
                            step(dve.tensor_tensor(d[q, 0:16], S[q, POOL_BUF:POOL_BUF + 16],
                                                   invtab[q, c, :], ALU.mult))
                        sync()
                        do(dve.tensor_tensor(d[:, 0:16], d[:, 0:16], z[:, POOL_BUF:POOL_BUF + 16],
                                             ALU.subtract))
                do(dve.tensor_scalar(invtab[:, c, :], invtab[:, c, :], 0.0, invw[:, c:c + 1],
                                     ALU.mult, ALU.add))
                step(dve.tensor_copy(pcarry[:, c, :], pp_[:, GT:GT + POOL_BUF]))
                if nt == 5:
                    step(dve.tensor_copy(plast[:, c, 0:POOL_BUF], pp_[:, GT:GT + POOL_BUF]))
                    step(dve.tensor_copy(
                        plast[:, c, POOL_BUF:].rearrange("p (b n) -> p b n", b=NB), psm[:, :, DT:]))
                sync()
                n = GT + (ST if nt == 5 else 0)
                signal(split(rs[:, c, 0, 0:n], rs[:, c, 1, 0:n], htmp[:, 0, 0:n]), d_ready, 2 * s + c + 1)

            def pool_out(s, nt, c):
                dve.wait_ge(pm_done, 2 * s + c + 1)
                pv = fm_view(4 + 2 * c, nt)
                k = 6 + c
                do(dve.tensor_scalar(as_fm(bufA, nt), pv, pscale[:, c:c + 1], None, ALU.mult))
                mix_out(s, nt, k, bufA[:, 0:GT + (ST if nt == 5 else 0)])

            def u_fm(s, nt, f, bank):
                c = f - 8
                wait_fm(s, f)
                dve.tensor_tensor(as_fm(bufB, nt), fm_view(bank, nt), as_fm(sg[:, c, :], nt),
                                  ALU.mult).then_inc(fm_evac, 1)
                dve.wait_ge(fm_evac, s * N_FM + f + 1)
                mix_out(s, nt, 2 + c, bufB[:, 0:GT + (ST if nt == 5 else 0)])

            def gate_rows(t):
                return rows[:, 0, :] if t < 4 else gs[0:ST, :]

            def end_residual(t):
                r = rows_of(t)
                a, x = acc[0:r, t, :], xt[0:r, t, :]
                do(dve.tensor_tensor(a, a, gate_rows(t)[0:r, :], ALU.mult))
                do(dve.scalar_tensor_tensor(x, x, ALPHA, a, ALU.mult, ALU.add))
                for i in range(2):
                    sums(t, i, xt[0:r, t, HALF * i:HALF * i + HALF])
                mean_var(t, 2, ln_end)

            def end_sums(t):
                r = rows_of(t)
                x = xt[0:r, t, :]
                dve.wait_ge(acc_gated, t + 1)
                do(dve.scalar_tensor_tensor(x, x, ALPHA, acc[0:r, t, :], ALU.mult, ALU.add))
                for i in range(2):
                    sums(t, i, xt[0:r, t, HALF * i:HALF * i + HALF])
                mean_var(t, 2, ln_end)

            def end_norm(s, t):
                r = rows_of(t)
                x = xt[0:r, t, :]
                do(normalise(x, x, t, ln_end))
                do(dve.tensor_tensor(x, x, rows[0:r, 1, :], ALU.mult))
                signal(dve.tensor_tensor(x, x, rows[0:r, 2, :], ALU.add), y_ready, 4 * s + t + 1)

            def super_dve(s, nt, first, last):
                todo = list(enumerate(v_order(nt)))

                def some_v(n):
                    for _ in range(n):
                        if todo:
                            pos, t = todo.pop(0)
                            v_tile(s, nt, t, pos)

                for pos, t in enumerate(v_order(nt)):
                    if pos < nt - 1:
                        dve.wait_ge(v_done, 3 * s + pos + 1)
                    else:
                        dve.wait_ge(slab_used, s * N_SLABS + 4)
                    sums(t, 0, ps[0:rows_of(t), V_BANK[t], :])
                    mean_var(t, 1, ln_now)
                    if t == 4:
                        sync()
                        rsqrt(4, 5, ln_now)
                        some_v(1)
                sync()
                rsqrt(0, 4, ln_now)
                some_v(1 if nt == 5 else 2)
                halves = 0
                for stage in mixer_stages(nt, first, True):
                    if stage[0] == "F":
                        f = stage[1]
                        (conv_fm if f < 6 else pool_fm if f < 8 else u_fm)(s, nt, f, fm_bank(f, nt, first))
                    elif stage[0] == "S":
                        for half in range(2):
                            for t in stage[1]:
                                halves += 1
                                sgu_half(s, nt, t, half, halves)
                        sync()
                        dve.wait_ge(sgu_evac, 8 * s + halves)
                    elif stage[0] == "V":
                        some_v(2)
                    elif stage[0] == "N":
                        end_norm(s - 1, stage[1])
                    elif stage[0] == "A":
                        ada_add(stage[1])
                        if stage[1] > ADA_FIRST:
                            ada_turned(stage[1] - 1)
                    elif stage[0] == "E":
                        ada_turned(stage[1])
                        second_modulation()
                    else:
                        pool_out(s, nt, stage[1])
                dve.wait_ge(rows_loaded, 96 * s + 48)
                for h in range(2):
                    cols = slice(HALF * h, HALF * h + HALF)
                    for t in range(nt):
                        if h == 0 and t == 4:
                            dve.wait_ge(gs_loaded, 16 * NB)
                        if h == 0 and t < 4:
                            dve.wait_ge(x_loaded[t], 16 * s + 16)
                        if t < nt - 1:
                            dve.wait_ge(o_done, 6 * s + (nt - 1) * h + t + 1)
                        else:
                            dve.wait_ge(slab_used, s * N_SLABS + SLAB_O + 4 * h + 4)
                        r = rows_of(t)
                        tmp = htmp[0:r, t % 2, 0:HALF]
                        signal(dve.tensor_tensor(tmp, ps[0:r, o_bank(h, t), :], gate_rows(t)[0:r, cols],
                                                 ALU.mult), o_evac, 8 * s + nt * h + t + 1)
                        x = xt[0:r, t, cols]
                        do(dve.scalar_tensor_tensor(x, x, ALPHA, tmp, ALU.mult, ALU.add))
                        sums(t, h, x)
                        if h == 1:
                            mean_var(t, 2, ln_now)
                            if t == 1:
                                scale_bias(0, 2, ln_now, o_stats, 2 * s + 1)
                scale_bias(2, nt, ln_now, o_stats, 2 * s + 2)
                for t in (2, 4)[:nt - 3]:
                    x = xt[0:rows_of(t), t, :]
                    signal(normalise(x, x, t, ln_now), xn_dve, s + 1 + (t == 4))
                for k in range(KD):
                    o_feature(s, nt, k)

                def hidden(f, i, parity):
                    dve.wait_ge(relu_done, s * 32 + f + 1)
                    n = GT + (ST if nt == 5 else 0)
                    hi, lo = (MH[:, p, 2 * parity + i, 0:n] for p in range(2))
                    x = htmp[:, i, 0:n]
                    signal(dve.tensor_copy(hi, x), s_hid_hi, s * 32 + f + 1)
                    signal(dve.tensor_tensor(lo, x, hi, ALU.subtract), hid_ready, s * 32 + f + 1)

                def first_x1(t):
                    r = rows_of(t)
                    x = xt[0:r, t, :]
                    do(dve.tensor_tensor(x, x, rows[0:r, 1, :], ALU.mult))
                    ins = dve.tensor_tensor(x, x, rows[0:r, 2, :], ALU.add)
                    if t == nt - 1:
                        signal(ins, x1_ready, s + 1)
                    else:
                        step(ins)

                def down(g, parity, start, last_slab, after=None):
                    for t in range(nt):
                        r = rows_of(t)
                        for h in range(2):
                            j = 2 * t + h
                            if j == 2 * nt - 1:
                                dve.wait_ge(slab_used, s * N_SLABS + last_slab + 1)
                            else:
                                dve.wait_ge(d_done, s * 112 + g * (2 * nt - 1) + j + 1)
                            a = acc[0:r, t, HALF * h:HALF * h + HALF]
                            src = ps[0:r, down_bank(nt, parity, j), :]
                            if start:
                                dve.tensor_copy(a, src).then_inc(d_evac, 1)
                            else:
                                dve.wait_ge(d_evac, s * 128 + (g - 1) * (2 * nt) + j + 1)
                                dve.tensor_tensor(a, a, src, ALU.add).then_inc(d_evac, 1)
                        if after:
                            after(t)

                for i in range(2):
                    hidden(i, i, 0)
                first_x1(0)
                if last:
                    dve.wait_ge(st_tr, 1)
                    for q, (_, n, _) in enumerate(STATES):
                        for c in range(2):
                            dve.tensor_copy(gs[0:n, 2 * P * q + P * c:2 * P * q + P * c + P],
                                            ps[0:n, 6 + c, P * q:P * q + P]).then_inc(st_rows, 1)
                for i in range(2):
                    hidden(2 + i, i, 1)
                down(0, 0, True, SLAB_UP0 + 5)
                for t in range(1, nt):
                    first_x1(t)
                dve.sem_inc(s_fence, 1)
                with dve.Fori(0, 6) as jj:
                    for par in (0, 1):
                        g = 2 * jj + 1 + par
                        for i in range(2):
                            hidden(2 * g + 2 + i, i, par)
                        down(g, 1 - par, False, SLAB_UP0 + 5 + 4 * g)
                for g in (13, 14):
                    for i in range(2):
                        hidden(2 * g + 2 + i, i, (g + 1) % 2)
                    if g == 14 and not last:
                        down(g, 0, False, SLAB_UP0 + 5 + 4 * g,
                             lambda t: x_tile(s + 1, t // 2) if t % 2 else None)
                    else:
                        down(g, g % 2, False, SLAB_UP0 + 5 + 4 * g)
                if not last:
                    down(15, 1, False, 87, lambda t: x_tile(s + 1, 2 + t // 2) if t % 2 else None)
                    dve.wait_ge(rows_loaded, 96 * s + 96)
                    dve.wait_ge(d_evac, s * 128 + 16 * 2 * nt)
                    for t in range(nt):
                        end_residual(t)
                    sync()
                    rsqrt(0, nt, ln_end)
                else:
                    def finish(t):
                        if t >= 1:
                            end_sums(t - 1)
                        if t in (2, 4):
                            scale_bias(t - 2, t, ln_end, e_stats, t // 2)
                        if t == 4:
                            end_sums(4)
                            scale_bias(4, 5, ln_end, e_stats, 3)

                    down(15, 1, False, 87, finish)
                    for t in range(nt):
                        dve.wait_ge(y_scaled, t + 1)
                        x = xt[0:rows_of(t), t, :]
                        signal(dve.tensor_tensor(x, x, rows[0:rows_of(t), 2, :], ALU.add),
                               y_ready, 4 * s + t + 1)

            ada_add(0)
            for u in range(1, 4):
                ada_add(u)
                ada_turned(u - 1)
            dve.wait_ge(s_prepe, 1)
            do(dve.tensor_copy(zstate[:, :, :], ps[:, 5, 0:32].rearrange("p (c n) -> p c n", c=2)))
            do(dve.tensor_copy(pstate[:, :, :], ps[:, 5, 128:368].rearrange("p (c n) -> p c n", c=2)))
            dve.wait_ge(s_prep, 1)
            dve.tensor_copy(raw[:, 1, :].rearrange("p (b n) -> p b n", b=2), ps[:, 6:8, :]).then_inc(s_pret, 1)
            for u in range(4, ADA_FIRST):
                ada_add(u)
                ada_turned(u - 1)
            ada_turned(ADA_FIRST - 1)
            dve.wait_ge(ada_T, ADA_FIRST)
            sc1 = modT[:, SC1 * KD:SC1 * KD + KD, :]
            signal(dve.tensor_scalar(sc1, sc1, 1.0, None, ALU.add), s_mod1, 1)
            x_sample()
            for t in range(4):
                x_tile(0, t)
            dve.wait_ge(s_prep, 2)
            super_dve(0, 4, True, False)
            before = local[0]
            with dve.Fori(1, SUPERS - 1) as s:
                base[0], local[0] = before + (s - 1) * DVE_STEPS, 0
                super_dve(s, 4, False, False)
                assert local[0] == DVE_STEPS, local[0]
            base[0], local[0] = before + (SUPERS - 2) * DVE_STEPS, 0
            super_dve(SUPERS - 1, 5, False, True)


_INS = ["x_prompt", "x_sample", "c_prompt", "c_sample", "state_conv", "state_pool", "w_ada", "b_ada",
        "w_in", "conv_w", "sgu_g", "sgu_b", "w_s", "b_s", "pool_w", "pool_scale", "w_out", "ln1_g",
        "ln1_b", "w_up", "w_down", "ln2_g", "ln2_b"]
_OUTS = [(1, SEQ, D), (NB, DT, D), (1, 1, CONV_BUF, W_CONV), (1, 1, POOL_BUF, W_POOL),
         (1, NB, CONV_BUF, W_CONV), (1, NB, POOL_BUF, W_POOL), (1, NB, DT, W_GMLP)]


def kernel(**inputs):
    import numpy as np
    import concourse.bacc as bacc
    from concourse.bass_utils import run_bass_kernel_spmd

    nc = bacc.Bacc("TRN2", target_bir_lowering=False, num_devices=1)
    arrays, args = {}, []
    for name in _INS:
        a = np.ascontiguousarray(inputs[name])
        arrays[f"in_{name}"] = a
        args.append(nc.dram_tensor(f"in_{name}", a.shape, mybir.dt.from_np(a.dtype), kind="ExternalInput").ap())
    for i, shape in enumerate(_OUTS):
        args.append(nc.dram_tensor(f"out_{i}", shape, F32, kind="ExternalOutput").ap())
    args.append(nc.dram_tensor("mod_rows", (1 + NB, 6 * D), F32).ap())
    decoder_layer_kernel(nc, *args)
    r = run_bass_kernel_spmd(nc, [arrays], core_ids=[0])
    return tuple(r.results[0][f"out_{i}"] for i in range(len(_OUTS)))
```

```python
from contextlib import ExitStack

import concourse.bass as bass
from concourse import mybir

F32 = mybir.dt.float32
F32R = mybir.dt.float32r
I32 = mybir.dt.int32
ACT = mybir.ActivationFunctionType
ALU = mybir.AluOpType

P = 128
D = 1024
KD = D // P
SEQ = 2048
GT = 512
SUPERS = SEQ // GT
NB, DT = 8, 8
ST = NB * DT
W_CONV, W_GMLP, W_POOL = 256, 512, 256
FF = 4 * D
HEADS = 8
HALF = D // 2
COL_B, COL_C, COL_X = 0, W_CONV, 2 * W_CONV
COL_U = 3 * W_CONV
COL_V = COL_U + W_GMLP
COL_P = COL_V + W_GMLP
CONV_BUF, POOL_BUF = 2, 15
WINDOWS = (2, 4, 8, 16)
ALPHA = 2.0 ** 0.25
EPS = 1e-5
RSQRT_MAGIC = float(0x5F3759DF)
SH1, SC1, G1, SH2, SC2, G2 = range(6)

SLOTS = 4
RAW = 2
N_SLABS = 88
SLAB_FM, SLAB_O, SLAB_UP0 = 4, 16, 24
N_FM = 12
MLP_GROUPS = 16
FM_PARTS = [("c", 0), ("x", 0), ("b", 0), ("pool", 0), ("u", 0), ("pool", 1), ("u", 1),
            ("c", 1), ("x", 1), ("b", 1), ("u", 2), ("u", 3)]
FM_COLS = [{"b": COL_B, "c": COL_C, "x": COL_X, "u": COL_U, "pool": COL_P}[part] + P * c
           for part, c in FM_PARTS]
O_PAIRS = [(0, 1), (2, 3), (6, 7), (4, 5)]
XN_ACT = (0, 1)
V_BANK = [4, 5, 6, 7, 3]
N_ADA = 24
ADA_COLS = 6 * D // N_ADA
ADA_FIRST = 2 * D // ADA_COLS


def ada_col(u):
    if u < ADA_FIRST:
        return (SH1 if u % 2 else SC1) * D + ADA_COLS * (u // 2)
    return ADA_COLS * u


N_PRE = 3 + 2 + 2 + 2 + 1 + 2 + 1
DVE_STEPS = 176


def bcast(ap, n):
    return ap.partition_broadcast(n)


def o_bank(h, t):
    return (4 + 5 * h + t) % 8


def decoder_layer_kernel(nc, x_prompt, x_sample, c_prompt, c_sample, state_conv, state_pool,
                         w_ada, b_ada, w_in, conv_w, sgu_g, sgu_b, w_s, b_s, pool_w, pool_scale,
                         w_out, ln1_g, ln1_b, w_up, w_down, ln2_g, ln2_b,
                         y_prompt, y_sample, o_conv_p, o_pool_p, o_conv_s, o_pool_s, o_v_s,
                         mod_rows):
    ctx = ExitStack()
    with ctx:
        ctx.enter_context(nc.allow_non_contiguous_dma(reason="small tables turned by the DMA, once"))

        def sb(name, shape, dt=F32):
            return ctx.enter_context(nc.sbuf_tensor(name, shape, dt))

        def sem(name):
            return ctx.enter_context(nc.semaphore(name))

        W = sb("w_hilo", [P, SLOTS, 2, D], F32R)
        raw = sb("w_raw", [P, RAW, D])
        hT = sb("hT", [P, 2, KD, GT + ST], F32R)
        MH = sb("mixT_hidden", [P, 2, KD, GT + ST], F32R)
        xt = sb("xt", [P, 5, D])
        acc = sb("acc", [P, 5, D])
        rs = sb("rs", [P, 2, 2, GT + ST], F32R)
        wsT = sb("wsT", [P, 2, HEADS, P], F32R)
        wsS = sb("wsS", [P, 2, HEADS, ST], F32R)
        bsR = sb("bsR", [P, 4, P])
        pwT = sb("pwT", [P, 2, 2, P], F32R)
        ident = sb("ident", [P, P])
        modT = sb("modT", [P, 6 * KD, 1 + NB])
        scale2 = sb("scale2", [P, KD, 1 + NB])
        bias2 = sb("bias2", [P, KD, 1 + NB])
        rows = sb("rows", [P, 3, D])
        gs = sb("gs", [P, D])
        sgu_gb = sb("sgu_gb", [P, 2, W_GMLP])
        htmp = sb("htmp", [P, 2, GT + ST])
        convw = sb("convw", [P, 2, 3])
        pscale = sb("pscale", [P, 2])
        invw = sb("invw", [P, 2])
        invtab = sb("invtab", [P, 2, 16])
        zcarry = sb("zcarry", [P, 2, CONV_BUF])
        pcarry = sb("pcarry", [P, 2, POOL_BUF])
        zstate = sb("zstate", [P, 2, NB * CONV_BUF])
        pstate = sb("pstate", [P, 2, NB * POOL_BUF])
        lnT = sb("lnT", [P, 2, KD])
        st = sb("st", [P, 5, 2, 6])
        siluT = sb("siluT", [P, KD * (1 + NB)])
        ln_now = (sb("mv", [P, 5, 2]), sb("rstd", [P, 5]), sb("rtmp", [P, 5]))
        ln_end = (sb("mv_end", [P, 5, 2]), sb("rstd_end", [P, 5]), sb("rtmp_end", [P, 5]))
        ps = ctx.enter_context(nc.psum_tensor("ps", [P, 8, 512], F32))

        flat = acc[:, :, :].rearrange("p t d -> p (t d)")
        off = [0]

        def scratch(n):
            off[0] += n
            assert off[0] <= 5 * D
            return flat[:, off[0] - n:off[0]]

        sg = scratch(4 * (GT + ST)).rearrange("p (c n) -> p c n", c=4)
        zp_ = scratch(CONV_BUF + GT)
        zs_ = scratch(NB * (CONV_BUF + DT)).rearrange("p (b n) -> p b n", b=NB)
        pp_ = scratch(POOL_BUF + GT)
        psm = scratch(NB * (POOL_BUF + DT)).rearrange("p (b n) -> p b n", b=NB)
        bufA = scratch(GT + ST)
        bufB = scratch(GT + ST)
        zlast = scratch(2 * (CONV_BUF + NB * CONV_BUF)).rearrange("p (c n) -> p c n", c=2)
        plast = scratch(2 * (POOL_BUF + NB * POOL_BUF)).rearrange("p (c n) -> p c n", c=2)

        STATES = [(o_conv_p[0, 0], CONV_BUF, 0), (o_conv_s[0].rearrange("b r c -> (b r) c"), NB * CONV_BUF, 1),
                  (o_pool_p[0, 0], POOL_BUF, 2), (o_pool_s[0].rearrange("b r c -> (b r) c"), NB * POOL_BUF, 3)]

        s_c = sem("s_c")
        s_pre = sem("s_pre")
        x0_loaded = sem("x0_loaded")
        ada_in = [sem(f"ada_in{i}") for i in range(4)]
        ada_mm = sem("ada_mm")
        ada_row = sem("ada_row")
        ada_tr = sem("ada_tr")
        ada_T = sem("ada_T")
        ada_out = [sem(f"ada_out{i}") for i in range(4)]
        x0_tr = sem("x0_tr")
        s_mod2 = sem("s_mod2")
        s_corner = sem("s_corner")
        s_fence = sem("s_fence")
        s_cT = sem("s_cT")
        s_ident = sem("s_ident")
        xs_split = sem("xs_split")
        s_silu = sem("s_silu")
        s_prepe = sem("s_prepe")
        s_prep = sem("s_prep")
        s_pool0 = sem("s_pool0")
        s_pret = sem("s_pret")
        s_chain = sem("s_chain")
        s_chain_act = sem("s_chain_act")
        raw_loaded = [sem(f"raw_loaded{i}") for i in range(RAW)]
        hi_done = sem("hi_done")
        lo_done = sem("lo_done")
        slab_used = sem("slab_used")
        x_loaded = [sem(f"x_loaded{t}") for t in range(5)]
        rows_loaded = sem("rows_loaded")
        gs_loaded = sem("gs_loaded")
        gs_x = sem("gs_x")
        xt_tr = sem("xt_tr")
        x_tmp = sem("x_tmp")
        x_split = sem("x_split")
        xs_tr = sem("xs_tr")
        o_tr = sem("o_tr")
        o_tmp = sem("o_tmp")
        o_split = sem("o_split")
        v_done = sem("v_done")
        v_stats = sem("v_stats")
        v_norm_act = sem("v_norm_act")
        v_norm = sem("v_norm")
        sgu_done = sem("sgu_done")
        sgu_evac = sem("sgu_evac")
        fm_evac = sem("fm_evac")
        d_ready = sem("d_ready")
        pm_done = sem("pm_done")
        mix_ready = sem("mix_ready")
        o_done = sem("o_done")
        o_evac = sem("o_evac")
        o_stats = sem("o_stats")
        xn_act = sem("xn_act")
        xn_dve = sem("xn_dve")
        x1_ready = sem("x1_ready")
        relu_done = sem("relu_done")
        hid_ready = sem("hid_ready")
        d_done = sem("d_done")
        d_evac = sem("d_evac")
        y_ready = sem("y_ready")
        e_stats = sem("e_stats")
        e_norm = sem("e_norm")
        acc_gated = sem("acc_gated")
        y_scaled = sem("y_scaled")
        y_stored = sem("y_stored")
        v_stored = sem("v_stored")
        s_hid_hi = sem("s_hid_hi")
        st_tr = sem("st_tr")
        st_rows = sem("st_rows")
        st_stored = sem("st_stored")

        w_in_v = w_in[0].rearrange("(k p) e -> p k e", p=P)
        w_out_v = w_out[0].rearrange("(k p) e -> p k e", p=P)
        w_up_v = w_up[0].rearrange("(k p) e -> p k e", p=P)
        w_down_v = w_down[0].rearrange("(f p) e -> p f e", p=P)
        w_ada_v = w_ada[0].rearrange("(k p) e -> p k e", p=P)

        def rows_of(t):
            return P if t < 4 else ST

        def tokens(t):
            return slice(P * t, P * t + rows_of(t))

        def chunks(nt):
            return [(0, GT)] if nt == 4 else [(0, (GT + ST) // 2), ((GT + ST) // 2, GT + ST)]

        def fm_bank(f, nt, first=False):
            if nt == 5 or first:
                return 2 * (f % 2)
            return f % 4

        def fm_turns(nt, first):
            return 2 if nt == 5 or first else 4

        def fm_view(bank, nt):
            n = GT if nt == 4 else (GT + ST) // 2
            return ps[:, bank:bank + len(chunks(nt)), 0:n]

        def as_fm(ap, nt):
            return ap[:, 0:GT + (ST if nt == 5 else 0)].rearrange("p (c n) -> p c n", c=len(chunks(nt)))

        def pieces(bank, nt):
            if nt == 4:
                return [(ps[:, bank, 0:GT], 0)]
            n = (GT + ST) // 2
            return [(ps[:, bank, 0:n], 0), (ps[:, bank + 1, 0:GT - n], n),
                    (ps[:, bank + 1, GT - n:n], None)]

        def v_order(nt):
            return [0, 1, 2, 3] if nt == 4 else [4, 0, 1, 2, 3]

        def mixer_stages(nt, first, vector):
            F = [("F", n) for n in range(N_FM)]
            S01, S23 = ("S", [0, 1], 0 if nt == 4 else 1), ("S", [2, 3], 2 if nt == 4 else 3)
            if nt == 5:
                S4 = ("S", [4], 0)
                a = [S4, ("V", 1), F[0], ("V", 1)] if vector else [F[0], S4]
                a += [F[1], F[2]] if not vector else [F[1]]
                a += [S01, ("V", 2)] + ([F[2]] if vector else []) + [S23, F[3], F[4], N(0)]
            elif vector or first:
                a = [F[0], F[1], S01, ("V", 2), F[2], S23, F[3], F[4]]
            else:
                a = F[0:4] + [S01, F[4], S23]
            a += [F[5], F[6], N(1), F[7], ("M", 0), N(2), F[8], ("M", 1), N(3)] + F[9:]
            if first:
                out, u = [], ADA_FIRST
                for x in a:
                    out.append(x)
                    if x[0] == "F":
                        for _ in range(2 if x[1] < 4 else 1):
                            out.append(("A", u))
                            u += 1
                a = out + [("E", u - 1)]
            return [x for x in a if vector or x[0] not in "VN"]

        def N(t):
            return "N", t

        def ada_pieces_after(f):
            return [ADA_FIRST + 2 * f, ADA_FIRST + 2 * f + 1] if f < 4 else [ADA_FIRST + 4 + f]

        def ada_buffer(u):
            b = (u % 3) if u < ADA_FIRST else (u % 2)
            t = (xt if b < 2 else acc)[:, 2 * (b % 2):2 * (b % 2) + 2, :]
            return t.rearrange("p t (a n) -> p (t a) n", a=4)

        def ada_bias(u):
            return gs[0:1 + NB, ADA_COLS * (u % 4):ADA_COLS * (u % 4) + ADA_COLS]

        x0_tile = [acc[:, 4, :], rows[:, 1, :], rows[:, 0, :], rows[:, 2, :]]
        prep, w_s_rows = acc[:, 2:4, :], rows[:, 0, :]

        def down_bank(nt, parity, j):
            return 4 + (2 * nt * parity + j) % 4

        def sgu_bank(t, half):
            if half and t >= 2:
                return V_BANK[t] - 2 if t < 4 else 2
            return V_BANK[t]

        block = ctx.enter_context(nc.Block())

        @block.sync
        def _(sp):
            def ada_weights(u):
                if u >= 3:
                    sp.wait_ge(ada_mm, u - 2 if u < ADA_FIRST else u - 1)
                sp.dma_start(ada_buffer(u), w_ada_v[:, :, ada_col(u):ada_col(u) + ADA_COLS]
                             ).then_inc(ada_in[u % 4], 16)

            def ada_bias_in(u):
                if u >= 4:
                    sp.wait_ge(ada_tr, u - 3)
                    sp.wait_ge(ada_out[u % 4], 16 * (u // 4))
                sp.dma_start(ada_bias(u), bcast(b_ada[0, ada_col(u):ada_col(u) + ADA_COLS], 1 + NB)
                             ).then_inc(ada_in[u % 4], 16)

            def ada_rows_out(u):
                sp.wait_ge(ada_row, u + 1)
                sp.dma_start(mod_rows[:, ada_col(u):ada_col(u) + ADA_COLS], ada_bias(u)
                             ).then_inc(ada_out[u % 4], 16)

            def ada_piece(u):
                ada_weights(u)
                ada_rows_out(u - 3)
                ada_bias_in(u)

            def x0_load(t):
                sp.dma_start(x0_tile[t], x_prompt[0, P * t:P * t + P, :]).then_inc(x0_loaded, 16)

            sp.dma_start(rows[0:1, 2, :], c_prompt).then_inc(s_c, 16)
            sp.dma_start(rows[1:1 + NB, 2, :], c_sample).then_inc(s_c, 16)
            ada_weights(0)
            ada_bias_in(0)
            sp.dma_start(w_s_rows.rearrange("p (h j) -> p h j", h=HEADS),
                         w_s[0].rearrange("h i j -> i h j")).then_inc(s_pre, 16)
            sp.dma_start(htmp[0:NB * CONV_BUF, 0, 0:W_CONV],
                         state_conv[0].rearrange("b r c -> (b r) c")).then_inc(s_pre, 16)
            sp.dma_start(htmp[0:NB * POOL_BUF, 1, 0:W_POOL],
                         state_pool[0].rearrange("b r c -> (b r) c")).then_inc(s_pre, 16)
            for half in range(2):
                sp.dma_start(bsR[64 * half:64 * half + 64, :, :],
                             bcast(b_s[0].rearrange("(q two) i -> two q i", two=2)[half], 64)
                             ).then_inc(s_pre, 16)
            sp.dma_start(sgu_gb[:, 0, :], bcast(sgu_g[0], P)).then_inc(s_pre, 16)
            sp.dma_start(sgu_gb[:, 1, :], bcast(sgu_b[0], P)).then_inc(s_pre, 16)
            for c in range(2):
                sp.dma_start(convw[:, c, :],
                             conv_w[0, :, P * c:P * c + P].rearrange("w p -> p w")).then_inc(s_pre, 16)
            sp.dma_start(pscale[:, :], pool_scale[0].rearrange("(c p) -> p c", p=P)).then_inc(s_pre, 16)
            sp.dma_start(lnT[:, 0, :], ln1_g[0].rearrange("(k p) -> p k", p=P)).then_inc(s_pre, 16)
            sp.dma_start(lnT[:, 1, :], ln1_b[0].rearrange("(k p) -> p k", p=P)).then_inc(s_pre, 16)
            sp.dma_start(xt[0:ST, 4, :], x_sample.rearrange("b t d -> (b t) d")).then_inc(s_pre, 16)
            for u in range(1, 3):
                ada_weights(u)
                ada_bias_in(u)
            for t in range(2):
                x0_load(t)
            sp.wait_ge(s_prep, 1)
            for g in range(4):
                q, c = 64 * (g % 2), g // 2
                sp.dma_start(prep[q:q + 64, 0, P * c + q:P * c + q + 64], pool_w[0, g]).then_inc(s_corner, 16)
            sp.wait_ge(s_pret, 1)
            for b in range(NB):
                sp.dma_start(prep[DT * b:DT * b + DT, 0, 2 * P:2 * P + HEADS * ST].rearrange(
                                 "p (h i) -> p h i", h=HEADS)[:, :, DT * b:DT * b + DT],
                             prep[0:DT, 1, :].rearrange("p (h i) -> p h i", h=HEADS)[:, :, 0:DT]
                             ).then_inc(s_corner, 16)
            for t in (2, 3):
                x0_load(t)

            def slab(s, n, src, sizes, i=None, free=True):
                slot = (n if i is None else i) % RAW
                if free:
                    sp.wait_ge(lo_done, s * N_SLABS + n - RAW + 1)
                dst = raw[:, slot, :]
                if sizes:
                    dst = dst.rearrange("p (k n) -> p k n", k=sizes)
                sp.dma_start(dst, src).then_inc(raw_loaded[slot], 16)

            def early_slab(s, n, free=True):
                if n < SLAB_FM:
                    slab(s, n, w_in_v[:, 2 * n:2 * n + 2, COL_V:COL_V + W_GMLP], 2, free=free)
                elif n < SLAB_O:
                    col = FM_COLS[n - SLAB_FM]
                    slab(s, n, w_in_v[:, :, col:col + P], KD)
                else:
                    h, k = (n - SLAB_O) // 4, O_PAIRS[(n - SLAB_O) % 4][0]
                    slab(s, n, w_out_v[:, k:k + 2, HALF * h:HALF * h + HALF], 2)

            def load_residual(s):
                for t in range(4):
                    sp.dma_start(xt[:, t, :], x_prompt[0, bass.ds(s * GT + P * t, P), :]
                                 ).then_inc(x_loaded[t], 16)
                sp.dma_start(rows[:, 0, :], bcast(mod_rows[0, G1 * D:G1 * D + D], P)).then_inc(rows_loaded, 16)
                sp.dma_start(rows[:, 1, :], bcast(ln1_g[0], P)).then_inc(rows_loaded, 16)
                sp.dma_start(rows[:, 2, :], bcast(ln1_b[0], P)).then_inc(rows_loaded, 16)

            def load_gs(which):
                for b in range(NB):
                    sp.dma_start(gs[DT * b:DT * b + DT, :],
                                 bcast(mod_rows[1 + b, which * D:which * D + D], DT)).then_inc(gs_loaded, 16)

            def store(s, t):
                sp.wait_ge(y_ready, 4 * s + t + 1)
                if t < 4:
                    dst = y_prompt[0, bass.ds(s * GT + P * t, P), :]
                else:
                    dst = y_sample.rearrange("b t d -> (b t) d")
                sp.dma_start(dst, xt[0:rows_of(t), t, :]).then_inc(y_stored, 16)

            def mixer_slab(s, n):
                early_slab(s, n)
                if 16 <= n < 20:
                    store(s - 1, n - 16)
                if n == 20:
                    sp.wait_ge(y_stored, 64 * s)
                    load_residual(s)

            def mlp_dma(s, nt, last):
                def up(g, f, i, n):
                    slab(s, n, w_up_v[:, :, bass.ds(f * P, P)], KD, i)

                def down(f, i, n):
                    slab(s, n, w_down_v[:, bass.ds(f, 1), :].rearrange("p a n -> p (a n)"), 0, i)

                def next_x(t):
                    if t:
                        sp.wait_ge(xt_tr, 4 * s + t)
                    sp.dma_start(gs[:, :], x_prompt[0, bass.ds(s * GT + GT + P * t, P), :]).then_inc(gs_x, 16)

                for i in range(2):
                    up(0, i, i, SLAB_UP0 + i)
                for i in range(2):
                    up(1, 2 + i, i, SLAB_UP0 + 2 + i)
                for i in range(2):
                    down(i, i, SLAB_UP0 + 4 + i)
                with sp.Fori(1, 4) as g:
                    for i in range(2):
                        up(g + 1, 2 * g + 2 + i, i, SLAB_UP0 + 2 + 4 * g + i)
                    for i in range(2):
                        down(2 * g + i, i, SLAB_UP0 + 4 + 4 * g + i)
                sp.wait_ge(x1_ready, s + 1)
                sp.dma_start(rows[:, 0, :], bcast(mod_rows[0, G2 * D:G2 * D + D], P)).then_inc(rows_loaded, 16)
                sp.dma_start(rows[:, 1, :], bcast(ln2_g[0], P)).then_inc(rows_loaded, 16)
                sp.dma_start(rows[:, 2, :], bcast(ln2_b[0], P)).then_inc(rows_loaded, 16)
                if last:
                    sp.wait_ge(st_rows, 8)
                    for dst, n, q in STATES:
                        sp.dma_start(dst, gs[0:n, 2 * P * q:2 * P * q + 2 * P]).then_inc(st_stored, 16)
                    sp.wait_ge(st_stored, 16 * len(STATES))
                    load_gs(G2)
                else:
                    next_x(0)
                with sp.Fori(4, 15) as g:
                    for i in range(2):
                        up(g + 1, 2 * g + 2 + i, i, SLAB_UP0 + 2 + 4 * g + i)
                    for i in range(2):
                        down(2 * g + i, i, SLAB_UP0 + 4 + 4 * g + i)
                for i in range(2):
                    down(30 + i, i, 86 + i)
                if not last:
                    for n in range(12):
                        if n in (0, 2, 3):
                            next_x({0: 1, 2: 2, 3: 3}[n])
                        early_slab(s + 1, n)

            ada_weights(3)
            ada_bias_in(3)
            for n in range(RAW):
                early_slab(0, n, free=False)
            ada_rows_out(0)
            ada_piece(4)
            for n in range(RAW, 9):
                if n < 7:
                    ada_piece(n + 3)
                early_slab(0, n)
            for f in range(N_FM):
                u = ada_pieces_after(f)
                if f:
                    ada_piece(u[0])
                early_slab(0, 9 + f)
                if f and len(u) > 1:
                    ada_piece(u[1])
            for u in range(N_ADA - 3, N_ADA):
                ada_rows_out(u)
            for i in range(4):
                sp.wait_ge(ada_out[i], 16 * (N_ADA // 4))
            sp.wait_ge(x_split, 8)
            load_residual(0)
            for n in range(21, 24):
                early_slab(0, n)
            mlp_dma(0, 4, False)
            with sp.Fori(1, SUPERS - 1) as s:
                for n in range(12, 24):
                    mixer_slab(s, n)
                mlp_dma(s, 4, False)
            s = SUPERS - 1
            for n in range(12, 16):
                mixer_slab(s, n)
            sp.wait_ge(v_norm, 4 * s + 1)
            sp.dma_start(o_v_s[0].rearrange("b t c -> (b t) c"), gs[0:ST, 0:W_GMLP]).then_inc(v_stored, 16)
            sp.wait_ge(v_stored, 16)
            load_gs(G1)
            for n in range(16, 24):
                mixer_slab(s, n)
            mlp_dma(s, 5, True)
            for t in range(5):
                store(s, t)
            sp.wait_ge(y_stored, 64 * SUPERS + 16)

        @block.gpsimd
        def _(pool):
            count = [0]

            def step(ins):
                count[0] += 1
                ins.then_inc(s_pool0, 1)
                pool.wait_ge(s_pool0, count[0])

            step(pool.memset(ident[:, :], 0.0))
            pool.affine_select(out=ident[:, :], in_=ident[:, :], compare_op=ALU.not_equal, fill=1.0,
                               base=0, pattern=[[-1, P]], channel_multiplier=1).then_inc(s_ident, 1)
            for m in (ln_now, ln_end):
                step(pool.memset(m[0][:, :, :], 1.0))
            pool.memset(prep[:, :, :], 0.0).then_inc(s_prep, 1)
            step(pool.memset(zcarry[:, :, :], 0.0))
            step(pool.memset(pcarry[:, :, :], 0.0))
            for g, w in enumerate(WINDOWS):
                q, c = 64 * (g % 2), g // 2
                step(pool.memset(invw[q:q + 64, c:c + 1], 1.0 / w))
                step(pool.memset(invtab[q:q + 64, c, :], 1.0 / w))
                for t in range(w - 1):
                    step(pool.memset(invtab[q:q + 64, c, t:t + 1], 1.0 / (t + 1)))
            def lo_part(j, count):
                pool.wait_ge(hi_done, count)
                pool.tensor_tensor(W[:, j, 1, :], raw[:, j % RAW, :], W[:, j, 0, :],
                                   ALU.subtract).then_inc(lo_done, 1)

            lo_part(0, 1)
            lo_part(1, 2)
            pool.wait_ge(s_corner, 16 * (4 + NB))
            v = prep[0:ST, 0, 2 * P:2 * P + HEADS * ST].rearrange("p (h i) -> p h i", h=HEADS)
            step(pool.affine_select(out=v, in_=v, compare_op=ALU.is_ge, fill=0.0,
                                    base=0, pattern=[[0, HEADS], [1, ST]], channel_multiplier=-1))
            step(pool.tensor_copy(wsS[0:ST, 0, :, :], v))
            step(pool.tensor_tensor(wsS[0:ST, 1, :, :], v, wsS[0:ST, 0, :, :], ALU.subtract))
            v = prep[:, 0, 0:2 * P].rearrange("p (c n) -> p c n", c=2)
            step(pool.tensor_copy(pwT[:, 0, :, :], v))
            step(pool.tensor_tensor(pwT[:, 1, :, :], v, pwT[:, 0, :, :], ALU.subtract))
            v = prep[:, 1, :].rearrange("p (h i) -> p h i", h=HEADS)
            step(pool.affine_select(out=v, in_=v, compare_op=ALU.is_ge, fill=0.0,
                                    base=0, pattern=[[0, HEADS], [1, P]], channel_multiplier=-1))
            step(pool.tensor_copy(wsT[:, 0, :, :], v))
            pool.tensor_tensor(wsT[:, 1, :, :], v, wsT[:, 0, :, :], ALU.subtract).then_inc(s_prep, 1)

            lo_part(2, 3)
            lo_part(3, 4)
            with pool.Fori(1, SUPERS * N_SLABS // SLOTS) as i:
                for j in range(SLOTS):
                    lo_part(j, SLOTS * i + j + 1)

            def gate_acc(t):
                pool.wait_ge(d_evac, 128 * (SUPERS - 1) + 15 * 10 + 2 * t + 2)
                a = acc[0:rows_of(t), t, :]
                pool.tensor_tensor(a, a, rows[:, 0, :] if t < 4 else gs[0:ST, :],
                                   ALU.mult).then_inc(acc_gated, 1)

            def gain(t):
                pool.wait_ge(e_norm, 3 * (SUPERS - 1) + t + 1)
                x = xt[0:rows_of(t), t, :]
                pool.tensor_tensor(x, x, rows[0:rows_of(t), 1, :], ALU.mult).then_inc(y_scaled, 1)

            pool.wait_ge(rows_loaded, 96 * SUPERS)
            pool.wait_ge(gs_loaded, 2 * 16 * NB)
            for t in range(5):
                gate_acc(t)
            for t in range(5):
                gain(t)

        @block.scalar
        def _(act):
            act.wait_ge(s_cT, 1)
            act.activation(siluT[:, :], ps[:, 0, 0:KD * (1 + NB)], ACT.Silu).then_inc(s_silu, 1)

            def hi_part(s, n, slot=None, turn=None, free=True):
                slot = n % SLOTS if slot is None else slot
                turn = n // RAW if turn is None else turn
                act.wait_ge(raw_loaded[slot % RAW], (s * (N_SLABS // RAW) + turn + 1) * 16)
                if free:
                    act.wait_ge(slab_used, s * N_SLABS + n - SLOTS + 1)
                act.activation(W[:, slot, 0, :], raw[:, slot % RAW, :], ACT.Copy).then_inc(hi_done, 1)

            def x_affine(s, t):
                act.wait_ge(xt_tr, 4 * (s - 1) + t + 1)
                for half in range(2):
                    if t:
                        act.wait_ge(x_split, 8 * s + 2 * t + half - 1)
                    else:
                        act.wait_ge(hid_ready, 32 * s - 1 + half)
                    for q in range(4):
                        k = 4 * half + q
                        ins = act.activation(htmp[:, half, P * q:P * q + P],
                                             ps[:, 2 * (t % 2) + half, P * q:P * q + P], ACT.Identity,
                                             bias=modT[:, SH1 * KD + k, 0:1], scale=modT[:, SC1 * KD + k, 0:1])
                    ins.then_inc(x_tmp, 1)

            def x0_affine(k):
                act.wait_ge(x0_tr, k + 1)
                act.wait_ge(ada_T, 2 * (k // 2) + 2)
                if k >= 2:
                    act.wait_ge(x_split, k - 1)
                act.activation(htmp[:, k % 2, 0:GT], ps[:, 2 * (k % 2), :], ACT.Identity,
                               bias=modT[:, SH1 * KD + k, 0:1], scale=modT[:, SC1 * KD + k, 0:1]
                               ).then_inc(x_tmp, 1)

            def relu2(s, f, i, n, nt, first=False):
                act.wait_ge(slab_used, s * N_SLABS + n + 1)
                if not first:
                    act.wait_ge(hid_ready, s * 32 + f - 1)
                h = as_fm(htmp[:, i, :], nt)
                act.activation(h, fm_view(2 * i, nt), ACT.Relu).then_inc(s_chain_act, 1)
                act.wait_ge(s_chain_act, s * 32 + f + 1)
                act.activation(h, h, ACT.Square).then_inc(relu_done, 1)

            def end_normal(t, count):
                act.wait_ge(e_stats, count)
                r = rows_of(t)
                act.activation(xt[0:r, t, :], xt[0:r, t, :], ACT.Identity, bias=ln_end[2][0:r, t:t + 1],
                               scale=ln_end[1][0:r, t:t + 1]).then_inc(e_norm, 1)

            def super_act(s, nt, first, last):
                def v_normal(t, count):
                    act.wait_ge(v_stats, count)
                    r = rows_of(t)
                    act.activation(ps[0:r, V_BANK[t], :], ps[0:r, V_BANK[t], :], ACT.Identity,
                                   bias=ln_now[2][0:r, t:t + 1], scale=ln_now[1][0:r, t:t + 1]
                                   ).then_inc(v_norm_act, 1)

                def o_normal(t):
                    act.wait_ge(o_stats, s + 1)
                    act.activation(xt[:, t, :], xt[:, t, :], ACT.Identity, bias=ln_now[2][:, t:t + 1],
                                   scale=ln_now[1][:, t:t + 1]).then_inc(xn_act, 1)

                for n in range(SLAB_UP0):
                    if n == 3 and nt == 5:
                        v_normal(4, s + 1)
                    if n == 4:
                        for t in range(4):
                            v_normal(t, s + nt - 3)
                        if not first:
                            for t in (1, 2, 3):
                                end_normal(t, s)
                    hi_part(s, n + SLOTS)
                o_normal(0)
                o_normal(1)
                if first:
                    act.wait_ge(s_mod2, 1)
                for k in range(KD):
                    act.wait_ge(o_tr, 8 * s + k + 1)
                    if k >= 2:
                        act.wait_ge(o_split, 8 * s + k - 1)
                    act.activation(htmp[:, k % 2, 0:GT], ps[:, 4 + 2 * (k % 2), :], ACT.Identity,
                                   bias=bias2[:, k, 0:1], scale=scale2[:, k, 0:1]).then_inc(o_tmp, 1)
                for i in range(2):
                    relu2(s, i, i, SLAB_UP0 + i, nt, first=True)
                    hi_part(s, SLAB_UP0 + SLOTS + i)
                for i in range(2):
                    relu2(s, 2 + i, i, SLAB_UP0 + 2 + i, nt)
                    hi_part(s, SLAB_UP0 + 2 + SLOTS + i)
                for i in range(2):
                    hi_part(s, SLAB_UP0 + 4 + SLOTS + i)

                def ups(g):
                    for i in range(2):
                        n = SLAB_UP0 + 2 + 4 * g + i
                        relu2(s, 2 * g + 2 + i, i, n, nt)
                        hi_part(s, n + SLOTS, slot=2 + i, turn=(SLAB_UP0 + 2 + SLOTS) // RAW + 2 * g)

                with act.Fori(1, 14) as g:
                    ups(g)
                    for i in range(2):
                        hi_part(s, SLAB_UP0 + 4 + 4 * g + i + SLOTS, slot=i,
                                turn=(SLAB_UP0 + 4 + SLOTS) // RAW + 2 * g)
                ups(14)
                if not last:
                    for half in range(2):
                        for t in (2 * half, 2 * half + 1):
                            x_affine(s + 1, t)
                        for i in range(2):
                            hi_part(s, N_SLABS + 2 * half + i)

            for n in range(4):
                x0_affine(2 * n)
                x0_affine(2 * n + 1)
                for m in ((0, 1), (2,), (3,), ())[n]:
                    hi_part(0, m, free=False)
            super_act(0, 4, True, False)
            with act.Fori(1, SUPERS - 1) as s:
                super_act(s, 4, False, False)
            super_act(SUPERS - 1, 5, False, True)
            for t in range(5):
                end_normal(t, SUPERS + (t > 1))

        @block.tensor
        def _(pe):
            def mm3(out, w_hi, w_lo, x_hi, x_lo, start, stop):
                pe.matmul(out, w_hi, x_hi, start=start, stop=False)
                pe.matmul(out, w_hi, x_lo, start=False, stop=False)
                return pe.matmul(out, w_lo, x_hi, start=False, stop=stop)

            def ada_product(u):
                pe.wait_ge(ada_in[u % 4], 32 * (u // 4 + 1))
                if u >= 2:
                    pe.wait_ge(ada_T, u - 1)
                if u in (ADA_FIRST, ADA_FIRST + 1):
                    pe.wait_ge(xs_split, 1)
                buf = ada_buffer(u)
                for k in range(KD):
                    ins = pe.matmul(ps[0:1 + NB, 1 + 2 * (u % 2), 0:ADA_COLS],
                                    siluT[:, (1 + NB) * k:(1 + NB) * (k + 1)], buf[:, k, :],
                                    start=(k == 0), stop=(k == KD - 1))
                ins.then_inc(ada_mm, 1)

            def ada_turn(u):
                pe.wait_ge(ada_row, u + 1)
                for q in range(2):
                    ins = pe.transpose(ps[:, 1 + 2 * (u % 2), (1 + NB) * q:(1 + NB) * (q + 1)],
                                       ada_bias(u)[:, P * q:P * q + P], ident[0:1 + NB, 0:1 + NB])
                ins.then_inc(ada_tr, 1)

            def x_transposes(src, t, s):
                for k in range(KD):
                    ins = pe.transpose(ps[:, 2 * (t % 2) + k // 4, P * (k % 4):P * (k % 4) + P],
                                       src[:, P * k:P * k + P], ident[:, :])
                ins.then_inc(xt_tr, 1)

            pe.wait_ge(s_c, 32)
            pe.wait_ge(s_ident, 1)
            for k in range(KD):
                ins = pe.transpose(ps[:, 0, (1 + NB) * k:(1 + NB) * (k + 1)],
                                   rows[0:1 + NB, 2, P * k:P * k + P], ident[0:1 + NB, 0:1 + NB])
            ins.then_inc(s_cT, 1)
            pe.wait_ge(s_silu, 1)
            ada_product(0)
            pe.wait_ge(s_pre, 16 * N_PRE)
            for c in range(2):
                pe.transpose(ps[:, 5, 16 * c:16 * c + 16], htmp[0:16, 0, P * c:P * c + P], ident[0:16, 0:16])
            for c in range(2):
                pe.transpose(ps[:, 5, 128 + 120 * c:128 + 120 * c + 120],
                             htmp[0:120, 1, P * c:P * c + P], ident[0:120, 0:120])
            for h in range(HEADS):
                ins = pe.transpose(ps[:, 6 + h // 4, P * (h % 4):P * (h % 4) + P],
                                   w_s_rows[:, P * h:P * h + P], ident[:, :])
            ins.then_inc(s_prepe, 1)

            def v_slab(s, n, nt, first=False):
                pe.wait_ge(lo_done, s * N_SLABS + n + 1)
                if first:
                    pe.wait_ge(x_split, 2 * n + 2)
                order = v_order(nt) if n else range(nt)
                for pos, t in enumerate(order):
                    r = rows_of(t)
                    if n == 0 and not first:
                        pe.wait_ge(x_split, 8 * s + 2 * min(t, 3) + 2)
                        pe.wait_ge(d_evac, 128 * s - 3 + min(t, 3))
                    for kk in range(2):
                        k = 2 * n + kk
                        ins = mm3(ps[0:r, V_BANK[t], :], hT[:, 0, k, tokens(t)], hT[:, 1, k, tokens(t)],
                                  W[:, n, 0, 512 * kk:512 * kk + 512], W[:, n, 1, 512 * kk:512 * kk + 512],
                                  k == 0, k == KD - 1)
                    if n == 3 and pos < nt - 1:
                        ins.then_inc(v_done, 1)
                ins.then_inc(slab_used, 1)

            def x0_transposes(k):
                if k >= 2:
                    pe.wait_ge(x_tmp, k - 1)
                for t in range(4):
                    ins = pe.transpose(ps[:, 2 * (k % 2), P * t:P * t + P],
                                       x0_tile[t][:, P * k:P * k + P], ident[:, :])
                ins.then_inc(x0_tr, 1)

            def ada_next(u):
                ada_product(u)
                ada_turn(u - 1)

            ada_next(1)
            for n in range(3):
                ada_next(2 * n + 2)
                if n == 0:
                    pe.wait_ge(x0_loaded, 64)
                x0_transposes(2 * n)
                x0_transposes(2 * n + 1)
                ada_next(2 * n + 3)
                if n < 2:
                    v_slab(0, n, 4, first=True)
            ada_turn(ADA_FIRST - 1)
            x0_transposes(6)
            x0_transposes(7)
            v_slab(0, 2, 4, first=True)
            pe.wait_ge(ada_T, ADA_FIRST)
            for k in range(KD):
                ins = pe.transpose(ps[:, 1 + 2 * (k // 4), P * (k % 4):P * (k % 4) + ST],
                                   xt[0:ST, 4, P * k:P * k + P], ident[0:ST, 0:ST])
            ins.then_inc(xs_tr, 1)
            v_slab(0, 3, 4, first=True)

            def fm_product(s, n, slot, bank, nt):
                pe.wait_ge(lo_done, s * N_SLABS + n + 1)
                w = W[:, slot, :, :].rearrange("p l (k n) -> p l k n", k=KD)
                for c, (a, b) in enumerate(chunks(nt)):
                    for k in range(KD):
                        ins = mm3(ps[:, bank + c, 0:b - a], w[:, 0, k, :], w[:, 1, k, :],
                                  hT[:, 0, k, a:b], hT[:, 1, k, a:b], k == 0, k == KD - 1)
                ins.then_inc(slab_used, 1)

            def sgu_half(s, nt, t, pos, half):
                r = rows_of(t)
                w = wsT if t < 4 else wsS
                n = 2 * r
                for q in range(2):
                    pair = 2 * half + q
                    v = rs[0:r, pos % 2, :, P * pair:P * pair + P]
                    ins = mm3(ps[:, sgu_bank(t, half), n * q:n * q + n], v[:, 0, :], v[:, 1, :],
                              w[0:r, 0, 2 * pair:2 * pair + 2, :], w[0:r, 1, 2 * pair:2 * pair + 2, :],
                              True, True)
                ins.then_inc(sgu_done, 1)

            def super_pe(s, nt, first, last):
                if not first:
                    for n in range(4):
                        v_slab(s, n, nt)
                halves = 0
                for stage in mixer_stages(nt, first, False):
                    if stage[0] == "F":
                        f = stage[1]
                        turns = fm_turns(nt, first)
                        if f >= turns:
                            pe.wait_ge(fm_evac, s * N_FM + f - turns + 1)
                        if f == 1 and nt == 5:
                            pe.wait_ge(sgu_evac, 8 * s + 2)
                        fm_product(s, SLAB_FM + f, f % SLOTS, fm_bank(f, nt, first), nt)
                    elif stage[0] == "S":
                        tiles, pos = stage[1], stage[2]
                        for half in range(2):
                            for i, t in enumerate(tiles):
                                if half == 0:
                                    pe.wait_ge(v_norm, 4 * s + pos + i + 1)
                                elif sgu_bank(t, 1) == V_BANK[t]:
                                    pe.wait_ge(sgu_evac, 8 * s + halves + i + 1)
                                else:
                                    pe.wait_ge(sgu_evac, 8 * s + halves)
                                sgu_half(s, nt, t, pos + i, half)
                        halves += 2 * len(tiles)
                    elif stage[0] == "A":
                        ada_product(stage[1])
                        if stage[1] > ADA_FIRST:
                            ada_turn(stage[1] - 1)
                    elif stage[0] == "E":
                        ada_turn(stage[1])
                    else:
                        c = stage[1]
                        pe.wait_ge(d_ready, 2 * s + c + 1)
                        for q, (a, b) in enumerate(chunks(nt)):
                            ins = mm3(ps[:, 4 + 2 * c + q, 0:b - a], pwT[:, 0, c, :], pwT[:, 1, c, :],
                                      rs[:, c, 0, a:b], rs[:, c, 1, a:b], True, True)
                        ins.then_inc(pm_done, 1)
                def o_product(h, q, t):
                    r = rows_of(t)
                    for kk, k in enumerate(O_PAIRS[q]):
                        ins = mm3(ps[0:r, o_bank(h, t), :],
                                  MH[:, 0, k, tokens(t)], MH[:, 1, k, tokens(t)],
                                  W[:, q, 0, 512 * kk:512 * kk + 512],
                                  W[:, q, 1, 512 * kk:512 * kk + 512],
                                  q == 0 and kk == 0, q == 3 and kk == 1)
                    return ins

                for h in range(2):
                    for q in range(4):
                        n = SLAB_O + 4 * h + q
                        pe.wait_ge(lo_done, s * N_SLABS + n + 1)
                        if h == 0:
                            pe.wait_ge(mix_ready, 8 * s + (8 if q == 3 else 6))
                        elif q == 0:
                            pe.wait_ge(o_evac, 8 * s + 2)
                            if first:
                                pe.wait_ge(ada_T, N_ADA)
                        if h == 1 and q == 2:
                            continue
                        for t in range(nt):
                            if h == 0 and q == 0 and t == 4:
                                pe.wait_ge(mix_ready, 8 * s + 7)
                            if h == 1 and q == 3:
                                ins = o_product(h, 2, t)
                                if t == nt - 1:
                                    ins.then_inc(slab_used, 1)
                            ins = o_product(h, q, t)
                            if q == 3 and t < nt - 1:
                                ins.then_inc(o_done, 1)
                        ins.then_inc(slab_used, 1)

                def o_transpose(k, t):
                    r, bank = rows_of(t), 4 + 2 * (k % 2)
                    dst = ps[:, bank, P * t:P * t + P] if t < 4 else ps[:, bank + 1, 0:ST]
                    return pe.transpose(dst, xt[0:r, t, P * k:P * k + P], ident[0:r, 0:r])

                def o_transposes(k):
                    pe.wait_ge(o_tmp, 8 * s + k - 1)
                    if nt == 5:
                        pe.wait_ge(o_split, 8 * s + k - 1)
                    for t in range(nt):
                        ins = o_transpose(k, t)
                    ins.then_inc(o_tr, 1)

                for t in range(nt):
                    if t in XN_ACT:
                        pe.wait_ge(xn_act, 2 * s + XN_ACT.index(t) + 1)
                    else:
                        pe.wait_ge(xn_dve, 2 * s + t - 1)
                    if t == 0:
                        pe.wait_ge(o_evac, 8 * s + 2 * nt)
                    for k in range(2):
                        ins = o_transpose(k, t)
                        if t == nt - 1:
                            ins.then_inc(o_tr, 1)
                w = W[:, 0:2, :, :].rearrange("p s l (k n) -> p s l k n", k=KD)
                for k in range(KD):
                    pe.wait_ge(o_split, 8 * s + k + 1)
                    for i in range(2):
                        if k == 0:
                            pe.wait_ge(lo_done, s * N_SLABS + SLAB_UP0 + i + 1)
                        for c, (a, b) in enumerate(chunks(nt)):
                            ins = mm3(ps[:, 2 * i + c, 0:b - a], w[:, i, 0, k, :], w[:, i, 1, k, :],
                                      hT[:, 0, k, a:b], hT[:, 1, k, a:b], k == 0, k == KD - 1)
                        if k == KD - 1:
                            ins.then_inc(slab_used, 1)
                    if k + 2 < KD:
                        o_transposes(k + 2)

                def up(g, slab0, slot0):
                    for i in range(2):
                        pe.wait_ge(relu_done, s * 32 + 2 * g + i - 1)
                        fm_product(s, slab0 + i, slot0 + i, 2 * i, nt)

                def down(g, parity, slab0, slot0, after=None):
                    pe.wait_ge(lo_done, s * N_SLABS + slab0 + 2)
                    pe.wait_ge(hid_ready, s * 32 + 2 * g + 2)
                    for t in range(nt):
                        r = rows_of(t)
                        for h in range(2):
                            j = 2 * t + h
                            if j >= 4 or not (isinstance(g, int) and g == 0):
                                pe.wait_ge(d_evac, s * 128 + g * (2 * nt) + j - 3)
                            end = j == 2 * nt - 1
                            for kk in range(2):
                                ins = mm3(ps[0:r, down_bank(nt, parity, j), :],
                                          MH[:, 0, 2 * parity + kk, tokens(t)],
                                          MH[:, 1, 2 * parity + kk, tokens(t)],
                                          W[:, slot0 + kk, 0, HALF * h:HALF * h + HALF],
                                          W[:, slot0 + kk, 1, HALF * h:HALF * h + HALF],
                                          kk == 0, kk == 1)
                                if end:
                                    ins.then_inc(slab_used, 1)
                            if not end:
                                ins.then_inc(d_done, 1)
                        if after:
                            after(t)

                def next_x(t):
                    pe.wait_ge(gs_x, 64 * s + 16 * t + 16)
                    if t < 2:
                        pe.wait_ge(relu_done, 32 * s + 31 + t)
                    else:
                        pe.wait_ge(x_tmp, 8 * (s + 1) + 2 * t - 2)
                    x_transposes(gs, t, s + 1)

                up(1, SLAB_UP0 + 2, 2)
                if last:
                    pe.wait_ge(o_tmp, 8 * s + 8)
                    for c in range(2):
                        for q, a in enumerate((zlast[:, c, 0:CONV_BUF], zlast[:, c, CONV_BUF:],
                                               plast[:, c, 0:POOL_BUF], plast[:, c, POOL_BUF:])):
                            ins = pe.transpose(ps[0:a.shape[1], 6 + c, P * q:P * q + P], a, ident[:, :])
                    ins.then_inc(st_tr, 1)
                down(0, 0, SLAB_UP0 + 4, 0,
                     after=(lambda t: pe.wait_ge(st_rows, 8) if t == 0 else None) if last else None)
                with pe.Fori(0, 6) as j:
                    for par in (1, 0):
                        g = 2 * j + (1 if par else 2)
                        up(g + 1, SLAB_UP0 + 2 + 4 * g, 2)
                        down(g, par, SLAB_UP0 + 4 + 4 * g, 0)
                up(14, SLAB_UP0 + 2 + 4 * 13, 2)
                down(13, 1, SLAB_UP0 + 4 + 4 * 13, 0)
                up(15, SLAB_UP0 + 2 + 4 * 14, 2)
                down(14, 0, SLAB_UP0 + 4 + 4 * 14, 0,
                     after=None if last else lambda t: None if t % 2 else next_x(t // 2))
                down(15, 1, 86, 2,
                     after=None if last else lambda t: None if t % 2 else next_x(2 + t // 2))

            super_pe(0, 4, True, False)
            with pe.Fori(1, SUPERS - 1) as s:
                super_pe(s, 4, False, False)
            super_pe(SUPERS - 1, 5, False, True)

        @block.vector
        def _(dve):
            base, local = [0], [0]

            def step(ins):
                ins.then_inc(s_chain, 1)
                local[0] += 1

            def sync():
                dve.wait_ge(s_chain, base[0] + local[0])

            def do(ins):
                step(ins)
                sync()

            def signal(ins, sem_, value):
                ins.then_inc(sem_, 1)
                dve.wait_ge(sem_, value)

            def ada_add(u):
                dve.wait_ge(ada_mm, u + 1)
                dve.tensor_tensor(ada_bias(u), ps[0:1 + NB, 1 + 2 * (u % 2), 0:ADA_COLS], ada_bias(u),
                                  ALU.add).then_inc(ada_row, 1)

            def ada_turned(u):
                dve.wait_ge(ada_tr, u + 1)
                q = ada_col(u) // P
                dst, src = modT[:, q:q + 2, :], ps[:, 1 + 2 * (u % 2), 0:2 * (1 + NB)].rearrange(
                    "p (q n) -> p q n", q=2)
                if q // KD == SC1:
                    dve.tensor_scalar(dst, src, 1.0, None, ALU.add).then_inc(ada_T, 1)
                else:
                    dve.tensor_copy(dst, src).then_inc(ada_T, 1)

            def second_modulation():
                dve.wait_ge(ada_T, N_ADA)
                sh2, sc2 = (modT[:, q * KD:q * KD + KD, :] for q in (SH2, SC2))
                lng, lnb = (lnT[:, i, :].unsqueeze(2).to_broadcast([P, KD, 1 + NB]) for i in range(2))
                do(dve.tensor_scalar(sc2, sc2, 1.0, None, ALU.add))
                do(dve.tensor_tensor(scale2[:, :, :], sc2, lng, ALU.mult))
                do(dve.tensor_tensor(bias2[:, :, :], sc2, lnb, ALU.mult))
                signal(dve.tensor_tensor(bias2[:, :, :], bias2[:, :, :], sh2, ALU.add), s_mod2, 1)

            def rsqrt(a, b, ln):
                mv, rstd, rtmp = ln
                var, y, u = mv[:, a:b, 1], rstd[:, a:b], rtmp[:, a:b]
                do(dve.tensor_scalar(var, var, EPS, None, ALU.add))
                do(dve.tensor_scalar(y.bitcast(I32), var.bitcast(I32), 1, None, ALU.logical_shift_right))
                do(dve.tensor_scalar(y.bitcast(I32), y.bitcast(I32), -1.0, RSQRT_MAGIC, ALU.mult, ALU.add))
                for _ in range(3):
                    do(dve.tensor_tensor(u, y, y, ALU.mult))
                    do(dve.scalar_tensor_tensor(u, u, -0.5, var, ALU.mult, ALU.mult))
                    do(dve.scalar_tensor_tensor(y, u, 1.5, y, ALU.add, ALU.mult))

            def sums(t, i, x):
                step(dve.bn_stats(st[0:rows_of(t), t, i, :], x))

            def mean_var(t, n, ln):
                r = rows_of(t)
                sync()
                dve.sem_inc(s_fence, 1)
                step(dve.bn_aggr(ln[0][0:r, t, :], st[0:r, t, 0:n, :].rearrange("p a b -> p (a b)")))

            def normalise(out, x, t, ln):
                r = rows_of(t)
                return dve.tensor_scalar(out, x, ln[0][0:r, t, 0:1], ln[1][0:r, t:t + 1],
                                         ALU.subtract, ALU.mult)

            def scale_bias(a, b, ln, sem_, value):
                sync()
                rsqrt(a, b, ln)
                signal(dve.scalar_tensor_tensor(ln[2][:, a:b], ln[0][:, a:b, 0], -1.0, ln[1][:, a:b],
                                                ALU.mult, ALU.mult), sem_, value)

            def split(hi, lo, x):
                do(dve.tensor_copy(hi, x))
                return dve.tensor_tensor(lo, x, hi, ALU.subtract)

            def modulate_sample(o, src, mul, add):
                do(dve.tensor_tensor(o, src, mul, ALU.mult))
                do(dve.tensor_tensor(o, o, add, ALU.add))

            def x_sample():
                dve.wait_ge(xs_tr, 1)
                x = acc[:, 0, 0:KD * ST].rearrange("p (k b t) -> p k b t", k=KD, b=NB)
                for half in range(2):
                    ks = slice(4 * half, 4 * half + 4)
                    src = ps[:, 1 + 2 * half, :].rearrange("p (k n) -> p k n", k=4)[:, :, 0:ST]
                    mul, add = (modT[:, q * KD + 4 * half:q * KD + 4 * half + 4, 1:].unsqueeze(3)
                                .to_broadcast([P, 4, NB, DT]) for q in (SC1, SH1))
                    modulate_sample(x[:, ks], src.rearrange("p k (b t) -> p k b t", b=NB), mul, add)
                x = acc[:, 0, 0:KD * ST].rearrange("p (k n) -> p k n", k=KD)
                signal(split(hT[:, 0, :, GT:GT + ST], hT[:, 1, :, GT:GT + ST], x), xs_split, 1)

            def x0_feature(k):
                dve.wait_ge(x_tmp, k + 1)
                signal(split(hT[:, 0, k, 0:GT], hT[:, 1, k, 0:GT], htmp[:, k % 2, 0:GT]), x_split, k + 1)

            def x_tile(s, t):
                for half in range(2):
                    n = 8 * s + 2 * t + half + 1
                    dve.wait_ge(x_tmp, n)
                    ks = slice(4 * half, 4 * half + 4)
                    x = htmp[:, half, 0:4 * P].rearrange("p (k n) -> p k n", k=4)
                    signal(split(hT[:, 0, ks, tokens(t)], hT[:, 1, ks, tokens(t)], x), x_split, n)

            def o_feature(s, nt, k):
                i, n = k % 2, GT + (ST if nt == 5 else 0)
                if nt == 5:
                    dve.wait_ge(o_tr, 8 * s + k + 1)
                    mul, add = (m[:, k, 1:].unsqueeze(2).to_broadcast([P, NB, DT]) for m in (scale2, bias2))
                    modulate_sample(htmp[:, i, GT:n].rearrange("p (b t) -> p b t", b=NB),
                                    ps[:, 5 + 2 * i, 0:ST].rearrange("p (b t) -> p b t", b=NB), mul, add)
                dve.wait_ge(o_tmp, 8 * s + k + 1)
                signal(split(hT[:, 0, k, 0:n], hT[:, 1, k, 0:n], htmp[:, i, 0:n]), o_split, 8 * s + k + 1)

            def v_tile(s, nt, t, pos):
                r = rows_of(t)
                x = htmp[0:r, 1, 0:W_GMLP] if t < 4 else gs[0:r, 0:W_GMLP]
                dve.wait_ge(v_norm_act, 4 * s + pos + 1)
                do(dve.tensor_tensor(x, ps[0:r, V_BANK[t], :], sgu_gb[0:r, 0, :], ALU.mult))
                do(dve.tensor_tensor(x, x, sgu_gb[0:r, 1, :], ALU.add))
                signal(split(rs[0:r, pos % 2, 0, 0:W_GMLP], rs[0:r, pos % 2, 1, 0:W_GMLP], x),
                       v_norm, 4 * s + pos + 1)

            def sgu_half(s, t, half, count):
                dve.wait_ge(sgu_done, 8 * s + count)
                r = rows_of(t)
                pr = slice(2 * half, 2 * half + 2)
                for odd in range(2):
                    q = slice(64 * odd, 64 * odd + 64)
                    src = ps[q, sgu_bank(t, half), 0:4 * r].rearrange("p (a h i) -> p a h i", a=2, h=2)[:, :, odd, :]
                    dst = sg[q, pr, tokens(t)]
                    bias = bsR[q, pr, 0:r]
                    if t == 4:
                        src = src.rearrange("p a (b i) -> p a b i", b=NB)
                        dst = dst.rearrange("p a (b i) -> p a b i", b=NB)
                        bias = bsR[q, pr, 0:DT].unsqueeze(2).to_broadcast([64, 2, NB, DT])
                    if odd:
                        dve.tensor_tensor(dst, src, bias, ALU.add).then_inc(sgu_evac, 1)
                    else:
                        step(dve.tensor_tensor(dst, src, bias, ALU.add))

            def copy_pieces(s, f, nt, bank, prompt, sample, other=None):
                ps_ = pieces(bank, nt)
                for n, (src, a) in enumerate(ps_):
                    w = src.shape[1]
                    if a is not None:
                        dst = prompt[:, a:a + w]
                        o = None if other is None else other[:, a:a + w]
                    else:
                        src = src.rearrange("p (b i) -> p b i", b=NB)
                        dst = sample
                        o = None if other is None else other[:, GT:GT + ST].rearrange("p (b i) -> p b i", b=NB)
                    ins = dve.tensor_copy(dst, src) if o is None else dve.tensor_tensor(dst, src, o, ALU.mult)
                    if n == len(ps_) - 1:
                        ins.then_inc(fm_evac, 1)
                    else:
                        step(ins)

            mix_order = [0, 2, 3, 6, 7, 1, 4, 5]

            def mix_out(s, nt, k, x):
                n = GT + (ST if nt == 5 else 0)
                signal(split(MH[:, 0, k, 0:n], MH[:, 1, k, 0:n], x),
                       mix_ready, 8 * s + mix_order.index(k) + 1)

            def wait_fm(s, f):
                dve.wait_ge(slab_used, s * N_SLABS + SLAB_FM + f + 1)

            def conv_fm(s, nt, f, bank):
                part, c = FM_PARTS[f]
                wait_fm(s, f)
                if part == "c":
                    dve.tensor_copy(as_fm(htmp[:, 0, :], nt), fm_view(bank, nt)).then_inc(fm_evac, 1)
                    dve.wait_ge(fm_evac, s * N_FM + f + 1)
                elif part == "x":
                    do(dve.tensor_copy(zp_[:, 0:CONV_BUF], zcarry[:, c, :]))
                    if nt == 5:
                        do(dve.tensor_copy(zs_[:, :, 0:CONV_BUF],
                                           zstate[:, c, :].rearrange("p (b n) -> p b n", b=NB)))
                    copy_pieces(s, f, nt, bank, zp_[:, CONV_BUF:], zs_[:, :, CONV_BUF:], htmp[:, 0, :])
                    sync()
                    dve.wait_ge(fm_evac, s * N_FM + f + 1)
                    seqs = [(bufA[:, 0:GT], lambda a: zp_[:, a:a + GT])]
                    if nt == 5:
                        seqs.append((bufA[:, GT:GT + ST].rearrange("p (b i) -> p b i", b=NB),
                                     lambda a: zs_[:, :, a:a + DT]))
                    for o, z in seqs:
                        do(dve.tensor_scalar(o, z(0), convw[:, c, 0:1], None, ALU.mult))
                        for a in (1, 2):
                            do(dve.scalar_tensor_tensor(o, z(a), convw[:, c, a:a + 1], o, ALU.mult, ALU.add))
                    step(dve.tensor_copy(zcarry[:, c, :], zp_[:, GT:GT + CONV_BUF]))
                    if nt == 5:
                        step(dve.tensor_copy(zlast[:, c, 0:CONV_BUF], zp_[:, GT:GT + CONV_BUF]))
                        step(dve.tensor_copy(
                            zlast[:, c, CONV_BUF:].rearrange("p (b n) -> p b n", b=NB), zs_[:, :, DT:]))
                    sync()
                else:
                    dve.tensor_tensor(as_fm(bufB, nt), fm_view(bank, nt), as_fm(bufA, nt),
                                      ALU.mult).then_inc(fm_evac, 1)
                    dve.wait_ge(fm_evac, s * N_FM + f + 1)
                    mix_out(s, nt, c, bufB[:, 0:GT + (ST if nt == 5 else 0)])

            def pool_fm(s, nt, f, bank):
                c = FM_PARTS[f][1]
                wait_fm(s, f)
                do(dve.tensor_copy(pp_[:, 0:POOL_BUF], pcarry[:, c, :]))
                if nt == 5:
                    do(dve.tensor_copy(psm[:, :, 0:POOL_BUF],
                                       pstate[:, c, :].rearrange("p (b n) -> p b n", b=NB)))
                copy_pieces(s, f, nt, bank, pp_[:, POOL_BUF:], psm[:, :, POOL_BUF:])
                sync()
                dve.wait_ge(fm_evac, s * N_FM + f + 1)
                seqs = [(pp_, lambda b, lo, hi: b[:, lo:hi], GT, htmp[:, 0, 0:GT], lambda b: b)]
                if nt == 5:
                    seqs.append((psm, lambda b, lo, hi: b[:, :, lo:hi], DT,
                                 htmp[:, 0, GT:GT + ST].rearrange("p (b i) -> p b i", b=NB),
                                 lambda b: b[:, 0:NB * (POOL_BUF + DT)].rearrange("p (b n) -> p b n", b=NB)))
                for z, cut, n, d, shape in seqs:
                    L = POOL_BUF + n
                    A, B = shape(bufA), shape(bufB)
                    do(dve.tensor_tensor(cut(A, 1, L), cut(z, 1, L), cut(z, 0, L - 1), ALU.add))
                    do(dve.tensor_tensor(cut(B, 3, L), cut(A, 3, L), cut(A, 1, L - 2), ALU.add))
                    if c == 1:
                        do(dve.tensor_tensor(cut(A, 7, L), cut(B, 7, L), cut(B, 3, L - 4), ALU.add))
                        do(dve.tensor_tensor(cut(B, 15, L), cut(A, 15, L), cut(A, 7, L - 8), ALU.add))
                    for q, S in ((slice(0, 64), A), (slice(64, P), B)):
                        step(dve.scalar_tensor_tensor(d[q], cut(S, POOL_BUF, L)[q], invw[q, c:c + 1],
                                                      cut(z, POOL_BUF, L)[q], ALU.mult, ALU.subtract))
                    sync()
                    if n == GT:
                        for q, S in ((slice(0, 64), A), (slice(64, P), B)):
                            step(dve.tensor_tensor(d[q, 0:16], S[q, POOL_BUF:POOL_BUF + 16],
                                                   invtab[q, c, :], ALU.mult))
                        sync()
                        do(dve.tensor_tensor(d[:, 0:16], d[:, 0:16], z[:, POOL_BUF:POOL_BUF + 16],
                                             ALU.subtract))
                do(dve.tensor_scalar(invtab[:, c, :], invtab[:, c, :], 0.0, invw[:, c:c + 1],
                                     ALU.mult, ALU.add))
                step(dve.tensor_copy(pcarry[:, c, :], pp_[:, GT:GT + POOL_BUF]))
                if nt == 5:
                    step(dve.tensor_copy(plast[:, c, 0:POOL_BUF], pp_[:, GT:GT + POOL_BUF]))
                    step(dve.tensor_copy(
                        plast[:, c, POOL_BUF:].rearrange("p (b n) -> p b n", b=NB), psm[:, :, DT:]))
                sync()
                n = GT + (ST if nt == 5 else 0)
                signal(split(rs[:, c, 0, 0:n], rs[:, c, 1, 0:n], htmp[:, 0, 0:n]), d_ready, 2 * s + c + 1)

            def pool_out(s, nt, c):
                dve.wait_ge(pm_done, 2 * s + c + 1)
                pv = fm_view(4 + 2 * c, nt)
                k = 6 + c
                do(dve.tensor_scalar(as_fm(bufB, nt), pv, pscale[:, c:c + 1], None, ALU.mult))
                mix_out(s, nt, k, bufB[:, 0:GT + (ST if nt == 5 else 0)])

            def u_fm(s, nt, f, bank):
                c = FM_PARTS[f][1]
                wait_fm(s, f)
                dve.tensor_tensor(as_fm(bufB, nt), fm_view(bank, nt), as_fm(sg[:, c, :], nt),
                                  ALU.mult).then_inc(fm_evac, 1)
                dve.wait_ge(fm_evac, s * N_FM + f + 1)
                mix_out(s, nt, 2 + c, bufB[:, 0:GT + (ST if nt == 5 else 0)])

            def gate_rows(t):
                return rows[:, 0, :] if t < 4 else gs[0:ST, :]

            def end_residual(t):
                r = rows_of(t)
                a, x = acc[0:r, t, :], xt[0:r, t, :]
                do(dve.tensor_tensor(a, a, gate_rows(t)[0:r, :], ALU.mult))
                do(dve.scalar_tensor_tensor(x, x, ALPHA, a, ALU.mult, ALU.add))
                for i in range(2):
                    sums(t, i, xt[0:r, t, HALF * i:HALF * i + HALF])
                mean_var(t, 2, ln_end)

            def end_sums(t):
                r = rows_of(t)
                x = xt[0:r, t, :]
                dve.wait_ge(acc_gated, t + 1)
                do(dve.scalar_tensor_tensor(x, x, ALPHA, acc[0:r, t, :], ALU.mult, ALU.add))
                for i in range(2):
                    sums(t, i, xt[0:r, t, HALF * i:HALF * i + HALF])
                mean_var(t, 2, ln_end)

            def end_norm(s, t):
                r = rows_of(t)
                x = xt[0:r, t, :]
                if t == 0:
                    do(normalise(x, x, t, ln_end))
                else:
                    dve.wait_ge(e_norm, 3 * s + t)
                do(dve.tensor_tensor(x, x, rows[0:r, 1, :], ALU.mult))
                signal(dve.tensor_tensor(x, x, rows[0:r, 2, :], ALU.add), y_ready, 4 * s + t + 1)

            def super_dve(s, nt, first, last):
                todo = list(enumerate(v_order(nt)))

                def some_v(n):
                    for _ in range(n):
                        if todo:
                            pos, t = todo.pop(0)
                            v_tile(s, nt, t, pos)

                if nt == 4 and not first:
                    end_norm(s - 1, 0)
                for pos, t in enumerate(v_order(nt)):
                    if pos < nt - 1:
                        dve.wait_ge(v_done, 3 * s + pos + 1)
                    else:
                        dve.wait_ge(slab_used, s * N_SLABS + 4)
                    sums(t, 0, ps[0:rows_of(t), V_BANK[t], :])
                    mean_var(t, 1, ln_now)
                    if t == 4:
                        scale_bias(4, 5, ln_now, v_stats, s + 1)
                if nt == 5:
                    some_v(1)
                scale_bias(0, 4, ln_now, v_stats, s + nt - 3)
                if nt == 4:
                    some_v(2)
                halves = 0
                for stage in mixer_stages(nt, first, True):
                    if stage[0] == "F":
                        f = stage[1]
                        work = {"u": u_fm, "pool": pool_fm}.get(FM_PARTS[f][0], conv_fm)
                        work(s, nt, f, fm_bank(f, nt, first))
                    elif stage[0] == "S":
                        for half in range(2):
                            for t in stage[1]:
                                halves += 1
                                sgu_half(s, t, half, halves)
                        sync()
                        dve.wait_ge(sgu_evac, 8 * s + halves)
                    elif stage[0] == "V":
                        some_v(stage[1])
                    elif stage[0] == "N":
                        if not first:
                            end_norm(s - 1, stage[1])
                    elif stage[0] == "A":
                        ada_add(stage[1])
                        if stage[1] > ADA_FIRST:
                            ada_turned(stage[1] - 1)
                    elif stage[0] == "E":
                        ada_turned(stage[1])
                        second_modulation()
                    else:
                        pool_out(s, nt, stage[1])
                dve.wait_ge(rows_loaded, 96 * s + 48)
                for h in range(2):
                    cols = slice(HALF * h, HALF * h + HALF)
                    for t in range(nt):
                        if h == 0 and t == 4:
                            dve.wait_ge(gs_loaded, 16 * NB)
                        if h == 0 and t < 4:
                            dve.wait_ge(x_loaded[t], 16 * s + 16)
                        if t < nt - 1:
                            dve.wait_ge(o_done, 6 * s + (nt - 1) * h + t + 1)
                        else:
                            dve.wait_ge(slab_used, s * N_SLABS + SLAB_O + 4 * h + 4)
                        r = rows_of(t)
                        tmp = htmp[0:r, t % 2, 0:HALF]
                        signal(dve.tensor_tensor(tmp, ps[0:r, o_bank(h, t), :], gate_rows(t)[0:r, cols],
                                                 ALU.mult), o_evac, 8 * s + nt * h + t + 1)
                        x = xt[0:r, t, cols]
                        do(dve.scalar_tensor_tensor(x, x, ALPHA, tmp, ALU.mult, ALU.add))
                        sums(t, h, x)
                        if h == 1:
                            mean_var(t, 2, ln_now)
                scale_bias(0, nt, ln_now, o_stats, s + 1)
                for t in range(2, nt):
                    x = xt[0:rows_of(t), t, :]
                    signal(normalise(x, x, t, ln_now), xn_dve, 2 * s + t - 1)
                for k in range(KD):
                    o_feature(s, nt, k)

                def hidden(f, i, parity):
                    dve.wait_ge(relu_done, s * 32 + f + 1)
                    n = GT + (ST if nt == 5 else 0)
                    hi, lo = (MH[:, p, 2 * parity + i, 0:n] for p in range(2))
                    x = htmp[:, i, 0:n]
                    signal(dve.tensor_copy(hi, x), s_hid_hi, s * 32 + f + 1)
                    signal(dve.tensor_tensor(lo, x, hi, ALU.subtract), hid_ready, s * 32 + f + 1)

                def first_x1(t):
                    r = rows_of(t)
                    x = xt[0:r, t, :]
                    do(dve.tensor_tensor(x, x, rows[0:r, 1, :], ALU.mult))
                    ins = dve.tensor_tensor(x, x, rows[0:r, 2, :], ALU.add)
                    if t == nt - 1:
                        signal(ins, x1_ready, s + 1)
                    else:
                        step(ins)

                def down(g, parity, start, last_slab, after=None):
                    for t in range(nt):
                        r = rows_of(t)
                        for h in range(2):
                            j = 2 * t + h
                            if j == 2 * nt - 1:
                                dve.wait_ge(slab_used, s * N_SLABS + last_slab + 1)
                            else:
                                dve.wait_ge(d_done, s * 112 + g * (2 * nt - 1) + j + 1)
                            a = acc[0:r, t, HALF * h:HALF * h + HALF]
                            src = ps[0:r, down_bank(nt, parity, j), :]
                            if start:
                                dve.tensor_copy(a, src).then_inc(d_evac, 1)
                            else:
                                dve.wait_ge(d_evac, s * 128 + (g - 1) * (2 * nt) + j + 1)
                                dve.tensor_tensor(a, a, src, ALU.add).then_inc(d_evac, 1)
                        if after:
                            after(t)

                for i in range(2):
                    hidden(i, i, 0)
                first_x1(0)
                if last:
                    dve.wait_ge(st_tr, 1)
                    for q, (_, n, _) in enumerate(STATES):
                        for c in range(2):
                            dve.tensor_copy(gs[0:n, 2 * P * q + P * c:2 * P * q + P * c + P],
                                            ps[0:n, 6 + c, P * q:P * q + P]).then_inc(st_rows, 1)
                for i in range(2):
                    hidden(2 + i, i, 1)
                down(0, 0, True, SLAB_UP0 + 5)
                for t in range(1, nt):
                    first_x1(t)
                dve.sem_inc(s_fence, 1)
                with dve.Fori(0, 6) as jj:
                    for par in (0, 1):
                        g = 2 * jj + 1 + par
                        for i in range(2):
                            hidden(2 * g + 2 + i, i, par)
                        down(g, 1 - par, False, SLAB_UP0 + 5 + 4 * g)
                for g in (13, 14):
                    for i in range(2):
                        hidden(2 * g + 2 + i, i, (g + 1) % 2)
                    if g == 14 and not last:
                        down(g, 0, False, SLAB_UP0 + 5 + 4 * g,
                             lambda t: x_tile(s + 1, t // 2) if t % 2 else None)
                    else:
                        down(g, g % 2, False, SLAB_UP0 + 5 + 4 * g)
                if not last:
                    down(15, 1, False, 87, lambda t: x_tile(s + 1, 2 + t // 2) if t % 2 else None)
                    dve.wait_ge(rows_loaded, 96 * s + 96)
                    dve.wait_ge(d_evac, s * 128 + 16 * 2 * nt)
                    for t in range(nt):
                        end_residual(t)
                    scale_bias(0, nt, ln_end, e_stats, s + 1)
                else:
                    def finish(t):
                        if t >= 1:
                            end_sums(t - 1)
                        if t == 2:
                            scale_bias(0, 2, ln_end, e_stats, SUPERS)
                        if t == 4:
                            end_sums(4)
                            scale_bias(2, 5, ln_end, e_stats, SUPERS + 1)

                    down(15, 1, False, 87, finish)
                    for t in range(nt):
                        dve.wait_ge(y_scaled, t + 1)
                        x = xt[0:rows_of(t), t, :]
                        signal(dve.tensor_tensor(x, x, rows[0:rows_of(t), 2, :], ALU.add),
                               y_ready, 4 * s + t + 1)

            ada_add(0)
            dve.wait_ge(s_prepe, 1)
            do(dve.tensor_copy(zstate[:, :, :], ps[:, 5, 0:32].rearrange("p (c n) -> p c n", c=2)))
            do(dve.tensor_copy(pstate[:, :, :], ps[:, 5, 128:368].rearrange("p (c n) -> p c n", c=2)))
            dve.wait_ge(s_prep, 1)
            dve.tensor_copy(prep[:, 1, :].rearrange("p (b n) -> p b n", b=2), ps[:, 6:8, :]).then_inc(s_pret, 1)

            def ada_next(u):
                ada_add(u)
                ada_turned(u - 1)

            ada_next(1)
            for n in range(3):
                ada_next(2 * n + 2)
                x0_feature(2 * n)
                x0_feature(2 * n + 1)
                ada_next(2 * n + 3)
            ada_turned(ADA_FIRST - 1)
            x0_feature(6)
            x0_feature(7)
            dve.wait_ge(ada_T, ADA_FIRST)
            x_sample()
            dve.wait_ge(s_prep, 2)
            super_dve(0, 4, True, False)
            before = local[0]
            with dve.Fori(1, SUPERS - 1) as s:
                base[0], local[0] = before + (s - 1) * DVE_STEPS, 0
                super_dve(s, 4, False, False)
                assert local[0] == DVE_STEPS, local[0]
            base[0], local[0] = before + (SUPERS - 2) * DVE_STEPS, 0
            super_dve(SUPERS - 1, 5, False, True)


_INS = ["x_prompt", "x_sample", "c_prompt", "c_sample", "state_conv", "state_pool", "w_ada", "b_ada",
        "w_in", "conv_w", "sgu_g", "sgu_b", "w_s", "b_s", "pool_w", "pool_scale", "w_out", "ln1_g",
        "ln1_b", "w_up", "w_down", "ln2_g", "ln2_b"]
_OUTS = [(1, SEQ, D), (NB, DT, D), (1, 1, CONV_BUF, W_CONV), (1, 1, POOL_BUF, W_POOL),
         (1, NB, CONV_BUF, W_CONV), (1, NB, POOL_BUF, W_POOL), (1, NB, DT, W_GMLP)]


def kernel(**inputs):
    import numpy as np
    import concourse.bacc as bacc
    from concourse.bass_utils import run_bass_kernel_spmd

    nc = bacc.Bacc("TRN2", target_bir_lowering=False, num_devices=1)
    arrays, args = {}, []
    for name in _INS:
        a = np.ascontiguousarray(inputs[name])
        arrays[f"in_{name}"] = a
        args.append(nc.dram_tensor(f"in_{name}", a.shape, mybir.dt.from_np(a.dtype), kind="ExternalInput").ap())
    for i, shape in enumerate(_OUTS):
        args.append(nc.dram_tensor(f"out_{i}", shape, F32, kind="ExternalOutput").ap())
    args.append(nc.dram_tensor("mod_rows", (1 + NB, 6 * D), F32).ap())
    decoder_layer_kernel(nc, *args)
    r = run_bass_kernel_spmd(nc, [arrays], core_ids=[0])
    return tuple(r.results[0][f"out_{i}"] for i in range(len(_OUTS)))
```
